# Optimizing a Trainium2 kernel written in Bass

```python
import math
import jax, jax.numpy as jnp
from jax import lax
import numpy as np

D_MODEL = 1024
BATCH = 1
SEQ = 512
DEPTH = 2

CHUNK = 64
Q_BLOCK = 128
EPS = 1e-6

MLA_HEADS = 8
QK_NOPE_DIM = 64
QK_ROPE_DIM = 32
V_HEAD_DIM = 64
Q_LORA_RANK = 768
KV_LORA_RANK = 256
ROPE_THETA = 10000.0
MLA_WIDTH = MLA_HEADS * V_HEAD_DIM

SSD_HEADS = 8
SSD_HEAD_DIM = 64
SSD_INNER = SSD_HEADS * SSD_HEAD_DIM
SSD_GROUPS = 2
SSD_STATE = 128
CONV_WIDTH = 4
CONV_DIM = SSD_INNER + 2 * SSD_GROUPS * SSD_STATE

MIX_WIDTH = MLA_WIDTH + SSD_INNER
D_FF = 4 * D_MODEL
IN_PROJ_DIM = Q_LORA_RANK + KV_LORA_RANK + QK_ROPE_DIM + SSD_INNER + CONV_DIM + SSD_HEADS

kernel_name = "hymba_mla_ssd_sandwich_trunk"

def rms_norm(x, w):
    xf = x.astype(jnp.float32)
    xf = xf * lax.rsqrt(jnp.mean(xf * xf, axis=-1, keepdims=True) + EPS)
    return xf.astype(x.dtype) * w

def rope_tables(positions):
    inv_freq = ROPE_THETA ** (-jnp.arange(0, QK_ROPE_DIM, 2, dtype=jnp.float32) / QK_ROPE_DIM)
    ang = positions[..., None].astype(jnp.float32) * inv_freq
    return jnp.cos(ang), jnp.sin(ang)

def apply_rope(t, cos, sin):
    half = t.shape[-1] // 2
    t1 = t[..., :half].astype(jnp.float32)
    t2 = t[..., half:].astype(jnp.float32)
    return jnp.concatenate([t1 * cos - t2 * sin, t2 * cos + t1 * sin], axis=-1).astype(t.dtype)

def mla_mixer(c_q, c_kv, k_rope, cos, sin, q_norm_w, w_uq, kv_norm_w, w_ukv):
    B, S, _ = c_q.shape
    q = (rms_norm(c_q, q_norm_w) @ w_uq).reshape(B, S, MLA_HEADS, QK_NOPE_DIM + QK_ROPE_DIM)
    q_nope = q[..., :QK_NOPE_DIM]
    q_rope = apply_rope(q[..., QK_NOPE_DIM:], cos[:, :, None], sin[:, :, None])
    k_rope = apply_rope(k_rope, cos, sin)
    kv = (rms_norm(c_kv, kv_norm_w) @ w_ukv).reshape(B, S, MLA_HEADS, QK_NOPE_DIM + V_HEAD_DIM)
    k_nope = kv[..., :QK_NOPE_DIM]
    v = kv[..., QK_NOPE_DIM:]
    scale = (QK_NOPE_DIM + QK_ROPE_DIM) ** -0.5
    nb = S // Q_BLOCK
    key_chunk = jnp.arange(S) // CHUNK

    def to_blocks(t):
        return jnp.moveaxis(t.reshape(B, nb, Q_BLOCK, *t.shape[2:]), 1, 0)

    def attend(args):
        blk, qn, qr = args
        s = (jnp.einsum("bqhd,bkhd->bhqk", qn, k_nope, preferred_element_type=jnp.float32)
             + jnp.einsum("bqhr,bkr->bhqk", qr, k_rope, preferred_element_type=jnp.float32)) * scale
        q_chunk = (blk * Q_BLOCK + jnp.arange(Q_BLOCK)) // CHUNK
        allowed = key_chunk[None, :] <= q_chunk[:, None]
        s = jnp.where(allowed[None, None], s, -jnp.inf)
        p = jax.nn.softmax(s, axis=-1).astype(v.dtype)
        return jnp.einsum("bhqk,bkhd->bqhd", p, v)

    o = lax.map(attend, (jnp.arange(nb), to_blocks(q_nope), to_blocks(q_rope)))
    return jnp.moveaxis(o, 0, 1).reshape(B, S, MLA_WIDTH)

def causal_depthwise_conv(x, w, b):
    S = x.shape[1]
    xp = jnp.pad(x, ((0, 0), (CONV_WIDTH - 1, 0), (0, 0)))
    y = xp[:, 0:S] * w[0]
    for k in range(1, CONV_WIDTH):
        y = y + xp[:, k:k + S] * w[k]
    return y + b

def segsum(a):
    L = a.shape[-1]
    cs = jnp.cumsum(a, axis=-1)
    diff = cs[..., :, None] - cs[..., None, :]
    tril = jnp.tril(jnp.ones((L, L), dtype=bool))
    return jnp.where(tril, diff, -jnp.inf)

def ssd_chunked(x, dt, A, Bm, Cm):
    Bsz, S, H, P = x.shape
    nc = S // CHUNK
    rep = H // SSD_GROUPS
    xdt = (x * dt[..., None]).reshape(Bsz, nc, CHUNK, H, P)
    a = jnp.transpose((dt * A).reshape(Bsz, nc, CHUNK, H), (0, 3, 1, 2))
    Bh = jnp.repeat(Bm, rep, axis=2).reshape(Bsz, nc, CHUNK, H, SSD_STATE)
    Ch = jnp.repeat(Cm, rep, axis=2).reshape(Bsz, nc, CHUNK, H, SSD_STATE)
    a_cs = jnp.cumsum(a, axis=-1)
    decay_in = jnp.exp(segsum(a))
    scores = jnp.einsum("bclhn,bcshn->bhcls", Ch, Bh) * decay_in
    y_diag = jnp.einsum("bhcls,bcshp->bclhp", scores, xdt)
    decay_states = jnp.exp(a_cs[..., -1:] - a_cs)
    states = jnp.einsum("bcshn,bhcs,bcshp->bchpn", Bh, decay_states, xdt)
    chunk_decay = jnp.exp(a_cs[..., -1])

    def step(h, inp):
        st, dec = inp
        return h * dec[..., None, None] + st, h

    init = jnp.zeros((Bsz, H, P, SSD_STATE), dtype=x.dtype)
    _, prev = lax.scan(step, init, (jnp.moveaxis(states, 1, 0), jnp.moveaxis(chunk_decay, 2, 0)))
    prev = jnp.moveaxis(prev, 0, 1)
    y_off = jnp.einsum("bclhn,bchpn,bhcl->bclhp", Ch, prev, jnp.exp(a_cs))
    return (y_diag + y_off).reshape(Bsz, S, H, P)

def ssd_mixer(z, xbc, dt_raw, conv_w, conv_b, dt_bias, a_log, d_skip, ssd_norm_w):
    B, S, _ = z.shape
    out_dtype = z.dtype
    xbc = jax.nn.silu(causal_depthwise_conv(xbc, conv_w, conv_b)).astype(jnp.float32)
    xs = xbc[..., :SSD_INNER].reshape(B, S, SSD_HEADS, SSD_HEAD_DIM)
    Bm = xbc[..., SSD_INNER:SSD_INNER + SSD_GROUPS * SSD_STATE].reshape(B, S, SSD_GROUPS, SSD_STATE)
    Cm = xbc[..., SSD_INNER + SSD_GROUPS * SSD_STATE:].reshape(B, S, SSD_GROUPS, SSD_STATE)
    dt = jax.nn.softplus(dt_raw.astype(jnp.float32) + dt_bias.astype(jnp.float32))
    A = -jnp.exp(a_log.astype(jnp.float32))
    y = ssd_chunked(xs, dt, A, Bm, Cm) + d_skip.astype(jnp.float32)[:, None] * xs
    y = y.reshape(B, S, SSD_INNER) * jax.nn.silu(z.astype(jnp.float32))
    yg = y.reshape(B, S, SSD_GROUPS, SSD_INNER // SSD_GROUPS)
    yg = yg * lax.rsqrt(jnp.mean(yg * yg, axis=-1, keepdims=True) + EPS)
    return (yg.reshape(B, S, SSD_INNER) * ssd_norm_w.astype(jnp.float32)).astype(out_dtype)

def setup_inputs(seed: int = 0) -> dict:
    key = jax.random.key(seed)
    ks = jax.random.split(key, 24)
    f32 = jnp.float32

    def normal(k, shape, scale):
        return jax.random.normal(k, shape, f32) * scale

    def gain(k, shape):
        return 1.0 + 0.02 * jax.random.normal(k, shape, f32)

    x = jax.random.normal(ks[0], (BATCH, SEQ, D_MODEL), f32)
    offset = jax.random.randint(ks[1], (BATCH, 1), 0, 4096, dtype=jnp.int32)
    positions = (offset + jnp.arange(SEQ, dtype=jnp.int32)[None, :]).astype(jnp.int32)
    dt0 = jnp.exp(jax.random.uniform(ks[2], (DEPTH, SSD_HEADS), f32)
                  * (math.log(0.1) - math.log(0.001)) + math.log(0.001))
    dt_bias = dt0 + jnp.log(-jnp.expm1(-dt0))
    a_log = jnp.log(jax.random.uniform(ks[3], (DEPTH, SSD_HEADS), f32, minval=1.0, maxval=16.0))
    return {
        "x": x,
        "positions": positions,
        "pre_mix_norm": gain(ks[4], (DEPTH, D_MODEL)),
        "w_in": normal(ks[5], (DEPTH, D_MODEL, IN_PROJ_DIM), D_MODEL ** -0.5),
        "q_norm": gain(ks[6], (DEPTH, Q_LORA_RANK)),
        "w_uq": normal(ks[7], (DEPTH, Q_LORA_RANK, MLA_HEADS * (QK_NOPE_DIM + QK_ROPE_DIM)), Q_LORA_RANK ** -0.5),
        "kv_norm": gain(ks[8], (DEPTH, KV_LORA_RANK)),
        "w_ukv": normal(ks[9], (DEPTH, KV_LORA_RANK, MLA_HEADS * (QK_NOPE_DIM + V_HEAD_DIM)), KV_LORA_RANK ** -0.5),
        "conv_w": normal(ks[10], (DEPTH, CONV_WIDTH, CONV_DIM), CONV_WIDTH ** -0.5),
        "conv_b": normal(ks[11], (DEPTH, CONV_DIM), 0.01),
        "dt_bias": dt_bias,
        "a_log": a_log,
        "d_skip": gain(ks[12], (DEPTH, SSD_HEADS)),
        "ssd_norm": gain(ks[13], (DEPTH, SSD_INNER)),
        "w_out": normal(ks[14], (DEPTH, MIX_WIDTH, D_MODEL), MIX_WIDTH ** -0.5),
        "post_mix_norm": gain(ks[15], (DEPTH, D_MODEL)),
        "pre_mlp_norm": gain(ks[16], (DEPTH, D_MODEL)),
        "w_up": normal(ks[17], (DEPTH, D_MODEL, D_FF), D_MODEL ** -0.5),
        "w_down": normal(ks[18], (DEPTH, D_FF, D_MODEL), D_FF ** -0.5),
        "post_mlp_norm": gain(ks[19], (DEPTH, D_MODEL)),
    }

def reference(x, positions, pre_mix_norm, w_in, q_norm, w_uq, kv_norm, w_ukv, conv_w, conv_b,
              dt_bias, a_log, d_skip, ssd_norm, w_out, post_mix_norm, pre_mlp_norm, w_up,
              w_down, post_mlp_norm):
    cos, sin = rope_tables(positions)
    s1 = Q_LORA_RANK
    s2 = s1 + KV_LORA_RANK
    s3 = s2 + QK_ROPE_DIM
    s4 = s3 + SSD_INNER
    s5 = s4 + CONV_DIM
    h = x
    for l in range(DEPTH):
        u = rms_norm(h, pre_mix_norm[l])
        proj = u @ w_in[l]
        c_q, c_kv, k_rope = proj[..., :s1], proj[..., s1:s2], proj[..., s2:s3]
        z, xbc, dt_raw = proj[..., s3:s4], proj[..., s4:s5], proj[..., s5:]
        y_att = mla_mixer(c_q, c_kv, k_rope, cos, sin, q_norm[l], w_uq[l], kv_norm[l], w_ukv[l])
        y_ssd = ssd_mixer(z, xbc, dt_raw, conv_w[l], conv_b[l], dt_bias[l], a_log[l], d_skip[l], ssd_norm[l])
        mixed = jnp.concatenate([y_att, y_ssd], axis=-1) @ w_out[l]
        h = h + rms_norm(mixed, post_mix_norm[l])
        m = rms_norm(h, pre_mlp_norm[l])
        m = jnp.square(jax.nn.relu(m @ w_up[l])) @ w_down[l]
        h = h + rms_norm(m, post_mlp_norm[l])
    return h


_drawn_inputs = setup_inputs


def setup_inputs(seed=0):
    import zlib

    import numpy as np

    out = dict(_drawn_inputs(seed))
    spreads = {}
    factors = {'q_norm': 8.0,
     'kv_norm': 8.0,
     'conv_b': 3.862,
     'd_skip': 5.304,
     'ssd_norm': 2.941,
     'post_mix_norm': 2.701,
     'pre_mlp_norm': 3.117,
     'post_mlp_norm': 3.547}
    for name, (base, spread) in spreads.items():
        noise = np.random.default_rng([zlib.crc32(name.encode()), seed]).standard_normal(out[name].shape)
        drawn = base * np.exp(spread * noise) if base else spread * noise
        out[name] = __import__('jax').numpy.asarray(drawn.astype(out[name].dtype))
    for name, factor in factors.items():
        out[name] = (out[name] * factor).astype(out[name].dtype)
    return out
```

```python
from contextlib import ExitStack

import numpy as np

import concourse.bass as bass
from concourse import mybir

F32 = mybir.dt.float32
F32R = mybir.dt.float32r
I32 = mybir.dt.int32
ACT = mybir.ActivationFunctionType
ALU = mybir.AluOpType
AX = mybir.AxisListType.X

P = 128
EPS = 1e-6
NEG = -1e30

D_MODEL, SEQ, DEPTH = 1024, 512, 2
HEADS, NOPE, ROPE, VDIM = 8, 64, 32, 64
QK = NOPE + ROPE
Q_RANK, KV_RANK = 768, 256
S_HEADS, GROUPS, STATE, TAPS = 8, 2, 128, 4
INNER = S_HEADS * 64
CONV = INNER + 2 * GROUPS * STATE
D_FF = 4 * D_MODEL
CHUNK = 64
TT = SEQ // P
KD = D_MODEL // P
HG = S_HEADS // GROUPS
SCALE = float(QK) ** -0.5

C_KV = Q_RANK
C_KR = C_KV + KV_RANK
C_Z = C_KR + ROPE
C_XBC = C_Z + INNER
C_DT = C_XBC + CONV

K_ID, K_TRI, K_ONE, K_SWAP, K_SEL, K_MASK, K_FREQ, K_SIGN = 0, 128, 256, 384, 512, 640, 768, 769
N_CONST = 770

V_PRE, V_Q, V_KV, V_CW, V_CB, V_SSD, V_MLP = 0, 8, 14, 16, 48, 56, 60
N_VEC = 68

RING, SPLIT = 4, 2
N_IN = 11
N_UQ = N_IN
N_UKV = N_UQ + 3
N_OUT = N_UKV + 1
N_MLP = N_OUT + 4
QUARTERS = 4
OUT_ROWS = ((4, 5), (6, 7), (0, 1), (2, 3))


def constants():
    c = np.zeros((P, N_CONST), np.float32)
    i = np.arange(P)
    c[:, K_ID:K_ID + P] = np.eye(P)
    c[:, K_TRI:K_TRI + P] = i[:, None] <= i[None, :]
    c[:, K_ONE:K_ONE + P] = 1
    c[i, K_SWAP + (i ^ (ROPE // 2))] = 1
    c[0, K_SEL:K_SEL + CHUNK] = 1
    c[0, K_MASK + CHUNK:K_MASK + P] = NEG
    half = np.arange(0, ROPE, 2, dtype=np.float32)
    c[:, K_FREQ] = (np.float32(10000.0) ** (-half / np.float32(ROPE)))[i % (ROPE // 2)]
    c[:, K_SIGN] = np.where(i % ROPE < ROPE // 2, -1, 1)
    return c


def two_pi_parts():
    parts, rest = [], 2 * np.pi
    for _ in range(5):
        e = np.floor(np.log2(rest)) - 7
        parts.append(float(np.floor(rest / 2 ** e) * 2 ** e))
        rest -= parts[-1]
    return parts


def trunk(nc, A, consts, out):
    ctx = ExitStack()
    with ctx:
        def sb(name, shape, dt=F32, stack=ctx):
            return stack.enter_context(nc.sbuf_tensor(name, shape, dt))

        H = sb("h", [P, TT, D_MODEL])
        XH = sb("x_hi", [P, KD, SEQ], F32R)
        XL = sb("x_lo", [P, KD, SEQ], F32R)
        RAW = sb("w_raw", [P, RING, 2048])
        WH = sb("w_hi", [P, SPLIT, 2048], F32R)
        WL = sb("w_lo", [P, SPLIT, 2048], F32R)
        COS = sb("cos", [P, SEQ])
        SIN = sb("sin", [P, SEQ])
        POST = sb("post_w", [P, D_MODEL])
        CT = sb("consts", [P, N_CONST])
        VEC = sb("vec_rows", [N_VEC, P])
        VC = sb("vec_cols", [P, N_VEC])
        SCR = sb("scratch", [P, 3, SEQ])
        DTB = sb("dt_bias_b", [P, S_HEADS])
        ALOG = sb("a_log_b", [P, S_HEADS])
        DSKB = sb("d_skip_b", [P, S_HEADS])
        DSK = sb("d_skip_rows", [P, S_HEADS // 2])
        N4 = sb("norm_small", [P, 5, TT])
        T4 = sb("norm_tmp", [P, TT])
        DTT = sb("dt_small", [P, 8, TT * S_HEADS])
        DT, AA, CST = DTT[:, 0, :], DTT[:, 1, :], DTT[:, 2, :]
        CLX = sb("chunk_log", [P, 2, HG, TT])
        MX = sb("row_max", [P, HEADS, TT])
        NM = sb("neg_max", [P, HEADS, TT])
        RSUM = sb("row_sum", [P, HEADS, TT])
        RINV = sb("row_inv", [P, HEADS, TT])

        def union(*variants):
            got, most = [], 0
            for v in variants:
                with ExitStack() as s:
                    got.append([sb(n, shape, dt, s) for n, shape, dt in v])
                most = max(most, sum(4 * int(np.prod(shape[1:])) for _, shape, _ in v))
            sb(variants[0][0][0] + "_zone", [P, most // 4])
            return got

        SM = sb("krope_dt", [40, SEQ])
        (CQ,), (V, PT), (UTOK,), (RELU, SQR) = union(
            [("c_rows", [P, 8, SEQ], F32)],
            [("v", [P, TT, HEADS * VDIM], F32), ("p_t", [P, TT, SEQ], F32)],
            [("u_tok", [P, TT, D_MODEL], F32)],
            [("relu", [P, 2, SEQ], F32), ("relu_sq", [P, 2, SEQ], F32)],
        )
        (XB, ZS, E, XD, XDD, BT, CBM, ST, Y), (Q, K, CH, CL), (_q, _k, PR), (MACC, AH, AL) = union(
            [("xbc", [P, 8, SEQ], F32), ("z_silu", [P, 4, SEQ], F32), ("decay", [P, HG, SEQ], F32),
             ("xdt", [P, TT, HG * 64], F32), ("xdt_dec", [P, TT - 1, HG * 64], F32),
             ("b_tok", [P, TT, STATE], F32), ("cb", [P, SEQ], F32),
             ("state", [P, TT - 1, HG * 64], F32), ("y", [P, 2, SEQ], F32)],
            [("q", [QK, HEADS, SEQ], F32), ("k", [QK, HEADS, SEQ], F32),
             ("c_hi", [P, 4, SEQ], F32R), ("c_lo", [P, 4, SEQ], F32R)],
            [("q_", [QK, HEADS, SEQ], F32), ("k_", [QK, HEADS, SEQ], F32),
             ("probs", [P, 2, TT, SEQ], F32)],
            [("mlp_acc", [P, TT, D_MODEL], F32), ("act_hi", [P, 8, SEQ], F32R),
             ("act_lo", [P, 8, SEQ], F32R)],
        )
        PS = ctx.enter_context(nc.psum_tensor("ps", [P, 8, 512], F32))

        ident, tri, ones = CT[:, K_ID:K_ID + P], CT[:, K_TRI:K_TRI + P], CT[:, K_ONE:K_ONE + P]
        swap = CT[:, K_SWAP:K_SWAP + P]

        def f32(ap):
            return ap.bitcast(F32)

        names = """raw0 raw1 raw2 raw3 params broad post_mlp hi_done lo_done w_used
            ssq nrm_x nrm_y utok ut_done xh xl vec_t vc proj act_ev conv0 conv3 xb sq_add
            cssq rsb_x rsb_y cqn ch cl dt_t dt_n dt_e dt_l a_ready cst cst_ready btok bt cb cbm csb dd e_ready
            xs_t xd xdd m_ready cdx st_mm st_ready yec yexp yo yd y_done ysq yssq y_n yhi ylo
            kswap kro q_done q_ev q_rr qswap q_ro q_rc kv_done k_ev v_ev
            s_done nm p_done pn pt_done pt_a pt_d pv o_hi o_lo o_done
            macc0 up_done relu a_done act_hi act_lo down_done down_free h_done
            dve_step act_step""".split()
        S = {n: ctx.enter_context(nc.semaphore(n)) for n in names}
        first, final = S[names[0]], S[names[-1]]
        (boot_ld, boot_v, boot_a, stored) = (ctx.enter_context(nc.semaphore(n))
                                             for n in ("boot_ld", "boot_v", "boot_a", "stored"))

        with nc.Block() as block:
            @block.sync
            def _(sp):
                sp.dma_start(CT[:, :], consts[:, :]).then_inc(boot_ld, 16)
                sp.dma_start(SCR[:, 0, :].bitcast(I32),
                             A["positions"][0:1, :].to_broadcast([P, SEQ])).then_inc(boot_ld, 16)
                sp.dma_start(H[:, :, :], A["x"].rearrange("a (t p) d -> p (a t) d", p=P)).then_inc(boot_ld, 16)

            @block.vector
            def _(v):
                n = [0]

                def step(ins):
                    n[0] += 1
                    ins.then_inc(boot_v, 1)
                    v.wait_ge(boot_v, n[0])

                v.wait_ge(boot_ld, 48)
                pos, ang, turns = SCR[:, 1, :], SCR[:, 2, :], UTOK[:, 0, 0:SEQ]
                step(v.tensor_copy(pos, SCR[:, 0, :].bitcast(I32)))
                step(v.tensor_scalar(ang, pos, CT[:, K_FREQ:K_FREQ + 1], None, ALU.mult))
                for table, shift, offset in ((SIN, 0.0, 0.0), (COS, 0.25, float(np.pi / 2))):
                    magic = 1.5 * 2.0 ** 23
                    step(v.tensor_scalar(turns, ang, float(1 / (2 * np.pi)), shift, ALU.mult, ALU.add))
                    step(v.tensor_scalar(turns, turns, magic, None, ALU.add))
                    step(v.tensor_scalar(turns, turns, -magic, None, ALU.add))
                    step(v.tensor_copy(table[:, :], ang))
                    for part in two_pi_parts():
                        step(v.scalar_tensor_tensor(table[:, :], turns, -part, table[:, :], ALU.mult, ALU.add))
                    step(v.tensor_scalar(table[:, :], table[:, :], offset, None, ALU.add))
                    step(v.tensor_scalar(table[:, :], table[:, :], 3.1415925, -3.1415925, ALU.min, ALU.max))
                v.wait_ge(boot_a, 1)
                v.tensor_scalar(SIN[:, :], SIN[:, :], CT[:, K_SIGN:K_SIGN + 1], None, ALU.mult)

            @block.scalar
            def _(a):
                a.wait_ge(boot_v, 2 + 2 * 11)
                a.activation(SIN[:, :], SIN[:, :], ACT.Sin).then_inc(boot_a, 1)
                a.activation(COS[:, :], COS[:, :], ACT.Sin)

        def w_view(buf, n, slot):
            rows, cols = chunk_shape(n)
            return buf[:, slot, 0:rows * cols].rearrange("p (k n) -> p k n", k=rows)

        def chunk_shape(n):
            if n == 0:
                return KD, 40
            if n < N_UQ:
                return KD, 256
            if n < N_UKV:
                return 2, HEADS * QK
            if n < N_MLP:
                return 2, 1024
            return (KD, 256) if (n - N_MLP) % 8 < 4 else (4, 512)

        def split_parts(n, slot):
            raw, hi, lo = (w_view(b, n, s) for b, s in ((RAW, n % RING), (WH, slot), (WL, slot)))
            if N_UQ <= n < N_OUT:
                a, b = (NOPE, ROPE) if n < N_UKV else (NOPE, VDIM)
                r = raw.rearrange("p k (h c) -> p k h c", h=HEADS)
                cut = lambda w: ((w[:, :, 0:HEADS * a].rearrange("p k (h c) -> p k h c", h=HEADS)),
                                 (w[:, :, HEADS * a:HEADS * (a + b)].rearrange("p k (h c) -> p k h c", h=HEADS)))
                (h0, h1), (l0, l1) = cut(hi), cut(lo)
                return [x for k in range(2) for x in ((r[:, k, :, 0:a], h0[:, k], l0[:, k]),
                                                      (r[:, k, :, a:a + b], h1[:, k], l1[:, k]))]
            return [(raw, hi, lo)]

        with nc.Fori(0, DEPTH) as layer:
            with nc.Block() as block:

                def at(name):
                    return A[name][bass.ds(layer, 1)]

                @block.sync
                def _(sp):
                    for name, row, n in (("pre_mix_norm", V_PRE, 8), ("q_norm", V_Q, 6), ("kv_norm", V_KV, 2),
                                         ("conv_b", V_CB, 8), ("ssd_norm", V_SSD, 4), ("pre_mlp_norm", V_MLP, 8)):
                        sp.dma_start(VEC[row:row + n, :],
                                     at(name).rearrange("a (r c) -> (a r) c", c=P)).then_inc(S["params"], 16)
                    sp.dma_start(VEC[V_CW:V_CW + 32, :],
                                 at("conv_w").rearrange("a k (r c) -> (a k r) c", c=P)).then_inc(S["params"], 16)

                    def load(n, src):
                        if n >= RING:
                            sp.wait_ge(S["hi_done"], n - RING + 1)
                            sp.wait_ge(S["lo_done"], n - RING + 1)
                        sp.dma_start(w_view(RAW, n, n % RING), src).then_inc(S[f"raw{n % RING}"], 16)

                    def rows(name, r0, r1, c0, c1):
                        return at(name)[:, r0:r1, c0:c1].rearrange("a (k p) n -> p (a k) n", p=P)

                    small = w_view(RAW, 0, 0)
                    sp.dma_start(small[:, :, 0:ROPE], rows("w_in", 0, D_MODEL, C_KR, C_Z)).then_inc(S["raw0"], 16)
                    sp.dma_start(small[:, :, ROPE:40],
                                 rows("w_in", 0, D_MODEL, C_DT, C_DT + S_HEADS)).then_inc(S["raw0"], 16)
                    starts = ([C_XBC + 256 * i for i in range(4)] + [C_Z + 256 * i for i in range(2)]
                              + [256 * i for i in range(4)])
                    for i, c in enumerate(starts):
                        load(1 + i, rows("w_in", 0, D_MODEL, c, c + 256))
                        if i == 2:
                            for buf, name in ((DTB, "dt_bias"), (ALOG, "a_log"), (DSKB, "d_skip")):
                                sp.dma_start(buf[:, :], at(name).to_broadcast([P, S_HEADS])).then_inc(S["broad"], 16)
                            sp.dma_start(POST[:, :], at("post_mix_norm").to_broadcast([P, D_MODEL])
                                         ).then_inc(S["broad"], 16)
                    for i in range(3):
                        load(N_UQ + i, rows("w_uq", 256 * i, 256 * i + 256, 0, HEADS * QK))
                    load(N_UKV, rows("w_ukv", 0, KV_RANK, 0, HEADS * (NOPE + VDIM)))
                    for i, (k, _) in enumerate(OUT_ROWS):
                        load(N_OUT + i, rows("w_out", P * k, P * k + 256, 0, D_MODEL))
                    with sp.Fori(0, QUARTERS) as q:
                        for i in range(8):
                            n = N_MLP + i
                            if i < 4:
                                src = at("w_up")[:, :, bass.ds(q * 1024 + 256 * i, 256)]
                            else:
                                half, kk = (i - 4) // 2, (i - 4) % 2
                                src = at("w_down")[:, bass.ds(q * 1024 + 512 * kk, 512), 512 * half:512 * half + 512]
                            src = src.rearrange("a (k p) n -> p (a k) n", p=P)
                            sp.wait_ge(S["hi_done"], q * 8 + (n - RING + 1))
                            sp.wait_ge(S["lo_done"], q * 8 + (n - RING + 1))
                            sp.dma_start(w_view(RAW, n, n % RING), src).then_inc(S[f"raw{n % RING}"], 16)
                    sp.wait_ge(S["h_done"], TT)
                    sp.dma_start(POST[:, :], at("post_mlp_norm").to_broadcast([P, D_MODEL])
                                 ).then_inc(S["post_mlp"], 16)

                N_BROAD = 16 * 4

                def chunk_ready(eng, n, q=None):
                    value = 16 * (n // RING + 1) + (16 if n % RING == 0 else 0)
                    eng.wait_ge(S[f"raw{n % RING}"], value if q is None else value + q * 32)

                @block.tensor
                def _(pe):
                    def three(dst, w, x, start, stop):
                        for i, (a, b) in enumerate(((w[1], x[0]), (w[0], x[1]), (w[0], x[0]))):
                            last = pe.matmul(dst, a, b, start=start and i == 0, stop=stop and i == 2)
                        return last

                    def weights(n, q=None):
                        pe.wait_ge(S["lo_done"], n + 1 if q is None else q * 8 + n + 1)
                        return w_view(WH, n, n % SPLIT), w_view(WL, n, n % SPLIT)

                    def transpose_norm(i):
                        for k in range(KD):
                            if i == 0 and k == KD - 1:
                                pe.wait_ge(S["vc"], 1)
                            for t in range(TT):
                                if k == 0:
                                    pe.wait_ge(S["utok"], TT * i + t + 1)
                                last = pe.transpose(PS[:, k, P * t:P * t + P], UTOK[:, t, P * k:P * k + P], ident)
                            last.then_inc(S["ut_done"], 1)

                    pe.wait_ge(S["params"], 7 * 16)
                    pe.transpose(PS[:, 7, 0:N_VEC], VEC[:, :], ident[0:N_VEC, 0:N_VEC]).then_inc(S["vec_t"], 1)
                    transpose_norm(0)

                    m = 0
                    for n in range(N_IN):
                        wh, wl = weights(n)
                        for c0, c1 in ([(0, 40)] if n == 0 else [(0, 128), (128, 256)]):
                            if m == 8:
                                pe.wait_ge(S["act_ev"], 1)
                            elif 9 <= m < 17:
                                pe.wait_ge(S["conv3"], m - 8)
                            elif m >= 17:
                                pe.wait_ge(S["act_ev"], m - 15)
                            for k in range(KD):
                                if m == 0:
                                    pe.wait_ge(S["xl"], KD)
                                last = three(PS[0:c1 - c0, m % 8, :], (wh[:, k, c0:c1], wl[:, k, c0:c1]),
                                             (XH[:, k, :], XL[:, k, :]), k == 0, k == KD - 1)
                            last.then_inc(S["proj"], 1)
                            m += 1

                    pe.wait_ge(S["act_ev"], 13)
                    for i, ops in ((0, 5), (1, 6)):
                        pe.wait_ge(S["sq_add"], ops)
                        pe.matmul(PS[:, i, :], ones, E[:, 2 + i, :], start=True, stop=True).then_inc(S["cssq"], 1)

                    for t in range(TT):
                        last = pe.transpose(PS[:, 2, 8 * t:8 * t + 8], SM[32:40, P * t:P * t + P], ident[32:40, 32:40])
                    last.then_inc(S["dt_t"], 1)
                    pe.wait_ge(S["a_ready"], 1)
                    pe.matmul(PS[:, 3, 0:32], tri, AA, start=True, stop=True).then_inc(S["cst"], 1)
                    pe.wait_ge(S["xb"], 8)
                    pe.wait_ge(S["cst_ready"], 1)
                    pe.wait_ge(S["rsb_x"], 2)
                    for g in range(GROUPS):
                        if g:
                            pe.wait_ge(S["ylo"], 2)
                        for c in range(TT):
                            last = pe.transpose(PS[:, 2, P * c:P * c + P], XB[:, 4 + g, P * c:P * c + P], ident)
                        last.then_inc(S["btok"], 1)
                        for c in range(TT):
                            last = pe.matmul(PS[:, 3, P * c:P * c + P], XB[:, 4 + g, P * c:P * c + P],
                                             XB[:, 6 + g, P * c:P * c + P], start=True, stop=True)
                        last.then_inc(S["cb"], 1)
                        for hh in range(HG):
                            for c in range(TT):
                                col = S_HEADS * c + HG * g + hh
                                last = pe.matmul(PS[:, 4 + hh, P * c:P * c + P],
                                                 AA[:, col:col + 1].to_broadcast([P, P]), tri, start=True, stop=True)
                            last.then_inc(S["csb"], 1)
                        for c in range(TT):
                            for jj in range(2):
                                last = pe.transpose(PS[:, c // 2, 256 * (c % 2) + P * jj:256 * (c % 2) + P * jj + P],
                                                    XB[:, 2 * g + jj, P * c:P * c + P], ident)
                            if c % 2:
                                last.then_inc(S["xs_t"], 1)
                        pe.wait_ge(S["bt"], g + 1)
                        pe.wait_ge(S["cbm"], g + 1)
                        for c in range(TT - 1):
                            pe.wait_ge(S["xdd"], 3 * g + c + 1)
                            pe.matmul(PS[:, 2 + c // 2, 256 * (c % 2):256 * (c % 2) + 256], BT[:, c, :], XDD[:, c, :],
                                      start=True, stop=True).then_inc(S["st_mm"], 1)
                        pe.wait_ge(S["xd"], 2 * g + 2)
                        for jj in range(2):
                            for hl in range(2):
                                for c in range(1, TT):
                                    col = S_HEADS * c + HG * g + 2 * jj + hl
                                    last = pe.matmul(PS[64 * hl:64 * hl + 64, jj, P * c:P * c + P],
                                                     AA[:, col:col + 1].to_broadcast([P, 64]), tri,
                                                     start=True, stop=True)
                            last.then_inc(S["yec"], 1)
                        for jj in range(2):
                            for hl in range(2):
                                hh = 2 * jj + hl
                                pe.wait_ge(S["m_ready"], HG * g + hh + 1)
                                for c in range(TT):
                                    last = pe.matmul(PS[64 * hl:64 * hl + 64, 4 + jj, P * c:P * c + P],
                                                     XD[:, c, 64 * hh:64 * hh + 64], E[:, hh, P * c:P * c + P],
                                                     start=True, stop=True)
                            last.then_inc(S["yd"], 1)
                            for c in range(1, TT):
                                pe.wait_ge(S["st_ready"], 3 * g + c)
                                last = pe.matmul(PS[:, 6 + jj, P * c:P * c + P], ST[:, c - 1, P * jj:P * jj + P],
                                                 XB[:, 6 + g, P * c:P * c + P], start=True, stop=True)
                            last.then_inc(S["yo"], 1)
                        for jj in range(2):
                            pe.wait_ge(S["ysq"], 2 * g + jj + 1)
                            last = pe.matmul(PS[:, 2, :], ones, E[:, 2 * jj, :], start=(jj == 0), stop=(jj == 1))
                        last.then_inc(S["yssq"], 1)

                    pe.wait_ge(S["ylo"], 4)
                    pe.matmul(PS[0:ROPE, 7, :], swap[0:ROPE, 0:ROPE], SM[0:ROPE, :], start=True, stop=True
                              ).then_inc(S["kswap"], 1)
                    for i in range(3):
                        n = N_UQ + i
                        wh, wl = weights(n)
                        for k in range(2):
                            pe.wait_ge(S["cl"], 2 * i + k + 1)
                            s = (2 * i + k) % 4
                            for mt in range(6):
                                cols = slice(P * mt, P * mt + P)
                                last = three(PS[:, mt, :], (wh[:, k, cols], wl[:, k, cols]),
                                             (CH[:, s, :], CL[:, s, :]), i + k == 0, i == 2 and k == 1)
                                if i == 2 and k == 1:
                                    last.then_inc(S["q_done"], 1)
                        if i < 2:
                            last.then_inc(S["w_used"], 1)
                    pe.wait_ge(S["cl"], 8)
                    wh, wl = weights(N_UKV)
                    for u in range(8):
                        bank = (6 + u) % 8
                        if u == 1:
                            pe.wait_ge(S["kro"], 1)
                        if u >= 6:
                            pe.wait_ge(S["q_rr"], u - 5)
                        elif u >= 2:
                            pe.wait_ge(S["q_ev"], u - 1)
                        for k in range(2):
                            if u < 4:
                                cols = slice(P * u, P * u + P)
                                last = three(PS[:, bank, :], (wh[:, k, cols], wl[:, k, cols]),
                                             (CH[:, 2 + k, :], CL[:, 2 + k, :]), k == 0, k == 1)
                            else:
                                toks = slice(P * (u - 4), P * (u - 4) + P)
                                last = three(PS[:, bank, :], (CH[:, 2 + k, toks], CL[:, 2 + k, toks]),
                                             (wh[:, k, 512:1024], wl[:, k, 512:1024]), k == 0, k == 1)
                        last.then_inc(S["kv_done"], 1)
                    for t in range(2):
                        pe.wait_ge(S["q_rr"], t + 1)
                        pe.wait_ge(S["k_ev"], t + 1)
                        pe.matmul(PS[:, 6 + t, :], swap, SCR[:, t, :], start=True, stop=True).then_inc(S["qswap"], 1)

                    pe.wait_ge(S["q_rc"], 8)
                    pe.wait_ge(S["k_ev"], 4)
                    pe.wait_ge(S["v_ev"], 4)

                    def scores(h):
                        for i in range(TT):
                            n = P * (i + 1)
                            if h:
                                pe.wait_ge(S["p_done"], TT * (h - 1) + i + 1)
                            pe.matmul(PS[:, i, 0:n], Q[:, h, P * i:P * i + P], K[:, h, 0:n], start=True, stop=False)
                            pe.matmul(PS[:, i, n - P:n], CT[0:1, K_SEL:K_SEL + P], CT[0:1, K_MASK:K_MASK + P],
                                      start=False, stop=True).then_inc(S["s_done"], 1)

                    scores(0)
                    for h in range(HEADS):
                        if h + 1 < HEADS:
                            scores(h + 1)
                        pe.wait_ge(S["pn"], h + 1)
                        for j in range(TT):
                            if j >= 2:
                                pe.wait_ge(S["pt_a" if j == 2 else "pt_d"], 2 * h + 1)
                            elif h:
                                pe.wait_ge(S["pt_a" if j == 0 else "pt_d"], 2 * h)
                            for i in range(j, TT):
                                last = pe.transpose(PS[:, 4 + j % 2, P * i:P * i + P],
                                                    PR[:, h % 2, i, P * j:P * j + P], ident)
                            last.then_inc(S["pt_done"], 1)
                        pe.wait_ge(S["pt_a"], 2 * h + 2)
                        pe.wait_ge(S["pt_d"], 2 * h + 2)
                        if h >= 4:
                            pe.wait_ge(S["o_lo"], h // 2 - 1)
                        rows = slice(64 * (h % 2), 64 * (h % 2) + 64)
                        for j in range(TT):
                            last = pe.matmul(PS[rows, 6 + (h // 2) % 2, P * j:SEQ], V[:, j, VDIM * h:VDIM * h + VDIM],
                                             PT[:, j, P * j:SEQ], start=(j == 0), stop=(j == TT - 1))
                        last.then_inc(S["pv"], 1)

                    pe.wait_ge(S["o_lo"], 4)
                    for i, pair in enumerate(OUT_ROWS):
                        n = N_OUT + i
                        wh, wl = weights(n)
                        order = ([(k, t) for k in range(2) for t in range(TT)] if i < 3 else
                                 [(k, t) for t in range(TT) for k in range(2)])
                        for k, t in order:
                            kt, toks = pair[k], slice(P * t, P * t + P)
                            for half in range(2):
                                cols = slice(512 * half, 512 * half + 512)
                                last = three(PS[:, 2 * t + half, :], (XH[:, kt, toks], XL[:, kt, toks]),
                                             (wh[:, k, cols], wl[:, k, cols]), i + k == 0, i == 3 and k == 1)
                            if i == 3 and k == 1:
                                last.then_inc(S["o_done"], 1)
                        if i < 3:
                            last.then_inc(S["w_used"], 1)

                    transpose_norm(1)
                    pe.wait_ge(S["xl"], 2 * KD)

                    def quarter(q):
                        for i in range(8):
                            wh, wl = weights(N_MLP + i, q)
                            if i < 4:
                                for f in (2 * i, 2 * i + 1):
                                    cols = slice(P * (f % 2), P * (f % 2) + P)
                                    pe.wait_ge(S["a_done"], q * 8 + f + 1)
                                    for k in range(KD):
                                        last = three(PS[:, 4 + f % 4, :], (wh[:, k, cols], wl[:, k, cols]),
                                                     (XH[:, k, :], XL[:, k, :]), k == 0, k == KD - 1)
                                    last.then_inc(S["up_done"], 1)
                            else:
                                half, kk = (i - 4) // 2, (i - 4) % 2
                                for k in range(4):
                                    if half == 0:
                                        pe.wait_ge(S["act_lo"], q * 8 + 4 * kk + k + 3)
                                    for t in range(TT):
                                        if kk + k == 0:
                                            pe.wait_ge(S["down_free"], q * 8 + TT * half + t + 5)
                                        f, toks = 4 * kk + k, slice(P * t, P * t + P)
                                        last = three(PS[:, t, :], (AH[:, f, toks], AL[:, f, toks]),
                                                     (wh[:, k, :], wl[:, k, :]), kk + k == 0, kk == 1 and k == 3)
                                last.then_inc(S["down_done"], 1)

                    with pe.Fori(0, QUARTERS) as q:
                        quarter(q)

                def chunk_used(eng, n, q=None):
                    if n < N_UQ:
                        eng.wait_ge(S["proj"], 2 * n + 1)
                    elif n < N_UQ + 2:
                        eng.wait_ge(S["w_used"], n - N_UQ + 1)
                    elif n < N_UKV:
                        eng.wait_ge(S["q_done"], 6)
                    elif n == N_UKV:
                        eng.wait_ge(S["kv_done"], 8)
                    elif n < N_OUT + 3:
                        eng.wait_ge(S["w_used"], n - N_OUT + 3)
                    elif q is None:
                        eng.wait_ge(S["o_done"], TT)
                    elif n < N_MLP:
                        eng.wait_ge(S["down_done"], q * 4 + 1)
                    elif n < N_MLP + 4:
                        eng.wait_ge(S["up_done"], q * 8 + 2 * (n - N_MLP) + 2)
                    else:
                        eng.wait_ge(S["down_done"], q * 4 + (n - N_MLP - 4) + 2)

                def cuts(n):
                    parts = split_parts(n, n % SPLIT)
                    for i, x in enumerate(parts):
                        yield x, i == len(parts) - 1

                @block.scalar
                def _(a):
                    n_steps = [0]

                    def step(ins):
                        n_steps[0] += 1
                        ins.then_inc(S["act_step"], 1)
                        a.wait_ge(S["act_step"], n_steps[0])

                    def hi(n, q=None):
                        chunk_ready(a, n, q)
                        if n >= SPLIT:
                            chunk_used(a, n - SPLIT, q)
                        for (raw, h, _), last in cuts(n):
                            ins = a.activation(h, raw, ACT.Copy)
                            if last:
                                ins.then_inc(S["hi_done"], 1)

                    def norm(i, source):
                        for t in range(TT):
                            x, ready = source(t)
                            if ready:
                                a.wait_ge(*ready)
                            a.activation(junk(t, x), x, ACT.Square, accum_out=N4[:, 0, t:t + 1]).then_inc(S["ssq"], 1)
                        a.wait_ge(S["nrm_x"], i + 1)
                        step(a.activation(N4[:, 2, :], N4[:, 1, :], ACT.Ln))
                        a.activation(N4[:, 3, :], N4[:, 2, :], ACT.Exp, scale=-0.5).then_inc(S["nrm_y"], 1)

                    def junk(t, like):
                        u = UTOK[:, t, :]
                        return u if len(like.shape) == 2 else u.rearrange("p (a b) -> p a b", a=2)

                    def x_high(i, v):
                        for k in range(KD):
                            a.wait_ge(S["ut_done"], KD * i + k + 1)
                            a.activation(XH[:, k, :], PS[:, k, :], ACT.Copy, scale=VC[:, v + k:v + k + 1]
                                         ).then_inc(S["xh"], 1)

                    def rsqrt_wide(i):
                        a.wait_ge(S["rsb_x"], i + 1)
                        step(a.activation(SCR[:, 0, :], SCR[:, 2, :], ACT.Ln))
                        a.activation(SCR[:, 0, :], SCR[:, 0, :], ACT.Exp, scale=-0.5).then_inc(S["rsb_y"], 1)

                    norm(0, lambda t: (H[:, t, :], None))
                    hi(0)
                    a.wait_ge(S["vec_t"], 1)
                    step(a.activation(VC[:, :], PS[:, 7, 0:N_VEC], ACT.Copy))
                    a.sem_inc(S["vc"], 1)
                    x_high(0, V_PRE)

                    def silu_x(c):
                        a.wait_ge(S["conv3"], c + 1)
                        a.activation(XB[:, c, :], XB[:, c, :], ACT.Silu).then_inc(S["xb"], 1)

                    m = 0
                    for n in range(N_IN):
                        hi(n + 1)
                        for _ in range(1 if n == 0 else 2):
                            a.wait_ge(S["proj"], m + 1)
                            src = PS[:, m % 8, :]
                            if m == 0:
                                a.activation(SM[:, :], src[0:40, :], ACT.Copy).then_inc(S["act_ev"], 1)
                            elif m < 9:
                                c = m - 1
                                a.activation(XB[:, c, :], src, ACT.Identity, bias=VC[:, V_CB + c:V_CB + c + 1],
                                             scale=VC[:, V_CW + 24 + c:V_CW + 25 + c]).then_inc(S["conv0"], 1)
                                if c:
                                    silu_x(c - 1)
                            elif m < 13:
                                if m == 9:
                                    silu_x(7)
                                a.activation(ZS[:, m - 9, :], src, ACT.Silu).then_inc(S["act_ev"], 1)
                            else:
                                i = m - 13
                                a.activation(CQ[:, i, :], src, ACT.Copy)
                                if i >= 2:
                                    a.wait_ge(S["sq_add"], max(1, i - 2))
                                a.activation(E[:, i % 2, :], src, ACT.Square).then_inc(S["act_ev"], 1)
                            m += 1
                    rsqrt_wide(0)
                    rsqrt_wide(1)

                    a.wait_ge(S["broad"], N_BROAD)
                    a.activation(ALOG[:, :], ALOG[:, :], ACT.Exp)
                    a.wait_ge(S["dt_n"], 1)
                    a.activation(DTT[:, 5, :], DTT[:, 4, :], ACT.Exp).then_inc(S["dt_e"], 1)
                    a.wait_ge(S["dt_n"], 2)
                    a.activation(DTT[:, 7, :], DTT[:, 6, :], ACT.Ln).then_inc(S["dt_l"], 1)

                    for g in range(GROUPS):
                        a.wait_ge(S["btok"], g + 1)
                        a.activation(BT[:, :, :], PS[:, 2, :].rearrange("p (c n) -> p c n", c=TT), ACT.Copy
                                     ).then_inc(S["bt"], 1)
                        for hh in range(HG):
                            a.wait_ge(S["dd"], HG * g + hh + 1)
                            a.activation(E[:, hh, :], E[:, hh, :], ACT.Exp).then_inc(S["e_ready"], 1)
                        a.activation(CLX[:, g], CLX[:, g], ACT.Exp).then_inc(S["cdx"], 1)
                        for jj in range(2):
                            a.wait_ge(S["yec"], 2 * g + jj + 1)
                            if jj:
                                a.wait_ge(S["y_done"], 2 * g + 1)
                            a.activation(SCR[:, 1, P:SEQ], PS[:, jj, P:SEQ], ACT.Exp).then_inc(S["yexp"], 1)
                        for jj in range(2):
                            a.wait_ge(S["y_done"], 2 * g + jj + 1)
                            a.activation(E[:, 2 * jj, :], Y[:, jj, :], ACT.Square).then_inc(S["ysq"], 1)
                        rsqrt_wide(2 + g)
                        for jj in range(2):
                            a.wait_ge(S["y_n"], 2 * g + jj + 1)
                            a.activation(XH[:, 4 + 2 * g + jj, :], Y[:, jj, :], ACT.Copy).then_inc(S["yhi"], 1)

                    def c_high(i):
                        if i == 0:
                            a.wait_ge(S["ylo"], 4)
                        if i == 4 or i == 6:
                            a.wait_ge(S["w_used"], (i - 4) // 2 + 1)
                        a.activation(CH[:, i % 4, :], CQ[:, i, :], ACT.Copy).then_inc(S["ch"], 1)

                    for i in range(4):
                        c_high(i)
                    for n in range(N_UQ, N_OUT):
                        hi(n + 1)
                        if n < N_UQ + 2:
                            for i in range(2):
                                c_high(4 + 2 * (n - N_UQ) + i)
                        elif n == N_UQ + 2:
                            for j in range(4):
                                a.wait_ge(S["q_done"], j + 1)
                                a.activation(Q[0:NOPE, 2 * j, :], PS[0:64, j, :], ACT.Copy)
                                a.activation(Q[0:NOPE, 2 * j + 1, :], PS[64:128, j, :], ACT.Copy
                                             ).then_inc(S["q_ev"], 1)
                            a.wait_ge(S["kro"], 1)
                            for t in range(2):
                                a.wait_ge(S["q_done"], 5 + t)
                                ins = a.activation(SCR[:, t, :], PS[:, 4 + t, :], ACT.Copy)
                                ins.then_inc(S["q_rr"], 1)
                        else:
                            for t in range(TT):
                                a.wait_ge(S["kv_done"], 5 + t)
                                a.activation(V[:, t, :], PS[:, (10 + t) % 8, :], ACT.Copy).then_inc(S["v_ev"], 1)
                            for t in range(2):
                                a.wait_ge(S["q_ro"], t + 1)
                                for i in range(4):
                                    a.activation(Q[NOPE:QK, 4 * t + i, :], SCR[ROPE * i:ROPE * i + ROPE, t, :],
                                                 ACT.Copy).then_inc(S["q_rc"], 1)
                    hi(N_OUT + 1)

                    def p_transposed(h):
                        for j in (0, 2):
                            a.wait_ge(S["pt_done"], TT * h + j + 1)
                            if j == 0 and h:
                                a.wait_ge(S["pv"], h)
                            a.activation(PT[:, j, P * j:SEQ], PS[:, 4, P * j:SEQ], ACT.Copy).then_inc(S["pt_a"], 1)
                        if h % 2:
                            a.wait_ge(S["pv"], h + 1)
                            a.activation(XH[:, h // 2, :], PS[:, 6 + (h // 2) % 2, :], ACT.Copy).then_inc(S["o_hi"], 1)

                    for h in range(HEADS):
                        a.wait_ge(S["nm"], h + 1)
                        if h >= 2:
                            a.wait_ge(S["pt_done"], TT * (h - 1))
                        for i in range(TT):
                            n = P * (i + 1)
                            a.activation(PR[:, h % 2, i, 0:n], PS[:, i, 0:n], ACT.Exp, bias=NM[:, h, i:i + 1],
                                         scale=SCALE, accum_out=RSUM[:, h, i:i + 1]).then_inc(S["p_done"], 1)
                        if h:
                            p_transposed(h - 1)
                    p_transposed(HEADS - 1)

                    for n in range(N_OUT, N_OUT + 3):
                        hi(n + 2)
                    norm(1, lambda t: (PS[:, 2 * t:2 * t + 2, :], (S["o_done"], t + 1)))
                    norm(2, lambda t: (H[:, t, :], (S["h_done"], t + 1)))
                    x_high(1, V_MLP)

                    def quarter(q, last):
                        for i in range(8):
                            if not (last and i == 7):
                                hi_next(i, q)
                            if i < 4:
                                for f in (2 * i, 2 * i + 1):
                                    a.wait_ge(S["up_done"], q * 8 + f + 1)
                                    a.wait_ge(S["a_done"], q * 8 + f + 3)
                                    a.activation(RELU[:, f % 2, :], PS[:, 4 + f % 4, :], ACT.Relu
                                                 ).then_inc(S["relu"], 1)
                                for f in (2 * i, 2 * i + 1):
                                    a.wait_ge(S["a_done"], q * 8 + f + 5)
                                    a.activation(AH[:, f, :], SQR[:, f % 2, :], ACT.Copy).then_inc(S["act_hi"], 1)

                    def hi_next(i, q):
                        n = N_MLP + i + 1
                        chunk_ready(a, n, q)
                        chunk_used(a, n - SPLIT, q)
                        a.activation(w_view(WH, n, n % SPLIT), w_view(RAW, n, n % RING), ACT.Copy).then_inc(S["hi_done"], 1)

                    with a.Fori(0, QUARTERS - 1) as q:
                        quarter(q, False)
                    quarter(QUARTERS - 1, True)
                    a.wait_ge(S["down_free"], 8 * QUARTERS + 8)
                    norm(3, lambda t: (MACC[:, t, :], None))

                @block.vector
                def _(v):
                    n_steps = [0]

                    def step(ins):
                        n_steps[0] += 1
                        ins.then_inc(S["dve_step"], 1)
                        v.wait_ge(S["dve_step"], n_steps[0])

                    def lo(n, q=None):
                        v.wait_ge(S["hi_done"], n + 1 if q is None else q * 8 + n + 1)
                        for (raw, h, l), last in cuts(n):
                            ins = v.tensor_tensor(l, raw, f32(h), ALU.subtract)
                            if last:
                                ins.then_inc(S["lo_done"], 1)

                    def newton(i):
                        v.wait_ge(S["ssq"], TT * (i + 1))
                        v.tensor_scalar(N4[:, 1, :], N4[:, 0, :], 1 / D_MODEL, EPS, ALU.mult, ALU.add
                                        ).then_inc(S["nrm_x"], 1)
                        v.wait_ge(S["nrm_y"], i + 1)
                        step(v.tensor_tensor(T4[:, :], N4[:, 3, :], N4[:, 3, :], ALU.mult))
                        step(v.scalar_tensor_tensor(T4[:, :], T4[:, :], -0.5, N4[:, 1, :], ALU.mult, ALU.mult))
                        step(v.scalar_tensor_tensor(N4[:, 4, :], T4[:, :], 1.5, N4[:, 3, :], ALU.add, ALU.mult))

                    def pre_norm(i):
                        newton(i)
                        for t in range(TT):
                            v.tensor_scalar(UTOK[:, t, :], H[:, t, :], N4[:, 4, t:t + 1], None, ALU.mult
                                            ).then_inc(S["utok"], 1)

                    def x_low(i, col):
                        for k in range(KD):
                            v.wait_ge(S["xh"], KD * i + k + 1)
                            v.scalar_tensor_tensor(XL[:, k, :], PS[:, k, :], VC[:, col + k:col + k + 1],
                                                   f32(XH[:, k, :]), ALU.mult, ALU.subtract).then_inc(S["xl"], 1)

                    def post_norm(i, source):
                        newton(i)
                        for t in range(TT):
                            x = source(t)
                            two = (lambda z: z) if len(x.shape) == 2 else (
                                lambda z: z.rearrange("p (a b) -> p a b", a=2))
                            step(v.scalar_tensor_tensor(two(UTOK[:, t, :]), x, N4[:, 4, t:t + 1], two(POST[:, :]),
                                                        ALU.mult, ALU.mult))
                            v.tensor_tensor(H[:, t, :], H[:, t, :], UTOK[:, t, :], ALU.add).then_inc(S["h_done"], 1)

                    def rsqrt_wide(i, src, count):
                        x, y, r = SCR[:, 2, :], SCR[:, 0, :], SCR[:, 1, :]
                        v.tensor_scalar(x, src, 1 / count, EPS, ALU.mult, ALU.add).then_inc(S["rsb_x"], 1)
                        v.wait_ge(S["rsb_y"], i + 1)
                        step(v.tensor_tensor(r, y, y, ALU.mult))
                        step(v.scalar_tensor_tensor(r, r, -0.5, x, ALU.mult, ALU.mult))
                        step(v.scalar_tensor_tensor(r, r, 1.5, y, ALU.add, ALU.mult))

                    pre_norm(0)
                    lo(0)
                    v.wait_ge(S["vc"], 1)
                    x_low(0, V_PRE)

                    for n in range(N_IN):
                        lo(n + 1)
                        if 1 <= n < 5:
                            for c in (2 * n - 2, 2 * n - 1):
                                v.wait_ge(S["conv0"], c + 1)
                                for s in range(1, TAPS):
                                    w = V_CW + 8 * (TAPS - 1 - s) + c
                                    ins = v.scalar_tensor_tensor(XB[:, c, s:SEQ], PS[:, (c + 1) % 8, 0:SEQ - s],
                                                                 VC[:, w:w + 1], XB[:, c, s:SEQ], ALU.mult, ALU.add)
                                    if s < TAPS - 1:
                                        step(ins)
                                ins.then_inc(S["conv3"], 1)

                    for i, (tiles, count) in enumerate(((range(6), Q_RANK), (range(6, 8), KV_RANK))):
                        v.wait_ge(S["cssq"], i + 1)
                        rsqrt_wide(i, PS[:, i, :], count)
                        for c in tiles:
                            v.scalar_tensor_tensor(CQ[:, c, :], CQ[:, c, :], VC[:, V_Q + c:V_Q + c + 1], SCR[:, 1, :],
                                                   ALU.mult, ALU.mult).then_inc(S["cqn"], 1)

                    v.wait_ge(S["dt_t"], 1)
                    v.wait_ge(S["broad"], N_BROAD)
                    for hl in range(2):
                        rows = slice(64 * hl, 64 * hl + 64)
                        v.tensor_copy(DSK[rows, :], DSKB[rows, hl::2])
                    th = lambda w: w.rearrange("p (t h) -> p t h", t=TT)
                    every_t = lambda w: w.unsqueeze(1).to_broadcast([P, TT, S_HEADS])
                    step(v.tensor_tensor(th(DT), th(PS[:, 2, 0:32]), every_t(DTB[:, :]), ALU.add))
                    step(v.tensor_scalar(DTT[:, 3, :], DT, -1.0, None, ALU.mult))
                    v.tensor_tensor(DTT[:, 4, :], DT, DTT[:, 3, :], ALU.min).then_inc(S["dt_n"], 1)
                    v.wait_ge(S["dt_e"], 1)
                    v.tensor_scalar(DTT[:, 6, :], DTT[:, 5, :], 1.0, None, ALU.add).then_inc(S["dt_n"], 1)
                    v.wait_ge(S["dt_n"], 2)
                    step(v.tensor_scalar(DTT[:, 3, :], DTT[:, 6, :], 1.0, 1e-30, ALU.subtract, ALU.max))
                    step(v.reciprocal(DTT[:, 3, :], DTT[:, 3, :]))
                    v.wait_ge(S["dt_l"], 1)
                    step(v.tensor_tensor(DTT[:, 3, :], DTT[:, 3, :], DTT[:, 5, :], ALU.mult))
                    step(v.tensor_tensor(DTT[:, 3, :], DTT[:, 3, :], DTT[:, 7, :], ALU.mult))
                    step(v.scalar_tensor_tensor(DT, DT, 0.0, DTT[:, 3, :], ALU.max, ALU.add))
                    v.scalar_tensor_tensor(th(AA), th(DT), -1.0, every_t(ALOG[:, :]), ALU.mult, ALU.mult
                                           ).then_inc(S["a_ready"], 1)
                    v.wait_ge(S["cst"], 1)
                    v.tensor_copy(CST, PS[:, 3, 0:32]).then_inc(S["cst_ready"], 1)
                    v.wait_ge(S["cst_ready"], 1)

                    for g in range(GROUPS):
                        v.wait_ge(S["cb"], g + 1)
                        blocks = lambda w: w.rearrange("p (c l) -> p c l", c=TT)
                        v.tensor_tensor(blocks(CBM[:, :]), blocks(PS[:, 3, :]),
                                        tri.unsqueeze(1).to_broadcast([P, TT, P]), ALU.mult).then_inc(S["cbm"], 1)
                        for hh in range(HG):
                            v.wait_ge(S["csb"], HG * g + hh + 1)
                            bank = PS[:, 4 + hh, :]
                            for c in range(TT):
                                col = S_HEADS * c + HG * g + hh
                                v.tensor_scalar(E[:, hh, P * c:P * c + P], bank[:, P * c:P * c + P],
                                                CST[:, col:col + 1], 0.0, ALU.subtract, ALU.min)
                            v.tensor_copy(CLX[:, g, hh, :], bank[:, P - 1:SEQ:P]).then_inc(S["dd"], 1)
                        for i in range(2):
                            v.wait_ge(S["xs_t"], 2 * g + i + 1)
                            chp = lambda w: w.rearrange("p (c h d) -> p c h d", c=2, h=HG)
                            dt4 = th(DT)[:, 2 * i:2 * i + 2, HG * g:HG * g + HG].unsqueeze(3).to_broadcast([P, 2, HG, 64])
                            v.tensor_tensor(XD[:, 2 * i:2 * i + 2, :].rearrange("p c (h d) -> p c h d", h=HG),
                                            chp(PS[:, i, :]), dt4, ALU.mult).then_inc(S["xd"], 1)
                        v.wait_ge(S["xdd"], 3 * g + 3)
                        v.wait_ge(S["cbm"], g + 1)
                        for hh in range(HG):
                            v.wait_ge(S["e_ready"], HG * g + hh + 1)
                            v.tensor_tensor(E[:, hh, :], E[:, hh, :], CBM[:, :], ALU.mult).then_inc(S["m_ready"], 1)
                        v.wait_ge(S["st_mm"], 3 * g + 2)
                        v.tensor_copy(ST[:, 0, :], PS[:, 2, 0:256]).then_inc(S["st_ready"], 1)
                        v.wait_ge(S["cdx"], g + 1)
                        for c in (1, 2):
                            v.wait_ge(S["st_ready"], 3 * g + c)
                            hd = lambda w: w.rearrange("p (h d) -> p h d", h=HG)
                            step(v.tensor_tensor(hd(SCR[:, 2, 0:256]), hd(ST[:, c - 1, :]),
                                                 CLX[:, g, :, c:c + 1].to_broadcast([P, HG, 64]), ALU.mult))
                            v.wait_ge(S["st_mm"], 3 * g + c + 1)
                            v.tensor_tensor(ST[:, c, :], SCR[:, 2, 0:256], PS[:, 2 + c // 2, 256 * (c % 2):256 * (c % 2) + 256],
                                            ALU.add).then_inc(S["st_ready"], 1)
                        for jj in range(2):
                            j = 2 * g + jj
                            y = Y[:, jj, :]
                            v.wait_ge(S["yexp"], j + 1)
                            v.wait_ge(S["yo"], j + 1)
                            step(v.tensor_tensor(SCR[:, 0, P:SEQ], PS[:, 6 + jj, P:SEQ], SCR[:, 1, P:SEQ], ALU.mult))
                            step(v.scalar_tensor_tensor(y, XB[:, j, :], DSK[:, j:j + 1], PS[:, 4 + jj, :],
                                                        ALU.mult, ALU.add))
                            step(v.tensor_tensor(y[:, P:SEQ], y[:, P:SEQ], SCR[:, 0, P:SEQ], ALU.add))
                            v.tensor_tensor(y, y, ZS[:, j, :], ALU.mult).then_inc(S["y_done"], 1)
                        v.wait_ge(S["yssq"], g + 1)
                        rsqrt_wide(2 + g, PS[:, 2, :], INNER // GROUPS)
                        for jj in range(2):
                            w = V_SSD + 2 * g + jj
                            v.scalar_tensor_tensor(Y[:, jj, :], Y[:, jj, :], VC[:, w:w + 1], SCR[:, 1, :],
                                                   ALU.mult, ALU.mult).then_inc(S["y_n"], 1)
                        for jj in range(2):
                            k = 2 * g + jj
                            v.wait_ge(S["yhi"], k + 1)
                            v.tensor_tensor(XL[:, 4 + k, :], Y[:, jj, :], f32(XH[:, 4 + k, :]), ALU.subtract
                                            ).then_inc(S["ylo"], 1)

                    v.wait_ge(S["kswap"], 1)
                    r = slice(0, ROPE)
                    v.tensor_tensor(SCR[r, 2, :], SM[r, :], COS[r, :], ALU.mult)
                    step(v.tensor_tensor(SCR[r, 1, :], PS[r, 7, :], SIN[r, :], ALU.mult))
                    step(v.tensor_tensor(SCR[r, 2, :], SCR[r, 2, :], SCR[r, 1, :], ALU.add))
                    v.tensor_copy(K[NOPE:QK, :, :], SCR[r, 2, :].unsqueeze(1).to_broadcast([ROPE, HEADS, SEQ])
                                  ).then_inc(S["kro"], 1)

                    def c_low(i):
                        v.wait_ge(S["ch"], i + 1)
                        v.tensor_tensor(CL[:, i % 4, :], CQ[:, i, :], f32(CH[:, i % 4, :]), ALU.subtract
                                        ).then_inc(S["cl"], 1)

                    for i in range(4):
                        c_low(i)
                    for n in range(N_UQ, N_OUT):
                        lo(n + 1)
                        if n < N_UQ + 2:
                            for i in range(2):
                                c_low(4 + 2 * (n - N_UQ) + i)
                        elif n == N_OUT - 1:
                            for u in range(4):
                                v.wait_ge(S["kv_done"], u + 1)
                                bank = (6 + u) % 8
                                v.tensor_copy(K[0:NOPE, 2 * u, :], PS[0:64, bank, :])
                                v.tensor_copy(K[0:NOPE, 2 * u + 1, :], PS[64:128, bank, :]).then_inc(S["k_ev"], 1)
                            for t in range(2):
                                v.wait_ge(S["qswap"], t + 1)
                                step(v.tensor_tensor(SCR[:, 2, :], SCR[:, t, :], COS[:, :], ALU.mult))
                                step(v.tensor_tensor(SCR[:, t, :], PS[:, 6 + t, :], SIN[:, :], ALU.mult))
                                v.tensor_tensor(SCR[:, t, :], SCR[:, t, :], SCR[:, 2, :], ALU.add
                                                ).then_inc(S["q_ro"], 1)
                                v.wait_ge(S["q_ro"], t + 1)
                    lo(N_OUT + 1)

                    def p_transposed(h):
                        for j in (1, 3):
                            v.wait_ge(S["pt_done"], TT * h + j + 1)
                            if j == 1 and h:
                                v.wait_ge(S["pv"], h)
                            v.tensor_copy(PT[:, j, P * j:SEQ], PS[:, 5, P * j:SEQ]).then_inc(S["pt_d"], 1)
                        if h % 2:
                            p = h // 2
                            v.wait_ge(S["o_hi"], p + 1)
                            v.tensor_tensor(XL[:, p, :], PS[:, 6 + p % 2, :], f32(XH[:, p, :]), ALU.subtract
                                            ).then_inc(S["o_lo"], 1)

                    for h in range(HEADS):
                        for i in range(TT):
                            v.wait_ge(S["s_done"], TT * h + i + 1)
                            ins = v.tensor_reduce(MX[:, h, i:i + 1], PS[:, i, 0:P * (i + 1)], AX, ALU.max)
                        step(ins)
                        v.tensor_scalar(NM[:, h, :], MX[:, h, :], -SCALE, None, ALU.mult).then_inc(S["nm"], 1)
                        if h:
                            p_transposed(h - 1)
                        v.wait_ge(S["p_done"], TT * (h + 1))
                        step(v.reciprocal(RINV[:, h, :], RSUM[:, h, :]))
                        for i in range(TT):
                            pr = PR[:, h % 2, i, 0:P * (i + 1)]
                            ins = v.tensor_scalar(pr, pr, RINV[:, h, i:i + 1], None, ALU.mult)
                        ins.then_inc(S["pn"], 1)
                    p_transposed(HEADS - 1)

                    for n in range(N_OUT, N_OUT + 3):
                        lo(n + 2)
                    post_norm(1, lambda t: PS[:, 2 * t:2 * t + 2, :])
                    v.wait_ge(S["h_done"], TT)
                    pre_norm(2)
                    x_low(1, V_MLP)

                    def quarter(q, last):
                        for i in range(8):
                            if not (last and i == 7):
                                n = N_MLP + i + 1
                                v.wait_ge(S["hi_done"], q * 8 + n + 1)
                                v.tensor_tensor(w_view(WL, n, n % SPLIT), w_view(RAW, n, n % RING),
                                                f32(w_view(WH, n, n % SPLIT)), ALU.subtract).then_inc(S["lo_done"], 1)
                            if i < 4:
                                for f in (2 * i, 2 * i + 1):
                                    v.wait_ge(S["relu"], q * 8 + f + 1)
                                    v.wait_ge(S["act_lo"], q * 8 + f + 1)
                                    v.scalar_tensor_tensor(SQR[:, f % 2, :], PS[:, 4 + f % 4, :], 0.0,
                                                           RELU[:, f % 2, :], ALU.max, ALU.mult
                                                           ).then_inc(S["a_done"], 1)
                            elif i % 2:
                                half = (i - 4) // 2
                                v.wait_ge(S["down_done"], q * 4 + i - 2)
                                for t in range(TT):
                                    acc = MACC[:, t, 512 * half:512 * half + 512]
                                    v.wait_ge(S["down_free"], q * 8 + 4 * half + t + 1)
                                    v.tensor_tensor(acc, acc, PS[:, t, :], ALU.add).then_inc(S["down_free"], 1)

                    v.wait_ge(S["macc0"], 1)
                    with v.Fori(0, QUARTERS - 1) as q:
                        quarter(q, False)
                    quarter(QUARTERS - 1, True)
                    v.wait_ge(S["post_mlp"], 16)
                    v.wait_ge(S["down_free"], 8 * QUARTERS + 8)
                    post_norm(3, lambda t: MACC[:, t, :])

                @block.gpsimd
                def _(g_):
                    g_.sem_inc(S["down_done"], 1)
                    g_.sem_inc(S["a_done"], 4)
                    g_.sem_inc(S["act_lo"], 2)
                    g_.sem_inc(S["down_free"], 8)
                    for i in range(6):
                        g_.wait_ge(S["act_ev"], 5 + (2 if i == 0 else i + 2 if i < 5 else 8))
                        if i in (0, 5):
                            ins = g_.tensor_tensor(E[:, 2 + i // 5, :], E[:, 0, :], E[:, 1, :], ALU.add)
                        else:
                            g_.wait_ge(S["sq_add"], i)
                            ins = g_.tensor_tensor(E[:, 2, :], E[:, 2, :], E[:, (i + 1) % 2, :], ALU.add)
                        ins.then_inc(S["sq_add"], 1)
                    for g in range(GROUPS):
                        g_.wait_ge(S["e_ready"], HG * (g + 1))
                        for c in range(TT - 1):
                            g_.wait_ge(S["xd"], 2 * g + c // 2 + 1)
                            end = E[:, :, P * c + P - 1:P * c + P].to_broadcast([P, HG, 64])
                            g_.tensor_tensor(XDD[:, c, :].rearrange("p (h d) -> p h d", h=HG),
                                             XD[:, c, :].rearrange("p (h d) -> p h d", h=HG), end, ALU.mult
                                             ).then_inc(S["xdd"], 1)
                    g_.wait_ge(S["o_done"], TT)
                    g_.memset(MACC[:, :, :], 0.0).then_inc(S["macc0"], 1)
                    with g_.Fori(0, QUARTERS) as q:
                        for f in range(8):
                            g_.wait_ge(S["act_hi"], q * 8 + f + 1)
                            g_.tensor_tensor(AL[:, f, :], SQR[:, f % 2, :], f32(AH[:, f, :]), ALU.subtract
                                             ).then_inc(S["act_lo"], 1)

            nc.all_engine_barrier(sems_to_clear=range(first.num, final.num + 1))

        with nc.Block() as block:
            @block.sync
            def _(sp):
                sp.dma_start(out.rearrange("a (t p) d -> p (a t) d", p=P), H[:, :, :]).then_inc(stored, 16)
                sp.wait_ge(stored, 16)


_INS = ["x", "positions", "pre_mix_norm", "w_in", "q_norm", "w_uq", "kv_norm", "w_ukv", "conv_w", "conv_b",
        "dt_bias", "a_log", "d_skip", "ssd_norm", "w_out", "post_mix_norm", "pre_mlp_norm", "w_up",
        "w_down", "post_mlp_norm"]


def kernel(**inputs):
    import concourse.bacc as _bacc
    from concourse import mybir as _mybir
    from concourse.bass_utils import run_bass_kernel_spmd as _run

    nc = _bacc.Bacc("TRN2", target_bir_lowering=False, num_devices=1)
    arrays, args = {}, {}
    for name in _INS:
        a = np.ascontiguousarray(inputs[name])
        arrays[f"in_{name}_dram"] = a
        args[name] = nc.dram_tensor(f"in_{name}_dram", a.shape, _mybir.dt.from_np(a.dtype), kind="ExternalInput").ap()
    arrays["constants_dram"] = constants()
    consts = nc.dram_tensor("constants_dram", (P, N_CONST), _mybir.dt.float32, kind="ExternalInput").ap()
    out = nc.dram_tensor("out_0_dram", (1, SEQ, D_MODEL), _mybir.dt.float32, kind="ExternalOutput").ap()
    trunk(nc, args, consts, out)
    r = _run(nc, [arrays], core_ids=[0])
    return r.results[0]["out_0_dram"]
```

```python
from contextlib import ExitStack

import numpy as np

import concourse.bass as bass
from concourse import mybir

F32 = mybir.dt.float32
F32R = mybir.dt.float32r
BF16 = mybir.dt.bfloat16
I32 = mybir.dt.int32
ACT = mybir.ActivationFunctionType
ALU = mybir.AluOpType
AX = mybir.AxisListType.X

P = 128
EPS = 1e-6
NEG = -1e30

D_MODEL, SEQ, DEPTH = 1024, 512, 2
HEADS, NOPE, ROPE, VDIM = 8, 64, 32, 64
QK = NOPE + ROPE
Q_RANK, KV_RANK = 768, 256
S_HEADS, GROUPS, STATE, TAPS = 8, 2, 128, 4
INNER = S_HEADS * 64
CONV = INNER + 2 * GROUPS * STATE
D_FF = 4 * D_MODEL
CHUNK = 64
TT = SEQ // P
KD = D_MODEL // P
HG = S_HEADS // GROUPS
SCALE = float(QK) ** -0.5

C_KV = Q_RANK
C_KR = C_KV + KV_RANK
C_Z = C_KR + ROPE
C_XBC = C_Z + INNER
C_DT = C_XBC + CONV

K_ID, K_TRI, K_ONE, K_SWAP, K_FREQ, K_SIGN = 0, 128, 256, 384, 512, 513
N_CONST = 514

V_Q, V_KV, V_CW, V_CB, V_SSD = 0, 6, 8, 40, 48
N_VEC = 52

RING, SPLIT = 4, 2
N_IN = 11
N_UQ = N_IN
N_UKV = N_UQ + 3
N_OUT = N_UKV + 1
N_MLP = N_OUT + 4
QUARTERS = 4
OUT_ROWS = ((4, 5), (6, 7), (0, 1), (2, 3))


def constants():
    c = np.zeros((P, N_CONST), np.float32)
    i = np.arange(P)
    c[:, K_ID:K_ID + P] = np.eye(P)
    c[:, K_TRI:K_TRI + P] = i[:, None] <= i[None, :]
    c[:, K_ONE:K_ONE + P] = 1
    c[i, K_SWAP + (i ^ (ROPE // 2))] = 1
    half = np.arange(0, ROPE, 2, dtype=np.float32)
    c[:, K_FREQ] = (np.float32(10000.0) ** (-half / np.float32(ROPE)))[i % (ROPE // 2)]
    c[:, K_SIGN] = np.where(i % ROPE < ROPE // 2, -1, 1)
    return c


def two_pi_parts():
    parts, rest = [], 2 * np.pi
    for _ in range(2):
        e = np.floor(np.log2(rest)) - 10
        parts.append(float(np.floor(rest / 2 ** e) * 2 ** e))
        rest -= parts[-1]
    return parts + [float(rest)]


S_UNITS = ((3,), (2, 0), (1,))
S_BANK = {3: (0, 0), 2: (1, 0), 0: (1, 384), 1: (2, 0)}
P_AT = {3: 0, 2: 512, 0: 896, 1: 1024}
M_SLOT = {3: 0, 2: 1, 0: 2, 1: 3}
T_UNITS = ((2,), (3, 1), (0,))
T_BANK = {0: (3, 0), 1: (4, 0), 3: (4, 384), 2: (5, 0)}
T_AT = {0: 0, 1: 512, 3: 896, 2: 1024}
PACKED = 1280


def trunk(nc, A, consts, out):
    ctx = ExitStack()
    with ctx:
        def sb(name, shape, dt=F32, stack=ctx):
            return stack.enter_context(nc.sbuf_tensor(name, shape, dt))

        H = sb("h", [P, TT, D_MODEL])
        XH = sb("x_hi", [P, KD, SEQ], F32R)
        XL = sb("x_lo", [P, KD, SEQ], F32R)
        RAW = sb("w_raw", [P, RING, 2048])
        WH = sb("w_hi", [P, SPLIT, 2048], F32R)
        WL = sb("w_lo", [P, SPLIT, 2048], F32R)
        COS = sb("cos", [P, SEQ])
        SIN = sb("sin", [P, SEQ])
        POST = sb("post_w", [P, D_MODEL])
        CT = sb("consts", [P, N_CONST])
        VEC = sb("vec_rows", [N_VEC, P])
        VC = sb("vec_cols", [P, N_VEC])
        SCR = sb("scratch", [P, 3, SEQ])
        DTB = sb("dt_bias_b", [P, S_HEADS])
        ALOG = sb("a_log_b", [P, S_HEADS])
        DSKB = sb("d_skip_b", [P, S_HEADS])
        DSK = sb("d_skip_rows", [P, S_HEADS // 2])
        N4 = sb("norm_small", [P, 7, TT])
        TRIR = sb("tri_r", [P, P], F32R)
        AHL = sb("a_halves", [P, 2, TT * S_HEADS], F32R)
        SQ = sb("squares", [P, SEQ])
        SQA = sb("squares_sum", [P, SEQ])
        SELB = sb("first_chunk", [1, P], BF16)
        MASKB = sb("mask_row", [1, CHUNK], BF16)
        DTT = sb("dt_small", [P, 8, TT * S_HEADS])
        DT, AA, CST = DTT[:, 0, :], DTT[:, 1, :], DTT[:, 2, :]
        CLX = sb("chunk_log", [P, 2, HG, TT])
        MX = sb("row_max", [P, HEADS, TT])
        NM = sb("neg_max", [P, HEADS, TT])
        RSUM = sb("row_sum", [P, HEADS, TT])
        RINV = sb("row_inv", [P, HEADS, TT])

        def union(*variants):
            got, most = [], 0
            for v in variants:
                with ExitStack() as s:
                    got.append([sb(n, shape, dt, s) for n, shape, dt in v])
                most = max(most, sum(4 * int(np.prod(shape[1:])) for _, shape, _ in v))
            sb(variants[0][0][0] + "_zone", [P, most // 4])
            return got

        SM = sb("krope_dt", [40, SEQ])
        (CQ,), (V, PT0), (UTOK,), (RELU, SQR) = union(
            [("c_rows", [P, 8, SEQ], F32)],
            [("v", [P, TT, HEADS * VDIM], F32), ("p_t0", [P, PACKED], F32)],
            [("u_tok", [P, TT, D_MODEL], F32)],
            [("relu", [P, 2, SEQ], F32), ("relu_sq", [P, 2, SEQ], F32)],
        )
        (XB, ZS, E, XD, XDD, BT, CBM, ST, Y), (Q, K), (_q, _k, PR, PT1), (MACC, AH, AL), (_, PREB) = union(
            [("xbc", [P, 8, SEQ], F32), ("z_silu", [P, 4, SEQ], F32), ("decay", [P, HG, SEQ], F32),
             ("xdt", [P, TT, HG * 64], F32), ("xdt_dec", [P, TT - 1, HG * 64], F32),
             ("b_tok", [P, TT, STATE], F32), ("cb", [P, SEQ], F32),
             ("state", [P, TT - 1, HG * 64], F32), ("y", [P, 2, SEQ], F32)],
            [("q", [QK, HEADS, SEQ], F32), ("k", [QK, HEADS, SEQ], F32)],
            [("q_", [QK, HEADS, SEQ], F32), ("k_", [QK, HEADS, SEQ], F32),
             ("probs", [P, 2, PACKED], F32), ("p_t1", [P, PACKED], F32)],
            [("mlp_acc", [P, TT, D_MODEL], F32), ("act_hi", [P, 8, SEQ], F32R),
             ("act_lo", [P, 8, SEQ], F32R)],
            [("pre_pad", [P, 47 * 256], F32), ("pre_w", [P, D_MODEL], F32)],
        )
        PT = (PT0, PT1)
        PS = ctx.enter_context(nc.psum_tensor("ps", [P, 8, 512], F32))

        ident, tri, ones = CT[:, K_ID:K_ID + P], CT[:, K_TRI:K_TRI + P], CT[:, K_ONE:K_ONE + P]
        swap = CT[:, K_SWAP:K_SWAP + P]

        def f32(ap):
            return ap.bitcast(F32)

        SIDE = [9, 10, 11, 12, 13, 14, 15, 16, 17, "q", 18, 19, 20]
        Z_TILES = (9, 10, 17, 18)
        C_TILES = (11, 12, 13, 14, 15, 16, 19, 20)
        KV_BANK = (4, 5, 2, 3, 0, 1, 4, 5)

        NORMS = ([(0, t) for t in range(TT)] + [(1, 0), (1, 1), (2, 0), (1, 2), (2, 1), (1, 3), (2, 2), (2, 3)]
                 + [(3, t) for t in range(TT)])

        def nth(i, t):
            return NORMS.index((i, t)) + 1

        def c_slot(i):
            return (i + 2) % 8

        def in_bank(item):
            if item == 0:
                return 0
            return SIDE.index(item) % 2 if item in SIDE else 1 + (item - 1) % 5

        names = """raw0 raw1 raw2 raw3 params broad pre_w post_mlp hi_done lo_done w_used
            ssq nrm_x nrm_y utok ut_done xh xl vec_t vc proj act_ev conv0 conv3 xb sq_add
            cssq rsb_x rsb_y cqn ch cl dt_t dt_n dt_e dt_l a_ready a_hi cst cst_ready btok bt cb cbm csb dd e_ready
            xs_t xd xdd m_ready cdx st_mm st_ready yexp yo yd y_done ysq yssq y_n yhi ylo zs
            kswap kro q_done q_ev q_rr qswap q_ro q_rc q_rd kv_done k_ev v_ev
            s_done mx nm p_done pn pt_done pt_a pt_d pv o_hi o_lo o_done
            macc0 up_done relu a_done act_hi act_lo down_k0 down_done down_free h_done
            dve_step act_step""".split()
        S = {n: ctx.enter_context(nc.semaphore(n)) for n in names}
        first, final = S[names[0]], S[names[-1]]
        (boot_ld, boot_h, boot_v, boot_a, boot_p, stored) = (
            ctx.enter_context(nc.semaphore(n)) for n in ("boot_ld", "boot_h", "boot_v", "boot_a", "boot_p", "stored"))

        with nc.Block() as block:
            @block.sync
            def _(sp):
                sp.dma_start(CT[:, :], consts[:, :]).then_inc(boot_ld, 16)
                sp.dma_start(SCR[:, 0, :].bitcast(I32),
                             A["positions"][0:1, :].to_broadcast([P, SEQ])).then_inc(boot_ld, 16)
                sp.dma_start(H[:, :, :], A["x"].rearrange("a (t p) d -> p (a t) d", p=P)).then_inc(boot_h, 16)
                sp.wait_ge(boot_h, 16)

            @block.vector
            def _(v):
                n = [0]

                def step(ins):
                    n[0] += 1
                    ins.then_inc(boot_v, 1)
                    v.wait_ge(boot_v, n[0])

                v.wait_ge(boot_ld, 32)
                pos, ang, turns = SCR[:, 1, :], SCR[:, 2, :], SQ[:, :]
                step(v.tensor_copy(pos, SCR[:, 0, :].bitcast(I32)))
                step(v.tensor_scalar(ang, pos, CT[:, K_FREQ:K_FREQ + 1], None, ALU.mult))
                magic = 1.5 * 2.0 ** 23
                step(v.tensor_scalar(turns, ang, float(1 / (2 * np.pi)), magic, ALU.mult, ALU.add))
                step(v.tensor_scalar(turns, turns, -magic, None, ALU.add))
                for part in two_pi_parts():
                    step(v.scalar_tensor_tensor(ang, turns, -part, ang, ALU.mult, ALU.add))
                step(v.tensor_scalar(SIN[:, :], ang, 3.1415925, -3.1415925, ALU.min, ALU.max))
                step(v.scalar_tensor_tensor(COS[:, :], SIN[:, :], -1.0, SIN[:, :], ALU.mult, ALU.max))
                step(v.tensor_scalar(COS[:, :], COS[:, :], -1.0, float(np.pi / 2), ALU.mult, ALU.add))
                v.wait_ge(boot_a, 1)
                v.tensor_scalar(SIN[:, :], SIN[:, :], CT[:, K_SIGN:K_SIGN + 1], None, ALU.mult)

            @block.scalar
            def _(a):
                a.wait_ge(boot_v, 10)
                a.activation(SIN[:, :], SIN[:, :], ACT.Sin).then_inc(boot_a, 1)
                a.activation(COS[:, :], COS[:, :], ACT.Sin)
                a.activation(TRIR[:, :], tri, ACT.Copy)

            @block.gpsimd
            def _(g_):
                g_.memset(SELB[:, :], 0.0).then_inc(boot_p, 1)
                g_.memset(MASKB[:, :], NEG)
                g_.wait_ge(boot_p, 1)
                g_.memset(SELB[:, 0:CHUNK], 1.0)

        def w_view(buf, n, slot):
            rows, cols = chunk_shape(n)
            return buf[:, slot, 0:rows * cols].rearrange("p (k n) -> p k n", k=rows)

        def chunk_shape(n):
            if n == 0:
                return KD, 40
            if n < N_UQ:
                return KD, 256
            if n < N_UKV:
                return 2, HEADS * QK
            if n < N_MLP:
                return 2, 1024
            return (KD, 256) if (n - N_MLP) % 8 < 4 else (4, 512)

        def split_parts(n, slot):
            raw, hi, lo = (w_view(b, n, s) for b, s in ((RAW, n % RING), (WH, slot), (WL, slot)))
            if N_UQ <= n < N_OUT:
                a, b = (NOPE, ROPE) if n < N_UKV else (NOPE, VDIM)
                r = raw.rearrange("p k (h c) -> p k h c", h=HEADS)
                cut = lambda w: ((w[:, :, 0:HEADS * a].rearrange("p k (h c) -> p k h c", h=HEADS)),
                                 (w[:, :, HEADS * a:HEADS * (a + b)].rearrange("p k (h c) -> p k h c", h=HEADS)))
                (h0, h1), (l0, l1) = cut(hi), cut(lo)
                return [x for k in range(2) for x in ((r[:, k, :, 0:a], h0[:, k], l0[:, k]),
                                                      (r[:, k, :, a:a + b], h1[:, k], l1[:, k]))]
            return [(raw, hi, lo)]

        with nc.Fori(0, DEPTH) as layer:
            with nc.Block() as block:

                def at(name):
                    return A[name][bass.ds(layer, 1)]

                @block.sync
                def _(sp):
                    sp.dma_start(PREB[:, :], at("pre_mix_norm").to_broadcast([P, D_MODEL])).then_inc(S["pre_w"], 16)
                    for name, row, n in (("q_norm", V_Q, 6), ("kv_norm", V_KV, 2), ("conv_b", V_CB, 8),
                                         ("ssd_norm", V_SSD, 4)):
                        sp.dma_start(VEC[row:row + n, :],
                                     at(name).rearrange("a (r c) -> (a r) c", c=P)).then_inc(S["params"], 16)
                    sp.dma_start(VEC[V_CW:V_CW + 32, :],
                                 at("conv_w").rearrange("a k (r c) -> (a k r) c", c=P)).then_inc(S["params"], 16)

                    def load(n, src):
                        if n >= RING:
                            sp.wait_ge(S["hi_done"], n - RING + 1)
                            sp.wait_ge(S["lo_done"], n - RING + 1)
                        sp.dma_start(w_view(RAW, n, n % RING), src).then_inc(S[f"raw{n % RING}"], 16)

                    def rows(name, r0, r1, c0, c1):
                        return at(name)[:, r0:r1, c0:c1].rearrange("a (k p) n -> p (a k) n", p=P)

                    small = w_view(RAW, 0, 0)
                    sp.dma_start(small[:, :, 0:ROPE], rows("w_in", 0, D_MODEL, C_KR, C_Z)).then_inc(S["raw0"], 16)
                    sp.dma_start(small[:, :, ROPE:40],
                                 rows("w_in", 0, D_MODEL, C_DT, C_DT + S_HEADS)).then_inc(S["raw0"], 16)
                    starts = ([C_XBC + 256 * i for i in range(4)] + [C_Z] + [256 * i for i in range(3)]
                              + [C_Z + 256, C_KV])
                    for i, c in enumerate(starts):
                        load(1 + i, rows("w_in", 0, D_MODEL, c, c + 256))
                        if i == 1:
                            for buf, name in ((DTB, "dt_bias"), (ALOG, "a_log"), (DSKB, "d_skip")):
                                sp.dma_start(buf[:, :], at(name).to_broadcast([P, S_HEADS])).then_inc(S["broad"], 16)
                            sp.dma_start(POST[:, :], at("post_mix_norm").to_broadcast([P, D_MODEL])
                                         ).then_inc(S["broad"], 16)
                    for i in range(3):
                        load(N_UQ + i, rows("w_uq", 256 * i, 256 * i + 256, 0, HEADS * QK))
                    load(N_UKV, rows("w_ukv", 0, KV_RANK, 0, HEADS * (NOPE + VDIM)))
                    for i, (k, _) in enumerate(OUT_ROWS):
                        load(N_OUT + i, rows("w_out", P * k, P * k + 256, 0, D_MODEL))
                    sp.wait_ge(S["y_n"], 4)
                    sp.dma_start(PREB[:, :], at("pre_mlp_norm").to_broadcast([P, D_MODEL])).then_inc(S["pre_w"], 16)
                    with sp.Fori(0, QUARTERS) as q:
                        for i in range(8):
                            n = N_MLP + i
                            if i < 4:
                                src = at("w_up")[:, :, bass.ds(q * 1024 + 256 * i, 256)]
                            else:
                                half, kk = (i - 4) // 2, (i - 4) % 2
                                src = at("w_down")[:, bass.ds(q * 1024 + 512 * kk, 512), 512 * half:512 * half + 512]
                            src = src.rearrange("a (k p) n -> p (a k) n", p=P)
                            sp.wait_ge(S["hi_done"], q * 8 + (n - RING + 1))
                            sp.wait_ge(S["lo_done"], q * 8 + (n - RING + 1))
                            sp.dma_start(w_view(RAW, n, n % RING), src).then_inc(S[f"raw{n % RING}"], 16)
                    sp.wait_ge(S["h_done"], TT)
                    sp.dma_start(POST[:, :], at("post_mlp_norm").to_broadcast([P, D_MODEL])
                                 ).then_inc(S["post_mlp"], 16)

                N_BROAD = 16 * 4

                def chunk_ready(eng, n, q=None):
                    value = 16 * (n // RING + 1) + (16 if n % RING == 0 else 0)
                    eng.wait_ge(S[f"raw{n % RING}"], value if q is None else value + q * 32)

                @block.tensor
                def _(pe):
                    def three(dst, w, x, start, stop):
                        for i, (a, b) in enumerate(((w[1], x[0]), (w[0], x[1]), (w[0], x[0]))):
                            last = pe.matmul(dst, a, b, start=start and i == 0, stop=stop and i == 2)
                        return last

                    def weights(n, q=None):
                        pe.wait_ge(S["lo_done"], n + 1 if q is None else q * 8 + n + 1)
                        return w_view(WH, n, n % SPLIT), w_view(WL, n, n % SPLIT)

                    def transpose_norm(i):
                        if i == 0:
                            pe.wait_ge(S["vc"], 1)
                        for t in range(TT):
                            pe.wait_ge(S["utok"], TT * i + t + 1)
                            for k in range(KD):
                                last = pe.transpose(PS[:, 2 * t + k // 4, P * (k % 4):P * (k % 4) + P],
                                                    UTOK[:, t, P * k:P * k + P], ident)
                                if k % 4 == 3:
                                    last.then_inc(S["ut_done"], 1)

                    pe.wait_ge(S["params"], 5 * 16)
                    pe.transpose(PS[:, 7, 0:N_VEC], VEC[:, :], ident[0:N_VEC, 0:N_VEC]).then_inc(S["vec_t"], 1)
                    transpose_norm(0)

                    held = {}

                    def in_tile(m, k0=0, k1=KD):
                        n = (m + 1) // 2
                        if n not in held:
                            held[n] = weights(n)
                        wh, wl = held[n]
                        c0, c1 = (0, 40) if m == 0 else (P * ((m + 1) % 2), P * ((m + 1) % 2) + P)
                        if m == 0:
                            pe.wait_ge(S["xl"], 2 * TT)
                        if k0:
                            pass
                        elif 6 <= m < 9:
                            pe.wait_ge(S["conv3"], m - 5)
                        elif m == 9:
                            pe.wait_ge(S["act_ev"], 1)
                        elif m == 10:
                            pe.wait_ge(S["conv3"], 6)
                        elif m > 10:
                            before_side(m)
                        for k in range(k0, k1):
                            last = three(PS[0:c1 - c0, in_bank(m), :], (wh[:, k, c0:c1], wl[:, k, c0:c1]),
                                         (XH[:, k, :], XL[:, k, :]), k == 0, k == KD - 1)
                        if k1 == KD:
                            last.then_inc(S["proj"], 1)

                    def before_side(item):
                        holder = SIDE[SIDE.index(item) - 2]
                        if holder == "q":
                            pe.wait_ge(S["rsb_x"], 2)
                        else:
                            pe.wait_ge(S["act_ev"], holder - 7)

                    def scan_begin(g):
                        if g:
                            pe.wait_ge(S["st_ready"], 3)
                        for c in range(TT):
                            last = pe.transpose(PS[:, 2, P * c:P * c + P], XB[:, 4 + g, P * c:P * c + P], ident)
                        last.then_inc(S["btok"], 1)
                        for c in range(TT):
                            last = pe.matmul(PS[:, 3, P * c:P * c + P], XB[:, 4 + g, P * c:P * c + P],
                                             XB[:, 6 + g, P * c:P * c + P], start=True, stop=True)
                        last.then_inc(S["cb"], 1)

                    def scan_decay(g):
                        if g:
                            pe.wait_ge(S["y_done"], 2)
                        else:
                            pe.wait_ge(S["conv3"], 5)
                        for hh in range(HG):
                            if g and hh == HG - 1:
                                pe.wait_ge(S["rsb_x"], 1)
                            for c in range(TT):
                                col = S_HEADS * c + HG * g + hh
                                for half in (1, 0):
                                    last = pe.matmul(PS[:, 4 + hh, P * c:P * c + P],
                                                     AHL[:, half, col:col + 1].to_broadcast([P, P]), TRIR[:, :],
                                                     start=half == 1, stop=half == 0)
                            last.then_inc(S["csb"], 1)

                    def scan_x(g):
                        pe.wait_ge(S["yexp"], 2 * g + 1)
                        for c in range(TT):
                            for jj in range(2):
                                last = pe.transpose(PS[:, 4 + c // 2, 256 * (c % 2) + P * jj:256 * (c % 2) + P * jj + P],
                                                    XB[:, 2 * g + jj, P * c:P * c + P], ident)
                            if c % 2:
                                last.then_inc(S["xs_t"], 1)

                    def scan_states(g):
                        pe.wait_ge(S["bt"], g + 1)
                        pe.wait_ge(S["cbm"], g + 1)
                        for c in range(TT - 1):
                            pe.wait_ge(S["xdd"], 3 * g + c + 1)
                            pe.matmul(PS[:, 2 + c // 2, 256 * (c % 2):256 * (c % 2) + 256], BT[:, c, :], XDD[:, c, :],
                                      start=True, stop=True).then_inc(S["st_mm"], 1)

                    def scan_y(g):
                        pe.wait_ge(S["xd"], 2 * g + 2)
                        pe.wait_ge(S["yexp"], 2 * g + 2)
                        for jj in range(2):
                            for hl in range(2):
                                hh = 2 * jj + hl
                                pe.wait_ge(S["m_ready"], HG * g + hh + 1)
                                for c in range(TT):
                                    last = pe.matmul(PS[64 * hl:64 * hl + 64, 6 + jj, P * c:P * c + P],
                                                     XD[:, c, 64 * hh:64 * hh + 64], E[:, hh, P * c:P * c + P],
                                                     start=True, stop=True)
                            last.then_inc(S["yd"], 1)
                        for jj in range(2):
                            for c in range(1, TT):
                                pe.wait_ge(S["st_ready"], 3 * g + c)
                                last = pe.matmul(PS[:, 4 + jj, P * c:P * c + P], ST[:, c - 1, P * jj:P * jj + P],
                                                 XB[:, 6 + g, P * c:P * c + P], start=True, stop=True)
                            last.then_inc(S["yo"], 1)

                    def scan_squares(g):
                        pe.wait_ge(S["y_done"], 2 * g + 2)
                        for jj in range(2):
                            pe.wait_ge(S["ysq"], 2 * g + jj + 1)
                            last = pe.matmul(PS[:, 7, :], ones, SCR[:, 1 + jj, :], start=(jj == 0), stop=(jj == 1))
                        last.then_inc(S["yssq"], 1)

                    for m in range(3):
                        in_tile(m)
                    pe.wait_ge(S["act_ev"], 1)
                    for t in range(TT):
                        last = pe.transpose(PS[:, 6, 8 * t:8 * t + 8], SM[32:40, P * t:P * t + P], ident[32:40, 32:40])
                    last.then_inc(S["dt_t"], 1)
                    for m in range(3, 6):
                        in_tile(m)
                    pe.wait_ge(S["a_ready"], 1)
                    pe.matmul(PS[:, 7, 0:32], tri, AA, start=True, stop=True).then_inc(S["cst"], 1)
                    in_tile(6)
                    in_tile(7)
                    pe.wait_ge(S["cst_ready"], 1)
                    pe.wait_ge(S["a_hi"], 2)
                    scan_decay(0)
                    in_tile(8)
                    in_tile(9)
                    pe.wait_ge(S["xb"], 8)
                    scan_begin(0)
                    scan_x(0)
                    in_tile(10)
                    scan_states(0)
                    in_tile(11)
                    scan_y(0)
                    scan_begin(1)
                    in_tile(12)
                    scan_squares(0)
                    scan_decay(1)
                    in_tile(13)
                    in_tile(14)
                    scan_x(1)
                    in_tile(15)
                    scan_states(1)
                    in_tile(16)
                    in_tile(17)
                    scan_y(1)
                    before_side("q")
                    pe.wait_ge(S["sq_add"], 5)
                    pe.matmul(PS[:, in_bank("q"), :], ones, SQA[:, :], start=True, stop=True).then_inc(S["cssq"], 1)
                    in_tile(18)
                    in_tile(19)
                    in_tile(20)
                    scan_squares(1)

                    pe.wait_ge(S["act_ev"], 13)
                    for i in range(3):
                        n = N_UQ + i
                        wh, wl = weights(n)
                        for k in range(2):
                            pe.wait_ge(S["cl"], 2 * i + k + 1)
                            s = c_slot(2 * i + k)
                            for mt in ((4, 5, 2, 3, 0, 1) if i == 2 and k == 1 else range(6)):
                                cols = slice(P * mt, P * mt + P)
                                last = three(PS[:, mt, :], (wh[:, k, cols], wl[:, k, cols]),
                                             (XH[:, s, :], XL[:, s, :]), i + k == 0, i == 2 and k == 1)
                                if i == 2 and k == 1:
                                    last.then_inc(S["q_done"], 1)
                        if i < 2:
                            last.then_inc(S["w_used"], 1)
                        if i == 0:
                            pe.wait_ge(S["sq_add"], 6)
                            pe.matmul(PS[:, 6, :], ones, SQA[:, :], start=True, stop=True).then_inc(S["cssq"], 1)
                            pe.wait_ge(S["rsb_x"], 3)
                            pe.matmul(PS[0:ROPE, 7, :], swap[0:ROPE, 0:ROPE], SM[0:ROPE, :], start=True, stop=True
                                      ).then_inc(S["kswap"], 1)
                    pe.wait_ge(S["cl"], 8)
                    wh, wl = weights(N_UKV)
                    for u in range(8):
                        if u < 2:
                            pe.wait_ge(S["q_rr"], u + 1)
                        elif u < 6:
                            pe.wait_ge(S["q_ev"], u - 1)
                        else:
                            pe.wait_ge(S["k_ev"], u - 5)
                        for k in range(2):
                            if u < 4:
                                cols = slice(P * u, P * u + P)
                                last = three(PS[:, KV_BANK[u], :], (wh[:, k, cols], wl[:, k, cols]),
                                             (XH[:, k, :], XL[:, k, :]), k == 0, k == 1)
                            else:
                                toks = slice(P * (u - 4), P * (u - 4) + P)
                                last = three(PS[:, KV_BANK[u], :], (XH[:, k, toks], XL[:, k, toks]),
                                             (wh[:, k, 512:1024], wl[:, k, 512:1024]), k == 0, k == 1)
                        last.then_inc(S["kv_done"], 1)
                        if u == 1:
                            pe.wait_ge(S["kro"], 1)
                            for t in range(2):
                                pe.matmul(PS[:, 6 + t, :], swap, SCR[:, t, :], start=True, stop=True
                                          ).then_inc(S["qswap"], 1)

                    pe.wait_ge(S["q_ev"], 4)
                    pe.wait_ge(S["q_rc"], 4)
                    pe.wait_ge(S["q_rd"], 4)
                    pe.wait_ge(S["k_ev"], 4)
                    pe.wait_ge(S["v_ev"], 4)
                    pe.wait_ge(S["ylo"], 4)

                    def scores(h):
                        for u, unit in enumerate(S_UNITS):
                            if h:
                                pe.wait_ge(S["p_done"], 3 * (h - 1) + u + 1)
                            for i in unit:
                                bank, col = S_BANK[i]
                                n = P * (i + 1)
                                pe.matmul(PS[:, bank, col:col + n], Q[:, h, P * i:P * i + P], K[:, h, 0:n],
                                          start=True, stop=False)
                                last = pe.matmul(PS[:, bank, col + n - CHUNK:col + n], SELB[:, :], MASKB[:, :],
                                                 start=False, stop=True)
                            last.then_inc(S["s_done"], 1)

                    def probs_transposed(h):
                        pe.wait_ge(S["pn"], h + 1)
                        for u, unit in enumerate(T_UNITS):
                            if h:
                                pe.wait_ge(S["pt_d"] if u == 1 else S["pt_a"], h if u == 1 else 2 * h - 1 + u // 2)
                            for j in unit:
                                bank, col = T_BANK[j]
                                for i in range(j, TT):
                                    at_p = P_AT[i] + P * j
                                    last = pe.transpose(PS[:, bank, col + P * (i - j):col + P * (i - j) + P],
                                                        PR[:, h % 2, at_p:at_p + P], ident)
                            last.then_inc(S["pt_done"], 1)

                    def values(h):
                        pe.wait_ge(S["pt_a"], 2 * h + 2)
                        pe.wait_ge(S["pt_d"], h + 1)
                        if h >= 4:
                            pe.wait_ge(S["o_lo"], h // 2 - 1)
                        rows = slice(64 * (h % 2), 64 * (h % 2) + 64)
                        for j in range(TT):
                            last = pe.matmul(PS[rows, 6 + (h // 2) % 2, P * j:SEQ], V[:, j, VDIM * h:VDIM * h + VDIM],
                                             PT[h % 2][:, T_AT[j]:T_AT[j] + SEQ - P * j],
                                             start=(j == 0), stop=(j == TT - 1))
                        last.then_inc(S["pv"], 1)

                    scores(0)
                    for h in range(HEADS):
                        if h + 1 < HEADS:
                            scores(h + 1)
                        if h:
                            values(h - 1)
                        probs_transposed(h)
                    values(HEADS - 1)

                    for i, pair in enumerate(OUT_ROWS):
                        n = N_OUT + i
                        wh, wl = weights(n)
                        order = ([(k, t) for k in range(2) for t in range(TT)] if i < 3 else
                                 [(k, t) for t in range(TT) for k in range(2)])
                        for k, t in order:
                            kt, toks = pair[k], slice(P * t, P * t + P)
                            if i + k == 0 and t == 3:
                                pe.wait_ge(S["o_lo"], 4)
                            for half in range(2):
                                cols = slice(512 * half, 512 * half + 512)
                                last = three(PS[:, 2 * t + half, :], (XH[:, kt, toks], XL[:, kt, toks]),
                                             (wh[:, k, cols], wl[:, k, cols]), i + k == 0, i == 3 and k == 1)
                            if i == 3 and k == 1:
                                last.then_inc(S["o_done"], 1)
                        if i < 3:
                            last.then_inc(S["w_used"], 1)

                    transpose_norm(1)
                    pe.wait_ge(S["xl"], 4 * TT)

                    def quarter(q):
                        for i in range(8):
                            wh, wl = weights(N_MLP + i, q)
                            if i < 4:
                                for f in (2 * i, 2 * i + 1):
                                    cols = slice(P * (f % 2), P * (f % 2) + P)
                                    pe.wait_ge(S["a_done"], q * 8 + f + 1)
                                    for k in range(KD):
                                        last = three(PS[:, 4 + f % 4, :], (wh[:, k, cols], wl[:, k, cols]),
                                                     (XH[:, k, :], XL[:, k, :]), k == 0, k == KD - 1)
                                    last.then_inc(S["up_done"], 1)
                            else:
                                half, kk = (i - 4) // 2, (i - 4) % 2
                                for k in range(4):
                                    if half == 0:
                                        pe.wait_ge(S["act_lo"], q * 8 + 4 * kk + k + 3)
                                    for t in range(TT):
                                        if kk + k == 0:
                                            pe.wait_ge(S["down_free"], q * 8 + TT * half + t + 5)
                                        f, toks = 4 * kk + k, slice(P * t, P * t + P)
                                        last = three(PS[:, t, :], (AH[:, f, toks], AL[:, f, toks]),
                                                     (wh[:, k, :], wl[:, k, :]), kk + k == 0, kk == 1 and k == 3)
                                        if kk == 1 and k == 3:
                                            last.then_inc(S["down_done"], 1)
                                if kk == 0:
                                    last.then_inc(S["down_k0"], 1)

                    with pe.Fori(0, QUARTERS) as q:
                        quarter(q)

                def chunk_used(eng, n, q=None):
                    if n < N_UQ:
                        eng.wait_ge(S["proj"], 2 * n + 1)
                    elif n < N_UQ + 2:
                        eng.wait_ge(S["w_used"], n - N_UQ + 1)
                    elif n < N_UKV:
                        eng.wait_ge(S["q_done"], 6)
                    elif n == N_UKV:
                        eng.wait_ge(S["kv_done"], 8)
                    elif n < N_OUT + 3:
                        eng.wait_ge(S["w_used"], n - N_OUT + 3)
                    elif q is None:
                        eng.wait_ge(S["o_done"], TT)
                    elif n < N_MLP:
                        eng.wait_ge(S["down_done"], q * 8 + 1)
                    elif n < N_MLP + 4:
                        eng.wait_ge(S["up_done"], q * 8 + 2 * (n - N_MLP) + 2)
                    elif (n - N_MLP) % 2 == 0:
                        eng.wait_ge(S["down_k0"], q * 2 + (n - N_MLP - 4) // 2 + 1)
                    else:
                        eng.wait_ge(S["down_done"], q * 8 + 4 * ((n - N_MLP - 4) // 2) + 5)

                def cuts(n):
                    parts = split_parts(n, n % SPLIT)
                    for i, x in enumerate(parts):
                        yield x, i == len(parts) - 1

                @block.scalar
                def _(a):
                    n_steps = [0]

                    def step(ins):
                        n_steps[0] += 1
                        ins.then_inc(S["act_step"], 1)
                        a.wait_ge(S["act_step"], n_steps[0])

                    def hi(n, q=None):
                        chunk_ready(a, n, q)
                        if n >= SPLIT:
                            chunk_used(a, n - SPLIT, q)
                        for (raw, h, _), last in cuts(n):
                            ins = a.activation(h, raw, ACT.Copy)
                            if last:
                                ins.then_inc(S["hi_done"], 1)

                    def squares(t, x, slot=0):
                        u = UTOK[:, t, 512 * slot:512 * slot + x.shape[-1] * (x.shape[1] if len(x.shape) == 3 else 1)]
                        if len(x.shape) == 3:
                            u = u.rearrange("p (a b) -> p a b", a=2)
                        a.activation(u, x, ACT.Square, accum_out=N4[:, slot, t:t + 1]).then_inc(S["ssq"], 1)

                    def power(i, t):
                        a.wait_ge(S["nrm_x"], nth(i, t))
                        step(a.activation(N4[:, 3, t:t + 1], N4[:, 2, t:t + 1], ACT.Ln))
                        a.activation(N4[:, 4, t:t + 1], N4[:, 3, t:t + 1], ACT.Exp, scale=-0.5
                                     ).then_inc(S["nrm_y"], 1)

                    def x_high(i, t):
                        for half in range(2):
                            a.wait_ge(S["ut_done"], 2 * TT * i + 2 * t + half + 1)
                            a.activation(XH[:, 4 * half:4 * half + 4, P * t:P * t + P],
                                         PS[:, 2 * t + half, :].rearrange("p (k n) -> p k n", k=4), ACT.Copy
                                         ).then_inc(S["xh"], 1)

                    def rsqrt_wide(i):
                        a.wait_ge(S["rsb_x"], i + 1)
                        step(a.activation(SCR[:, 0, :], SCR[:, 2, :], ACT.Ln))
                        a.activation(SCR[:, 0, :], SCR[:, 0, :], ACT.Exp, scale=-0.5).then_inc(S["rsb_y"], 1)

                    a.preload_act_table_set("natural_log_exp_and_others")
                    for t in range(TT):
                        squares(t, H[:, t, :])
                        if t:
                            power(0, t - 1)
                    power(0, TT - 1)
                    hi(0)
                    a.wait_ge(S["vec_t"], 1)
                    a.activation(VC[:, :], PS[:, 7, 0:N_VEC], ACT.Copy).then_inc(S["vc"], 1)
                    for t in range(TT):
                        x_high(0, t)
                    a.wait_ge(S["vc"], 1)

                    def silu_x(c):
                        a.wait_ge(S["conv3"], c + 1)
                        a.activation(XB[:, c, :], XB[:, c, :], ACT.Silu).then_inc(S["xb"], 1)

                    def out_of_bank(m):
                        a.wait_ge(S["proj"], m + 1)
                        src = PS[:, in_bank(m), :]
                        if m == 0:
                            a.activation(SM[:, :], src[0:40, :], ACT.Copy).then_inc(S["act_ev"], 1)
                        elif m < 9:
                            c = m - 1
                            a.activation(XB[:, c, :], src, ACT.Identity, bias=VC[:, V_CB + c:V_CB + c + 1],
                                         scale=VC[:, V_CW + 24 + c:V_CW + 25 + c]).then_inc(S["conv0"], 1)
                        elif m in Z_TILES:
                            a.activation(ZS[:, Z_TILES.index(m), :], src, ACT.Copy).then_inc(S["act_ev"], 1)
                        else:
                            i = C_TILES.index(m)
                            a.activation(CQ[:, i, :], src, ACT.Copy)
                            if i == 6:
                                a.wait_ge(S["cssq"], 1)
                            elif i >= 2:
                                a.wait_ge(S["sq_add"], min(i - 1, 5))
                            a.activation((SQA if i in (0, 6) else SQ)[:, :], src, ACT.Square).then_inc(S["act_ev"], 1)

                    for m in range(9):
                        if m == 0 or m % 2:
                            hi((m + 1) // 2 + 1)
                        out_of_bank(m)
                        if m >= 2:
                            silu_x(m - 2)
                        if m == 4:
                            a.preload_act_table_set("natural_log_exp_and_others")
                            a.wait_ge(S["broad"], N_BROAD)
                            a.activation(ALOG[:, :], ALOG[:, :], ACT.Exp)
                            a.wait_ge(S["dt_n"], 1)
                            a.activation(DTT[:, 5, :], DTT[:, 4, :], ACT.Exp).then_inc(S["dt_e"], 1)
                            a.wait_ge(S["dt_n"], 2)
                            a.activation(DTT[:, 7, :], DTT[:, 6, :], ACT.Ln).then_inc(S["dt_l"], 1)
                    silu_x(7)
                    a.preload_act_table_set("natural_log_exp_and_others")

                    def chunk_then(m):
                        if m % 2:
                            hi((m + 1) // 2 + 1)
                        out_of_bank(m)

                    def b_tokens(g):
                        a.wait_ge(S["btok"], g + 1)
                        a.activation(BT[:, :, :], PS[:, 2, :].rearrange("p (c n) -> p c n", c=TT), ACT.Copy
                                     ).then_inc(S["bt"], 1)

                    def decays(g):
                        if g:
                            a.wait_ge(S["y_n"], 2)
                        for jj in range(2):
                            a.wait_ge(S["dd"], HG * g + 2 * jj + 2)
                            for hl in range(2):
                                rows = slice(64 * hl, 64 * hl + 64)
                                ins = a.activation(Y[rows, jj, P:SEQ], PS[rows, 4 + 2 * jj + hl, P:SEQ], ACT.Exp)
                            ins.then_inc(S["yexp"], 1)
                            for hh in (2 * jj, 2 * jj + 1):
                                a.activation(E[:, hh, :], E[:, hh, :], ACT.Exp).then_inc(S["e_ready"], 1)
                        a.activation(CLX[:, g], CLX[:, g], ACT.Exp).then_inc(S["cdx"], 1)

                    def z_silu(g):
                        a.wait_ge(S["act_ev"], 11 if g else 3)
                        a.activation(ZS[:, 2 * g:2 * g + 2, :], ZS[:, 2 * g:2 * g + 2, :], ACT.Silu
                                     ).then_inc(S["zs"], 1)
                        a.preload_act_table_set("natural_log_exp_and_others")

                    def y_squares(g):
                        for jj in range(2):
                            a.wait_ge(S["y_done"], 2 * g + jj + 1)
                            a.activation(SCR[:, 1 + jj, :], Y[:, jj, :], ACT.Square).then_inc(S["ysq"], 1)

                    decays(0)
                    b_tokens(0)
                    chunk_then(9)
                    chunk_then(10)
                    chunk_then(11)
                    z_silu(0)
                    b_tokens(1)
                    y_squares(0)
                    chunk_then(12)
                    rsqrt_wide(0)
                    chunk_then(13)
                    decays(1)
                    chunk_then(14)
                    chunk_then(15)
                    chunk_then(16)
                    chunk_then(17)
                    rsqrt_wide(1)
                    chunk_then(18)
                    z_silu(1)
                    chunk_then(19)
                    y_squares(1)
                    chunk_then(20)

                    def c_high(i):
                        a.wait_ge(S["proj"], 21)
                        a.wait_ge(S["cqn"], i + 1)
                        a.activation(XH[:, c_slot(i), :], CQ[:, i, :], ACT.Copy).then_inc(S["ch"], 1)

                    for i in range(6):
                        c_high(i)
                    rsqrt_wide(2)
                    hi(N_UQ + 1)
                    rsqrt_wide(3)
                    hi(N_UQ + 2)
                    c_high(6)
                    c_high(7)
                    hi(N_UKV)
                    a.wait_ge(S["kro"], 1)
                    for t in range(2):
                        a.wait_ge(S["q_done"], t + 1)
                        a.activation(SCR[:, t, :], PS[:, 4 + t, :], ACT.Copy).then_inc(S["q_rr"], 1)

                    def q_nope(j):
                        a.activation(Q[0:NOPE, 2 * j, :], PS[0:64, j, :], ACT.Copy)
                        a.activation(Q[0:NOPE, 2 * j + 1, :], PS[64:128, j, :], ACT.Copy).then_inc(S["q_ev"], 1)

                    for j in (2, 3):
                        a.wait_ge(S["q_done"], j + 1)
                        q_nope(j)
                    a.wait_ge(S["q_done"], 6)
                    for k in range(4):
                        a.wait_ge(S["y_n"], k + 1)
                        a.activation(XH[:, 4 + k, :], XB[:, k, :], ACT.Copy).then_inc(S["yhi"], 1)
                    hi(N_OUT)
                    a.wait_ge(S["ylo"], 4)
                    for j in (0, 1):
                        q_nope(j)
                    a.wait_ge(S["q_ro"], 1)
                    for i in range(4):
                        a.activation(Q[NOPE:QK, i, :], SCR[ROPE * i:ROPE * i + ROPE, 0, :], ACT.Copy
                                     ).then_inc(S["q_rc"], 1)
                    for t in range(TT):
                        a.wait_ge(S["kv_done"], 5 + t)
                        a.activation(V[:, t, :], PS[:, KV_BANK[4 + t], :], ACT.Copy).then_inc(S["v_ev"], 1)
                    hi(N_OUT + 1)

                    def p_transposed(h):
                        if h >= 2:
                            a.wait_ge(S["pv"], h - 1)
                        for u, j, n in ((0, 2, 256), (2, 0, 512)):
                            a.wait_ge(S["pt_done"], 3 * h + u + 1)
                            a.activation(PT[h % 2][:, T_AT[j]:T_AT[j] + n], PS[:, T_BANK[j][0], 0:n], ACT.Copy
                                         ).then_inc(S["pt_a"], 1)

                    def o_high(p):
                        a.wait_ge(S["pv"], 2 * p + 2)
                        a.activation(XH[:, p, :], PS[:, 6 + p % 2, :], ACT.Copy).then_inc(S["o_hi"], 1)

                    for h in range(HEADS):
                        if h >= 2:
                            a.wait_ge(S["pt_done"], 3 * (h - 1))
                        for u, unit in enumerate(S_UNITS):
                            a.wait_ge(S["nm"], 3 * h + u + 1)
                            for i in unit:
                                (bank, col), n, m = S_BANK[i], P * (i + 1), M_SLOT[i]
                                ins = a.activation(PR[:, h % 2, P_AT[i]:P_AT[i] + n], PS[:, bank, col:col + n], ACT.Exp,
                                                   bias=NM[:, h, m:m + 1], scale=SCALE, accum_out=RSUM[:, h, m:m + 1])
                            ins.then_inc(S["p_done"], 1)
                        if h >= 3 and h % 2:
                            o_high((h - 2) // 2)
                        if h:
                            p_transposed(h - 1)
                    p_transposed(HEADS - 1)
                    o_high(HEADS // 2 - 1)
                    hi(N_OUT + 2)

                    hi(N_OUT + 3)
                    hi(N_OUT + 4)
                    for i, t in NORMS[TT:3 * TT]:
                        if i == 1:
                            a.wait_ge(S["o_done"], t + 1)
                            squares(t, PS[:, 2 * t:2 * t + 2, :])
                        else:
                            a.wait_ge(S["h_done"], t + 1)
                            squares(t, H[:, t, :])
                        power(i, t)
                        if i == 2 and t >= 1:
                            x_high(1, t - 1)
                    x_high(1, TT - 1)

                    def quarter(q, last):
                        for i in range(8):
                            if not (last and i == 7):
                                hi_next(i, q)
                            if i < 4:
                                for f in (2 * i, 2 * i + 1):
                                    a.wait_ge(S["up_done"], q * 8 + f + 1)
                                    a.wait_ge(S["a_done"], q * 8 + f + 3)
                                    a.activation(RELU[:, f % 2, :], PS[:, 4 + f % 4, :], ACT.Relu
                                                 ).then_inc(S["relu"], 1)
                                for f in (2 * i, 2 * i + 1):
                                    a.wait_ge(S["a_done"], q * 8 + f + 5)
                                    a.activation(AH[:, f, :], SQR[:, f % 2, :], ACT.Copy).then_inc(S["act_hi"], 1)

                    def hi_next(i, q):
                        n = N_MLP + i + 1
                        chunk_ready(a, n, q)
                        chunk_used(a, n - SPLIT, q)
                        a.activation(w_view(WH, n, n % SPLIT), w_view(RAW, n, n % RING), ACT.Copy).then_inc(S["hi_done"], 1)

                    with a.Fori(0, QUARTERS - 1) as q:
                        quarter(q, False)
                    quarter(QUARTERS - 1, True)
                    for half in range(2):
                        for t in range(TT):
                            a.wait_ge(S["down_free"], 8 * QUARTERS + 4 * half + t + 1)
                            squares(t, MACC[:, t, 512 * half:512 * half + 512], half)
                            if half and t:
                                power(3, t - 1)
                    power(3, TT - 1)

                @block.vector
                def _(v):
                    n_steps = [0]

                    def step(ins):
                        n_steps[0] += 1
                        ins.then_inc(S["dve_step"], 1)
                        v.wait_ge(S["dve_step"], n_steps[0])

                    def lo(n, q=None):
                        v.wait_ge(S["hi_done"], n + 1 if q is None else q * 8 + n + 1)
                        for (raw, h, l), last in cuts(n):
                            ins = v.tensor_tensor(l, raw, f32(h), ALU.subtract)
                            if last:
                                ins.then_inc(S["lo_done"], 1)

                    def mean(i, t):
                        if i < 3:
                            v.wait_ge(S["ssq"], nth(i, t))
                            total = N4[:, 0, t:t + 1]
                        else:
                            v.wait_ge(S["ssq"], nth(3, t) + TT)
                            total = N4[:, 5, t:t + 1]
                            step(v.tensor_tensor(total, N4[:, 0, t:t + 1], N4[:, 1, t:t + 1], ALU.add))
                        v.tensor_scalar(N4[:, 2, t:t + 1], total, 1 / D_MODEL, EPS, ALU.mult, ALU.add
                                        ).then_inc(S["nrm_x"], 1)

                    def scale(i, t):
                        x, y, tmp = N4[:, 2, t:t + 1], N4[:, 4, t:t + 1], N4[:, 5, t:t + 1]
                        v.wait_ge(S["nrm_y"], nth(i, t))
                        step(v.tensor_tensor(tmp, y, y, ALU.mult))
                        step(v.scalar_tensor_tensor(tmp, tmp, -0.5, x, ALU.mult, ALU.mult))
                        step(v.scalar_tensor_tensor(N4[:, 6, t:t + 1], tmp, 1.5, y, ALU.add, ALU.mult))

                    def pre_norm(i, t):
                        v.wait_ge(S["pre_w"], 32 if i else 16)
                        v.scalar_tensor_tensor(UTOK[:, t, :], H[:, t, :], N4[:, 6, t:t + 1], PREB[:, :],
                                               ALU.mult, ALU.mult).then_inc(S["utok"], 1)

                    def x_low(i, t):
                        for half in range(2):
                            v.wait_ge(S["xh"], 2 * TT * i + 2 * t + half + 1)
                            tile = (slice(None), slice(4 * half, 4 * half + 4), slice(P * t, P * t + P))
                            v.tensor_tensor(XL[tile], PS[:, 2 * t + half, :].rearrange("p (k n) -> p k n", k=4),
                                            f32(XH[tile]), ALU.subtract).then_inc(S["xl"], 1)

                    def post_norm(t, x):
                        two = (lambda z: z) if len(x.shape) == 2 else (
                            lambda z: z.rearrange("p (a b) -> p a b", a=2))
                        step(v.scalar_tensor_tensor(two(UTOK[:, t, :]), x, N4[:, 6, t:t + 1], two(POST[:, :]),
                                                    ALU.mult, ALU.mult))
                        v.tensor_tensor(H[:, t, :], H[:, t, :], UTOK[:, t, :], ALU.add).then_inc(S["h_done"], 1)

                    def rsqrt_wide(i, src, count):
                        x, y, r = SCR[:, 2, :], SCR[:, 0, :], SCR[:, 1, :]
                        v.tensor_scalar(x, src, 1 / count, EPS, ALU.mult, ALU.add).then_inc(S["rsb_x"], 1)
                        v.wait_ge(S["rsb_y"], i + 1)
                        step(v.tensor_tensor(r, y, y, ALU.mult))
                        step(v.scalar_tensor_tensor(r, r, -0.5, x, ALU.mult, ALU.mult))
                        step(v.scalar_tensor_tensor(r, r, 1.5, y, ALU.add, ALU.mult))

                    for t in range(TT):
                        mean(0, t)
                        scale(0, t)
                        pre_norm(0, t)
                    lo(0)
                    for t in range(TT):
                        x_low(0, t)

                    th = lambda w: w.rearrange("p (t h) -> p t h", t=TT)
                    every_t = lambda w: w.unsqueeze(1).to_broadcast([P, TT, S_HEADS])

                    def decay_logs(g):
                        for hh in range(HG):
                            v.wait_ge(S["csb"], HG * g + hh + 1)
                            bank = PS[:, 4 + hh, :]
                            for c in range(TT):
                                col = S_HEADS * c + HG * g + hh
                                v.tensor_scalar(E[:, hh, P * c:P * c + P], bank[:, P * c:P * c + P],
                                                CST[:, col:col + 1], 0.0, ALU.subtract, ALU.min)
                            v.tensor_copy(CLX[:, g, hh, :], bank[:, P - 1:SEQ:P]).then_inc(S["dd"], 1)

                    lo(1)
                    v.wait_ge(S["vc"], 1)
                    for n in range(1, 5):
                        lo(n + 1)
                        for c in (2 * n - 2, 2 * n - 1):
                            if c == 7:
                                decay_logs(0)
                            v.wait_ge(S["conv0"], c + 1)
                            for s in range(1, TAPS):
                                w = V_CW + 8 * (TAPS - 1 - s) + c
                                ins = v.scalar_tensor_tensor(XB[:, c, s:SEQ], PS[:, in_bank(c + 1), 0:SEQ - s],
                                                             VC[:, w:w + 1], XB[:, c, s:SEQ], ALU.mult, ALU.add)
                                if s < TAPS - 1:
                                    step(ins)
                            ins.then_inc(S["conv3"], 1)
                        if n == 1:
                            v.wait_ge(S["dt_t"], 1)
                            v.wait_ge(S["broad"], N_BROAD)
                            for hl in range(2):
                                part = slice(64 * hl, 64 * hl + 64)
                                v.tensor_copy(DSK[part, :], DSKB[part, hl::2])
                            step(v.tensor_tensor(th(DT), th(PS[:, 6, 0:32]), every_t(DTB[:, :]), ALU.add))
                            step(v.tensor_scalar(DTT[:, 3, :], DT, -1.0, None, ALU.mult))
                            v.tensor_tensor(DTT[:, 4, :], DT, DTT[:, 3, :], ALU.min).then_inc(S["dt_n"], 1)
                        elif n == 2:
                            v.wait_ge(S["dt_e"], 1)
                            v.tensor_scalar(DTT[:, 6, :], DTT[:, 5, :], 1.0, None, ALU.add).then_inc(S["dt_n"], 1)
                            v.wait_ge(S["dt_n"], 2)
                            step(v.tensor_scalar(DTT[:, 3, :], DTT[:, 6, :], 1.0, 1e-30, ALU.subtract, ALU.max))
                            step(v.reciprocal(DTT[:, 3, :], DTT[:, 3, :]))
                            v.wait_ge(S["dt_l"], 1)
                            step(v.tensor_tensor(DTT[:, 3, :], DTT[:, 3, :], DTT[:, 5, :], ALU.mult))
                            step(v.tensor_tensor(DTT[:, 3, :], DTT[:, 3, :], DTT[:, 7, :], ALU.mult))
                            step(v.scalar_tensor_tensor(DT, DT, 0.0, DTT[:, 3, :], ALU.max, ALU.add))
                            v.scalar_tensor_tensor(th(AA), th(DT), -1.0, every_t(ALOG[:, :]), ALU.mult, ALU.mult
                                                   ).then_inc(S["a_ready"], 1)
                            v.wait_ge(S["a_ready"], 1)
                            v.tensor_copy(AHL[:, 0, :], AA).then_inc(S["a_hi"], 1)
                            v.wait_ge(S["a_hi"], 1)
                            v.tensor_tensor(AHL[:, 1, :], AA, f32(AHL[:, 0, :]), ALU.subtract).then_inc(S["a_hi"], 1)
                        elif n == 3:
                            v.wait_ge(S["cst"], 1)
                            v.tensor_copy(CST, PS[:, 7, 0:32]).then_inc(S["cst_ready"], 1)
                            v.wait_ge(S["cst_ready"], 1)


                    def masked_cb(g):
                        v.wait_ge(S["cb"], g + 1)
                        blocks = lambda w: w.rearrange("p (c l) -> p c l", c=TT)
                        v.tensor_tensor(blocks(CBM[:, :]), blocks(PS[:, 3, :]),
                                        tri.unsqueeze(1).to_broadcast([P, TT, P]), ALU.mult).then_inc(S["cbm"], 1)

                    def x_dt(g):
                        for i in range(2):
                            v.wait_ge(S["xs_t"], 2 * g + i + 1)
                            chp = lambda w: w.rearrange("p (c h d) -> p c h d", c=2, h=HG)
                            dt4 = th(DT)[:, 2 * i:2 * i + 2, HG * g:HG * g + HG].unsqueeze(3).to_broadcast([P, 2, HG, 64])
                            v.tensor_tensor(XD[:, 2 * i:2 * i + 2, :].rearrange("p c (h d) -> p c h d", h=HG),
                                            chp(PS[:, 4 + i, :]), dt4, ALU.mult).then_inc(S["xd"], 1)

                    def block_scores(g):
                        v.wait_ge(S["xdd"], 3 * g + 3)
                        v.wait_ge(S["cbm"], g + 1)
                        for hh in range(HG):
                            v.wait_ge(S["e_ready"], HG * g + hh + 1)
                            v.tensor_tensor(E[:, hh, :], E[:, hh, :], CBM[:, :], ALU.mult).then_inc(S["m_ready"], 1)

                    def states(g):
                        v.wait_ge(S["st_mm"], 3 * g + 2)
                        v.tensor_copy(ST[:, 0, :], PS[:, 2, 0:256]).then_inc(S["st_ready"], 1)
                        v.wait_ge(S["cdx"], g + 1)
                        for c in (1, 2):
                            v.wait_ge(S["st_ready"], 3 * g + c)
                            hd = lambda w: w.rearrange("p (h d) -> p h d", h=HG)
                            step(v.tensor_tensor(hd(SCR[:, 2, 0:256]), hd(ST[:, c - 1, :]),
                                                 CLX[:, g, :, c:c + 1].to_broadcast([P, HG, 64]), ALU.mult))
                            v.wait_ge(S["st_mm"], 3 * g + c + 1)
                            v.tensor_tensor(ST[:, c, :], SCR[:, 2, 0:256],
                                            PS[:, 2 + c // 2, 256 * (c % 2):256 * (c % 2) + 256],
                                            ALU.add).then_inc(S["st_ready"], 1)

                    def outputs(g):
                        v.wait_ge(S["zs"], g + 1)
                        for jj in range(2):
                            j = 2 * g + jj
                            y = Y[:, jj, :]
                            v.wait_ge(S["yexp"], j + 1)
                            v.wait_ge(S["yd"], j + 1)
                            v.wait_ge(S["yo"], j + 1)
                            step(v.tensor_tensor(SCR[:, 0, P:SEQ], PS[:, 4 + jj, P:SEQ], y[:, P:SEQ], ALU.mult))
                            step(v.scalar_tensor_tensor(y, XB[:, j, :], DSK[:, j:j + 1], PS[:, 6 + jj, :],
                                                        ALU.mult, ALU.add))
                            step(v.tensor_tensor(y[:, P:SEQ], y[:, P:SEQ], SCR[:, 0, P:SEQ], ALU.add))
                            v.tensor_tensor(y, y, ZS[:, j, :], ALU.mult).then_inc(S["y_done"], 1)

                    def outputs_normalised(g, i):
                        v.wait_ge(S["yssq"], g + 1)
                        rsqrt_wide(i, PS[:, 7, :], INNER // GROUPS)
                        for jj in range(2):
                            w = V_SSD + 2 * g + jj
                            v.scalar_tensor_tensor(XB[:, 2 * g + jj, :], Y[:, jj, :], VC[:, w:w + 1], SCR[:, 1, :],
                                                   ALU.mult, ALU.mult).then_inc(S["y_n"], 1)

                    def c_normalised(which, i):
                        tiles, count = (range(6), Q_RANK) if which == "q" else (range(6, 8), KV_RANK)
                        v.wait_ge(S["cssq"], 1 if which == "q" else 2)
                        rsqrt_wide(i, PS[:, in_bank("q") if which == "q" else 6, :], count)
                        for c in tiles:
                            v.scalar_tensor_tensor(CQ[:, c, :], CQ[:, c, :], VC[:, V_Q + c:V_Q + c + 1], SCR[:, 1, :],
                                                   ALU.mult, ALU.mult).then_inc(S["cqn"], 1)

                    def c_low(i):
                        v.wait_ge(S["ch"], i + 1)
                        v.tensor_tensor(XL[:, c_slot(i), :], CQ[:, i, :], f32(XH[:, c_slot(i), :]), ALU.subtract
                                        ).then_inc(S["cl"], 1)

                    masked_cb(0)
                    x_dt(0)
                    lo(6)
                    block_scores(0)
                    states(0)
                    lo(7)
                    outputs(0)
                    masked_cb(1)
                    outputs_normalised(0, 0)
                    lo(8)
                    decay_logs(1)
                    x_dt(1)
                    lo(9)
                    block_scores(1)
                    states(1)
                    lo(10)
                    c_normalised("q", 1)
                    outputs(1)
                    lo(11)
                    for i in range(6):
                        c_low(i)
                    outputs_normalised(1, 2)
                    lo(N_UQ + 1)

                    v.wait_ge(S["kswap"], 1)
                    v.wait_ge(S["y_n"], 4)
                    r = slice(0, ROPE)
                    v.tensor_tensor(SCR[r, 2, :], SM[r, :], COS[r, :], ALU.mult)
                    step(v.tensor_tensor(SCR[r, 1, :], PS[r, 7, :], SIN[r, :], ALU.mult))
                    step(v.tensor_tensor(SCR[r, 2, :], SCR[r, 2, :], SCR[r, 1, :], ALU.add))
                    v.tensor_copy(K[NOPE:QK, :, :], SCR[r, 2, :].unsqueeze(1).to_broadcast([ROPE, HEADS, SEQ])
                                  ).then_inc(S["kro"], 1)

                    v.wait_ge(S["kro"], 1)
                    c_normalised("kv", 3)
                    lo(N_UQ + 2)
                    c_low(6)
                    c_low(7)
                    lo(N_UKV)
                    for k in range(4):
                        v.wait_ge(S["yhi"], k + 1)
                        v.tensor_tensor(XL[:, 4 + k, :], XB[:, k, :], f32(XH[:, 4 + k, :]), ALU.subtract
                                        ).then_inc(S["ylo"], 1)
                    for u in range(4):
                        v.wait_ge(S["kv_done"], u + 1)
                        v.tensor_copy(K[0:NOPE, 2 * u, :], PS[0:64, KV_BANK[u], :])
                        v.tensor_copy(K[0:NOPE, 2 * u + 1, :], PS[64:128, KV_BANK[u], :]
                                      ).then_inc(S["k_ev"], 1)
                        if u in (1, 2):
                            t = u - 1
                            v.wait_ge(S["qswap"], t + 1)
                            step(v.tensor_tensor(SCR[:, 2, :], SCR[:, t, :], COS[:, :], ALU.mult))
                            step(v.tensor_tensor(SCR[:, t, :], PS[:, 6 + t, :], SIN[:, :], ALU.mult))
                            v.tensor_tensor(SCR[:, t, :], SCR[:, t, :], SCR[:, 2, :], ALU.add
                                            ).then_inc(S["q_ro"], 1)
                            v.wait_ge(S["q_ro"], t + 1)
                    for i in range(4):
                        v.tensor_copy(Q[NOPE:QK, 4 + i, :], SCR[ROPE * i:ROPE * i + ROPE, 1, :]
                                      ).then_inc(S["q_rd"], 1)
                    lo(N_OUT)
                    lo(N_OUT + 1)

                    def p_transposed(h):
                        if h >= 2:
                            v.wait_ge(S["pv"], h - 1)
                        v.wait_ge(S["pt_done"], 3 * h + 2)
                        v.tensor_copy(PT[h % 2][:, T_AT[1]:T_AT[1] + 512], PS[:, T_BANK[1][0], :]).then_inc(S["pt_d"], 1)

                    def o_low(p):
                        v.wait_ge(S["o_hi"], p + 1)
                        v.tensor_tensor(XL[:, p, :], PS[:, 6 + p % 2, :], f32(XH[:, p, :]), ALU.subtract
                                        ).then_inc(S["o_lo"], 1)

                    for h in range(HEADS):
                        for u, unit in enumerate(S_UNITS):
                            v.wait_ge(S["s_done"], 3 * h + u + 1)
                            for i in unit:
                                (bank, col), n, m = S_BANK[i], P * (i + 1), M_SLOT[i]
                                ins = v.tensor_reduce(MX[:, h, m:m + 1], PS[:, bank, col:col + n], AX, ALU.max)
                            ins.then_inc(S["mx"], 1)
                            v.wait_ge(S["mx"], 3 * h + u + 1)
                            m0, m1 = M_SLOT[unit[0]], M_SLOT[unit[-1]] + 1
                            v.tensor_scalar(NM[:, h, m0:m1], MX[:, h, m0:m1], -SCALE, None, ALU.mult
                                            ).then_inc(S["nm"], 1)
                        if h >= 3 and h % 2:
                            o_low((h - 2) // 2)
                        if h:
                            p_transposed(h - 1)
                        v.wait_ge(S["p_done"], 3 * h + 3)
                        step(v.reciprocal(RINV[:, h, :], RSUM[:, h, :]))
                        for i in range(TT):
                            pr, m = PR[:, h % 2, P_AT[i]:P_AT[i] + P * (i + 1)], M_SLOT[i]
                            ins = v.tensor_scalar(pr, pr, RINV[:, h, m:m + 1], None, ALU.mult)
                        ins.then_inc(S["pn"], 1)
                    p_transposed(HEADS - 1)
                    o_low(HEADS // 2 - 1)
                    lo(N_OUT + 2)
                    lo(N_OUT + 3)
                    lo(N_OUT + 4)
                    for i, t in NORMS[TT:3 * TT]:
                        mean(i, t)
                        scale(i, t)
                        if i == 1:
                            post_norm(t, PS[:, 2 * t:2 * t + 2, :])
                        else:
                            pre_norm(1, t)
                            if t >= 1:
                                x_low(1, t - 1)
                    x_low(1, TT - 1)

                    def quarter(q, last):
                        for i in range(8):
                            if not (last and i == 7):
                                n = N_MLP + i + 1
                                v.wait_ge(S["hi_done"], q * 8 + n + 1)
                                v.tensor_tensor(w_view(WL, n, n % SPLIT), w_view(RAW, n, n % RING),
                                                f32(w_view(WH, n, n % SPLIT)), ALU.subtract).then_inc(S["lo_done"], 1)
                            if i < 4:
                                for f in (2 * i, 2 * i + 1):
                                    v.wait_ge(S["relu"], q * 8 + f + 1)
                                    v.wait_ge(S["act_lo"], q * 8 + f + 1)
                                    v.scalar_tensor_tensor(SQR[:, f % 2, :], PS[:, 4 + f % 4, :], 0.0,
                                                           RELU[:, f % 2, :], ALU.max, ALU.mult
                                                           ).then_inc(S["a_done"], 1)
                            elif i % 2:
                                half = (i - 4) // 2
                                for t in range(TT):
                                    acc = MACC[:, t, 512 * half:512 * half + 512]
                                    v.wait_ge(S["down_done"], q * 8 + 4 * half + t + 2)
                                    v.wait_ge(S["down_free"], q * 8 + 4 * half + t + 1)
                                    v.tensor_tensor(acc, acc, PS[:, t, :], ALU.add).then_inc(S["down_free"], 1)

                    v.wait_ge(S["macc0"], 1)
                    with v.Fori(0, QUARTERS - 1) as q:
                        quarter(q, False)
                    quarter(QUARTERS - 1, True)
                    v.wait_ge(S["post_mlp"], 16)
                    v.wait_ge(S["down_free"], 8 * QUARTERS + 8)
                    for t in range(TT):
                        mean(3, t)
                        scale(3, t)
                        post_norm(t, MACC[:, t, :])

                @block.gpsimd
                def _(g_):
                    g_.sem_inc(S["down_done"], 1)
                    g_.sem_inc(S["a_done"], 4)
                    g_.sem_inc(S["act_lo"], 2)
                    g_.sem_inc(S["down_free"], 8)
                    def add_squares(i):
                        g_.wait_ge(S["act_ev"], C_TILES[i] - 7)
                        if i > 1:
                            g_.wait_ge(S["sq_add"], i - 1 if i < 6 else 5)
                        g_.tensor_tensor(SQA[:, :], SQA[:, :], SQ[:, :], ALU.add).then_inc(S["sq_add"], 1)

                    def x_dt_decay(g):
                        g_.wait_ge(S["e_ready"], HG * (g + 1))
                        for c in range(TT - 1):
                            g_.wait_ge(S["xd"], 2 * g + c // 2 + 1)
                            end = E[:, :, P * c + P - 1:P * c + P].to_broadcast([P, HG, 64])
                            g_.tensor_tensor(XDD[:, c, :].rearrange("p (h d) -> p h d", h=HG),
                                             XD[:, c, :].rearrange("p (h d) -> p h d", h=HG), end, ALU.mult
                                             ).then_inc(S["xdd"], 1)

                    x_dt_decay(0)
                    for i in range(1, 4):
                        add_squares(i)
                    x_dt_decay(1)
                    for i in (4, 5, 7):
                        add_squares(i)
                    g_.wait_ge(S["o_done"], TT)
                    g_.memset(MACC[:, :, :], 0.0).then_inc(S["macc0"], 1)
                    with g_.Fori(0, QUARTERS) as q:
                        for f in range(8):
                            g_.wait_ge(S["act_hi"], q * 8 + f + 1)
                            g_.tensor_tensor(AL[:, f, :], SQR[:, f % 2, :], f32(AH[:, f, :]), ALU.subtract
                                             ).then_inc(S["act_lo"], 1)

            nc.all_engine_barrier(sems_to_clear=range(first.num, final.num + 1))

        with nc.Block() as block:
            @block.sync
            def _(sp):
                sp.dma_start(out.rearrange("a (t p) d -> p (a t) d", p=P), H[:, :, :]).then_inc(stored, 16)
                sp.wait_ge(stored, 16)


_INS = ["x", "positions", "pre_mix_norm", "w_in", "q_norm", "w_uq", "kv_norm", "w_ukv", "conv_w", "conv_b",
        "dt_bias", "a_log", "d_skip", "ssd_norm", "w_out", "post_mix_norm", "pre_mlp_norm", "w_up",
        "w_down", "post_mlp_norm"]


def kernel(**inputs):
    import concourse.bacc as _bacc
    from concourse import mybir as _mybir
    from concourse.bass_utils import run_bass_kernel_spmd as _run

    nc = _bacc.Bacc("TRN2", target_bir_lowering=False, num_devices=1)
    arrays, args = {}, {}
    for name in _INS:
        a = np.ascontiguousarray(inputs[name])
        arrays[f"in_{name}_dram"] = a
        args[name] = nc.dram_tensor(f"in_{name}_dram", a.shape, _mybir.dt.from_np(a.dtype), kind="ExternalInput").ap()
    arrays["constants_dram"] = constants()
    consts = nc.dram_tensor("constants_dram", (P, N_CONST), _mybir.dt.float32, kind="ExternalInput").ap()
    out = nc.dram_tensor("out_0_dram", (1, SEQ, D_MODEL), _mybir.dt.float32, kind="ExternalOutput").ap()
    trunk(nc, args, consts, out)
    r = _run(nc, [arrays], core_ids=[0])
    return r.results[0]["out_0_dram"]
```

```python
from contextlib import ExitStack

import numpy as np

import concourse.bass as bass
from concourse import mybir

F32 = mybir.dt.float32
F32R = mybir.dt.float32r
BF16 = mybir.dt.bfloat16
I32 = mybir.dt.int32
ACT = mybir.ActivationFunctionType
ALU = mybir.AluOpType
AX = mybir.AxisListType.X

P = 128
EPS = 1e-6
NEG = -1e30

D_MODEL, SEQ, DEPTH = 1024, 512, 2
HEADS, NOPE, ROPE, VDIM = 8, 64, 32, 64
QK = NOPE + ROPE
Q_RANK, KV_RANK = 768, 256
S_HEADS, GROUPS, STATE, TAPS = 8, 2, 128, 4
INNER = S_HEADS * 64
CONV = INNER + 2 * GROUPS * STATE
D_FF = 4 * D_MODEL
CHUNK = 64
TT = SEQ // P
KD = D_MODEL // P
HG = S_HEADS // GROUPS
SCALE = float(QK) ** -0.5

C_KV = Q_RANK
C_KR = C_KV + KV_RANK
C_Z = C_KR + ROPE
C_XBC = C_Z + INNER
C_DT = C_XBC + CONV

K_ID, K_TRI, K_ONE, K_SWAP, K_FREQ, K_SIGN = 0, 128, 256, 384, 512, 513
N_CONST = 514

V_PRE, V_Q, V_KV, V_CW, V_CB, V_SSD, V_MLP = 0, 8, 14, 16, 48, 56, 60
N_VEC = 68

RING, SPLIT = 4, 2
N_IN = 11
N_UQ = N_IN
N_UKV = N_UQ + 3
N_OUT = N_UKV + 1
N_MLP = N_OUT + 4
QUARTERS = 4
OUT_ROWS = ((4, 5), (6, 7), (0, 1), (2, 3))


def constants():
    c = np.zeros((P, N_CONST), np.float32)
    i = np.arange(P)
    c[:, K_ID:K_ID + P] = np.eye(P)
    c[:, K_TRI:K_TRI + P] = i[:, None] <= i[None, :]
    c[:, K_ONE:K_ONE + P] = 1
    c[i, K_SWAP + (i ^ (ROPE // 2))] = 1
    half = np.arange(0, ROPE, 2, dtype=np.float32)
    c[:, K_FREQ] = (np.float32(10000.0) ** (-half / np.float32(ROPE)))[i % (ROPE // 2)]
    c[:, K_SIGN] = np.where(i % ROPE < ROPE // 2, -1, 1)
    return c


def two_pi_parts():
    parts, rest = [], 2 * np.pi
    for _ in range(2):
        e = np.floor(np.log2(rest)) - 10
        parts.append(float(np.floor(rest / 2 ** e) * 2 ** e))
        rest -= parts[-1]
    return parts + [float(rest)]


S_UNITS = ((3,), (2, 0), (1,))
S_BANK = {3: (0, 0), 2: (1, 0), 0: (1, 384), 1: (2, 0)}
P_AT = {3: 0, 2: 512, 0: 896, 1: 1024}
M_SLOT = {3: 0, 2: 1, 0: 2, 1: 3}
T_UNITS = ((2,), (3, 1), (0,))
T_BANK = {0: (3, 0), 1: (4, 0), 3: (4, 384), 2: (5, 0)}
T_AT = {0: 0, 1: 512, 3: 896, 2: 1024}
PACKED = 1280


def trunk(nc, A, consts, out):
    ctx = ExitStack()
    with ctx:
        def sb(name, shape, dt=F32, stack=ctx):
            return stack.enter_context(nc.sbuf_tensor(name, shape, dt))

        H = sb("h", [P, TT, D_MODEL])
        XH = sb("x_hi", [P, KD, SEQ], F32R)
        XL = sb("x_lo", [P, KD, SEQ], F32R)
        RAW = sb("w_raw", [P, RING, 2048])
        WH = sb("w_hi", [P, SPLIT, 2048], F32R)
        WL = sb("w_lo", [P, SPLIT, 2048], F32R)
        COS = sb("cos", [P, SEQ])
        SIN = sb("sin", [P, SEQ])
        POST = sb("post_w", [P, D_MODEL])
        CT = sb("consts", [P, N_CONST])
        VEC = sb("vec_rows", [N_VEC, P])
        VC = sb("vec_cols", [P, N_VEC])
        SCR = sb("scratch", [P, 3, SEQ])
        DTB = sb("dt_bias_b", [P, S_HEADS])
        ALOG = sb("a_log_b", [P, S_HEADS])
        DSKB = sb("d_skip_b", [P, S_HEADS])
        DSK = sb("d_skip_rows", [P, S_HEADS // 2])
        N4 = sb("norm_small", [P, 7, TT])
        TRIR = sb("tri_r", [P, P], F32R)
        AHL = sb("a_halves", [P, 2, TT * S_HEADS], F32R)
        SQ = sb("squares", [P, SEQ])
        SQA = sb("squares_sum", [P, SEQ])
        SELB = sb("first_chunk", [1, P], BF16)
        MASKB = sb("mask_row", [1, CHUNK], BF16)
        DTT = sb("dt_small", [P, 8, TT * S_HEADS])
        DT, AA, CST = DTT[:, 0, :], DTT[:, 1, :], DTT[:, 2, :]
        CLX = sb("chunk_log", [P, 2, HG, TT])
        MX = sb("row_max", [P, HEADS, TT])
        NM = sb("neg_max", [P, HEADS, TT])
        RSUM = sb("row_sum", [P, HEADS, TT])
        RINV = sb("row_inv", [P, HEADS, TT])

        def union(*variants):
            got, most = [], 0
            for v in variants:
                with ExitStack() as s:
                    got.append([sb(n, shape, dt, s) for n, shape, dt in v])
                most = max(most, sum(4 * int(np.prod(shape[1:])) for _, shape, _ in v))
            sb(variants[0][0][0] + "_zone", [P, most // 4])
            return got

        SM = sb("krope_dt", [40, SEQ])
        (CQ,), (V, PT0), (UTOK,), (RELU, SQR) = union(
            [("c_rows", [P, 8, SEQ], F32)],
            [("v", [P, TT, HEADS * VDIM], F32), ("p_t0", [P, PACKED], F32)],
            [("u_tok", [P, TT, D_MODEL], F32)],
            [("relu", [P, 2, SEQ], F32), ("relu_sq", [P, 2, SEQ], F32)],
        )
        (XB, ZS, E, XD, XDD, BT, CBM, ST, Y), (Q, K), (_q, _k, PR, PT1), (MACC, AH, AL) = union(
            [("xbc", [P, 8, SEQ], F32), ("z_silu", [P, 4, SEQ], F32), ("decay", [P, HG, SEQ], F32),
             ("xdt", [P, TT, HG * 64], F32), ("xdt_dec", [P, TT - 1, HG * 64], F32),
             ("b_tok", [P, TT, STATE], F32), ("cb", [P, SEQ], F32),
             ("state", [P, TT - 1, HG * 64], F32), ("y", [P, 2, SEQ], F32)],
            [("q", [QK, HEADS, SEQ], F32), ("k", [QK, HEADS, SEQ], F32)],
            [("q_", [QK, HEADS, SEQ], F32), ("k_", [QK, HEADS, SEQ], F32),
             ("probs", [P, 2, PACKED], F32), ("p_t1", [P, PACKED], F32)],
            [("mlp_acc", [P, TT, D_MODEL], F32), ("act_hi", [P, 8, SEQ], F32R),
             ("act_lo", [P, 8, SEQ], F32R)],
        )
        PT = (PT0, PT1)
        PS = ctx.enter_context(nc.psum_tensor("ps", [P, 8, 512], F32))

        ident, tri, ones = CT[:, K_ID:K_ID + P], CT[:, K_TRI:K_TRI + P], CT[:, K_ONE:K_ONE + P]
        swap = CT[:, K_SWAP:K_SWAP + P]

        def f32(ap):
            return ap.bitcast(F32)

        SIDE = [9, 10, 11, 12, 13, 14, 15, 16, 17, "q", 18, 19, 20]
        Z_TILES = (9, 10, 17, 18)
        C_TILES = (11, 12, 13, 14, 15, 16, 19, 20)
        KV_BANK = (4, 5, 2, 3, 0, 1, 4, 5)

        NORMS = [x for i in (1, 3) for x in [(i, 0)] + [y for t in range(1, TT) for y in ((i, t), (i + 1, t - 1))]
                 + [(i + 1, TT - 1)]]

        def nth(i, t):
            return NORMS.index((i, t)) + 1

        TWO_CHUNKS = ((0, 0), (0, 1), (1, 0), (1, 1), (0, 2), (1, 2), (0, 3), (1, 3))
        MLP_ORDER = (4, 5, 6, 7, 0, 1, 2, 3)

        def c_slot(i):
            return (i + 2) % 8

        def in_bank(item):
            if item == 0:
                return 0
            return SIDE.index(item) % 2 if item in SIDE else 1 + (item - 1) % 5

        names = """raw0 raw1 raw2 raw3 params broad post_mlp hi_done lo_done w_used
            ssq nrm_x nrm_y utok ut_done xh xl vec_t vc proj act_ev conv0 conv3 xb sq_add
            cssq rsb_x rsb_y cqn ch cl dt_t dt_n dt_e dt_l a_ready a_hi cst cst_ready btok bt cb cbm csb dd e_ready
            xs_t xd xdd m_ready cdx st_mm st_ready yexp yo yd y_done ysq yssq y_n yhi ylo zs
            kswap kro q_done q_ev q_rr qswap q_ro q_rc kv_done k_ev v_ev
            s_done mx nm p_done pn pt_done pt_a pt_d pv o_hi o_lo o_done
            macc0 up_done relu a_done act_hi act_lo down_k0 down_done down_free post_x h_done h_pool next_w1 next_rest next_hi stored
            dve_step act_step""".split()
        S = {n: ctx.enter_context(nc.semaphore(n)) for n in names}
        first, final = S[names[0]], S[names[-1]]
        boot_h = [ctx.enter_context(nc.semaphore(f"boot_h{t}")) for t in range(TT)]
        (boot_ld, boot_v, boot_a, boot_ssq, boot_x, boot_y, boot_s, boot_p, boot_w1, boot_rest, boot_hi, boot_sin) = (
            ctx.enter_context(nc.semaphore(n)) for n in (
                "boot_ld", "boot_v", "boot_a", "boot_ssq", "boot_x", "boot_y", "boot_s", "boot_p", "boot_w1",
                "boot_rest", "boot_hi", "boot_sin"))

        def mean_square(v, t, total):
            return v.tensor_scalar(N4[:, 2, t:t + 1], total, -1 / D_MODEL, -EPS, ALU.mult, ALU.add)

        POWER_SCALE = -2.0 ** (2 / 3)
        THREE_C2 = 3 * 2.0 ** (-2 / 3)

        def newton(v, step, t):
            x, y, tmp = N4[:, 2, t:t + 1], N4[:, 4, t:t + 1], N4[:, 5, t:t + 1]
            step(v.scalar_tensor_tensor(tmp, y, x, y, ALU.mult, ALU.mult))
            step(v.scalar_tensor_tensor(N4[:, 6, t:t + 1], tmp, THREE_C2, y, ALU.add, ALU.mult))

        def normalised(v, t):
            return v.tensor_scalar(UTOK[:, t, :], H[:, t, :], N4[:, 6, t:t + 1], None, ALU.mult)


        def w_view(buf, n, slot):
            rows, cols = chunk_shape(n)
            return buf[:, slot, 0:rows * cols].rearrange("p (k n) -> p k n", k=rows)

        def chunk_shape(n):
            if n == 0:
                return KD, 40
            if n < N_UQ:
                return KD, 256
            if n < N_UKV:
                return 2, HEADS * QK
            if n < N_MLP:
                return 2, 1024
            return (KD, 256) if (n - N_MLP) % 8 < 4 else (4, 512)

        def split_parts(n, slot):
            raw, hi, lo = (w_view(b, n, s) for b, s in ((RAW, n % RING), (WH, slot), (WL, slot)))
            if N_UQ <= n < N_OUT:
                a, b = (NOPE, ROPE) if n < N_UKV else (NOPE, VDIM)
                r = raw.rearrange("p k (h c) -> p k h c", h=HEADS)
                cut = lambda w: ((w[:, :, 0:HEADS * a].rearrange("p k (h c) -> p k h c", h=HEADS)),
                                 (w[:, :, HEADS * a:HEADS * (a + b)].rearrange("p k (h c) -> p k h c", h=HEADS)))
                (h0, h1), (l0, l1) = cut(hi), cut(lo)
                return [x for k in range(2) for x in ((r[:, k, :, 0:a], h0[:, k], l0[:, k]),
                                                      (r[:, k, :, a:a + b], h1[:, k], l1[:, k]))]
            return [(raw, hi, lo)]

        def rows_of(w, r0, r1, c0, c1):
            return w[:, r0:r1, c0:c1].rearrange("a (k p) n -> p (a k) n", p=P)

        FIRST_DMAS = 9

        def first_loads(sp, of, chunk1, rest):
            sp.dma_start(w_view(RAW, 1, 1), rows_of(of("w_in"), 0, D_MODEL, C_XBC, C_XBC + 256)).then_inc(chunk1, 16)
            for name, row, n in (("pre_mix_norm", V_PRE, 8), ("q_norm", V_Q, 6), ("kv_norm", V_KV, 2),
                                 ("conv_b", V_CB, 8), ("ssd_norm", V_SSD, 4), ("pre_mlp_norm", V_MLP, 8)):
                sp.dma_start(VEC[row:row + n, :], of(name).rearrange("a (r c) -> (a r) c", c=P)).then_inc(rest, 16)
            sp.dma_start(VEC[V_CW:V_CW + 32, :], of("conv_w").rearrange("a k (r c) -> (a k r) c", c=P)
                         ).then_inc(rest, 16)
            small = w_view(RAW, 0, 0)
            for at_col, c0, c1 in ((0, C_KR, C_Z), (ROPE, C_DT, C_DT + S_HEADS)):
                sp.dma_start(small[:, :, at_col:at_col + c1 - c0], rows_of(of("w_in"), 0, D_MODEL, c0, c1)
                             ).then_inc(rest, 16)

        def split_high(a, n):
            return a.activation(w_view(WH, n, n % SPLIT), w_view(RAW, n, n % RING), ACT.Copy)

        def split_low(eng, n, part=slice(0, 2048)):
            return eng.tensor_tensor(WL[:, n % SPLIT, part], RAW[:, n % RING, part], f32(WH[:, n % SPLIT, part]),
                                     ALU.subtract)

        with nc.Block() as block:
            @block.sync
            def _(sp):
                sp.dma_start(CT[:, :], consts[:, :]).then_inc(boot_ld, 16)
                sp.dma_start(SCR[:, 0, :].bitcast(I32),
                             A["positions"][0:1, :].to_broadcast([P, SEQ])).then_inc(boot_ld, 16)
                for t in range(TT):
                    sp.dma_start(H[:, t, :], A["x"][0, P * t:P * t + P, :]).then_inc(boot_h[t], 16)
                first_loads(sp, lambda name: A[name][0:1], boot_w1, boot_rest)
                sp.wait_ge(boot_rest, 16 * FIRST_DMAS)

            @block.vector
            def _(v):
                n = [0]

                def step(ins):
                    n[0] += 1
                    ins.then_inc(boot_v, 1)
                    v.wait_ge(boot_v, n[0])

                v.wait_ge(boot_ld, 32)
                pos, ang, turns = SCR[:, 1, :], SCR[:, 2, :], SQ[:, :]
                step(v.tensor_copy(pos, SCR[:, 0, :].bitcast(I32)))
                step(v.tensor_scalar(ang, pos, CT[:, K_FREQ:K_FREQ + 1], None, ALU.mult))
                magic = 1.5 * 2.0 ** 23
                step(v.tensor_scalar(turns, ang, float(1 / (2 * np.pi)), magic, ALU.mult, ALU.add))
                step(v.tensor_scalar(turns, turns, -magic, None, ALU.add))
                def mean(t):
                    v.wait_ge(boot_ssq, t + 1)
                    mean_square(v, t, N4[:, 0, t:t + 1]).then_inc(boot_x, 1)

                mean(0)
                step(v.scalar_tensor_tensor(ang, turns, -two_pi_parts()[0], ang, ALU.mult, ALU.add))
                for t in range(TT):
                    if t + 1 < TT:
                        mean(t + 1)
                    if t < 2:
                        step(v.scalar_tensor_tensor(ang, turns, -two_pi_parts()[t + 1], ang, ALU.mult, ALU.add))
                    elif t == 2:
                        v.tensor_scalar(SIN[:, :], ang, 3.1415925, -3.1415925, ALU.min, ALU.max).then_inc(boot_sin, 1)
                    v.wait_ge(boot_y, t + 1)
                    newton(v, step, t)
                    normalised(v, t)
                v.wait_ge(boot_sin, 1)
                step(v.scalar_tensor_tensor(COS[:, :], SIN[:, :], -1.0, SIN[:, :], ALU.mult, ALU.max))
                v.tensor_scalar(COS[:, :], COS[:, :], -1.0, float(np.pi / 2), ALU.mult, ALU.add).then_inc(boot_sin, 1)
                v.wait_ge(boot_hi, 1)
                split_low(v, 1, slice(0, 1024))
                v.wait_ge(boot_a, 1)
                v.tensor_scalar(SIN[:, :], SIN[:, :], CT[:, K_SIGN:K_SIGN + 1], None, ALU.mult)

            @block.scalar
            def _(a):
                def power(t):
                    a.wait_ge(boot_x, t + 1)
                    a.activation(N4[:, 3, t:t + 1], N4[:, 2, t:t + 1], ACT.Ln, scale=POWER_SCALE).then_inc(boot_s, 1)
                    a.wait_ge(boot_s, t + 1)
                    a.activation(N4[:, 4, t:t + 1], N4[:, 3, t:t + 1], ACT.Exp, scale=-0.5).then_inc(boot_y, 1)

                a.preload_act_table_set("natural_log_exp_and_others")
                for t in range(TT):
                    a.wait_ge(boot_h[t], 16)
                    a.activation(UTOK[:, t, :], H[:, t, :], ACT.Square, accum_out=N4[:, 0, t:t + 1]
                                 ).then_inc(boot_ssq, 1)
                    if t:
                        power(t - 1)
                power(TT - 1)
                a.wait_ge(boot_w1, 16)
                split_high(a, 1).then_inc(boot_hi, 1)
                a.activation(TRIR[:, :], tri, ACT.Copy)
                a.wait_ge(boot_sin, 2)
                a.activation(SIN[:, :], SIN[:, :], ACT.Sin).then_inc(boot_a, 1)
                a.activation(COS[:, :], COS[:, :], ACT.Sin)

            @block.gpsimd
            def _(g_):
                g_.memset(SELB[:, :], 0.0).then_inc(boot_p, 1)
                g_.memset(MASKB[:, :], NEG)
                g_.wait_ge(boot_p, 1)
                g_.memset(SELB[:, 0:CHUNK], 1.0)
                g_.wait_ge(boot_hi, 1)
                split_low(g_, 1, slice(1024, 2048))

        with nc.Fori(0, DEPTH) as layer:
            with nc.Block() as block:

                LAST = N_MLP + 8 * QUARTERS

                def at(name):
                    return A[name][bass.ds(layer, 1)]

                def stream_ready(eng, i, t):
                    if i == 1:
                        eng.wait_ge(S["h_done"], t + 1)
                    elif t < TT - 1:
                        eng.wait_ge(S["h_pool"], t + 1)
                    else:
                        eng.wait_ge(S["h_done"], TT + 1)

                def at_next(name):
                    return A[name][bass.ds(DEPTH - 1 - layer, 1)]

                @block.sync
                def _(sp):
                    def load(n, src):
                        if n >= RING:
                            sp.wait_ge(S["hi_done"], max(n - RING + 1, 2))
                            sp.wait_ge(S["lo_done"], max(n - RING + 1, 2))
                        sp.dma_start(w_view(RAW, n, n % RING), src).then_inc(S[f"raw{n % RING}"], 16)

                    def rows(name, r0, r1, c0, c1):
                        return rows_of(at(name), r0, r1, c0, c1)

                    starts = ([C_XBC + 256 * i for i in range(4)] + [C_Z] + [256 * i for i in range(3)]
                              + [C_Z + 256, C_KV])
                    for i, c in enumerate(starts[1:]):
                        load(2 + i, rows("w_in", 0, D_MODEL, c, c + 256))
                        if i == 1:
                            for buf, name in ((DTB, "dt_bias"), (ALOG, "a_log"), (DSKB, "d_skip")):
                                sp.dma_start(buf[:, :], at(name).to_broadcast([P, S_HEADS])).then_inc(S["broad"], 16)
                            sp.dma_start(POST[:, :], at("post_mix_norm").to_broadcast([P, D_MODEL])
                                         ).then_inc(S["broad"], 16)
                    for i in range(3):
                        load(N_UQ + i, rows("w_uq", 256 * i, 256 * i + 256, 0, HEADS * QK))
                    load(N_UKV, rows("w_ukv", 0, KV_RANK, 0, HEADS * (NOPE + VDIM)))
                    for i, (k, _) in enumerate(OUT_ROWS):
                        load(N_OUT + i, rows("w_out", P * k, P * k + 256, 0, D_MODEL))
                    with sp.Fori(0, QUARTERS) as q:
                        for i in range(8):
                            n = N_MLP + i
                            if i < 4:
                                src = at("w_up")[:, :, bass.ds(q * 1024 + 256 * i, 256)]
                            else:
                                half, kk = (i - 4) // 2, (i - 4) % 2
                                src = at("w_down")[:, bass.ds(q * 1024 + 512 * kk, 512), 512 * half:512 * half + 512]
                            src = src.rearrange("a (k p) n -> p (a k) n", p=P)
                            sp.wait_ge(S["hi_done"], q * 8 + (n - RING + 1))
                            sp.wait_ge(S["lo_done"], q * 8 + (n - RING + 1))
                            sp.dma_start(w_view(RAW, n, n % RING), src).then_inc(S[f"raw{n % RING}"], 16)
                    sp.wait_ge(S["h_done"], TT)
                    sp.dma_start(POST[:, :], at("post_mlp_norm").to_broadcast([P, D_MODEL])
                                 ).then_inc(S["post_mlp"], 16)
                    sp.wait_ge(S["hi_done"], LAST - 1)
                    sp.wait_ge(S["lo_done"], LAST - 1)
                    first_loads(sp, at_next, S["next_w1"], S["next_rest"])
                    for t in range(TT):
                        stream_ready(sp, 3, t)
                        sp.dma_start(out[0, P * t:P * t + P, :], H[:, t, :]).then_inc(S["stored"], 16)
                    sp.wait_ge(S["next_rest"], 16 * FIRST_DMAS)
                    sp.wait_ge(S["stored"], 16 * TT)

                N_BROAD = 16 * 4

                def chunk_ready(eng, n, q=None):
                    value = 16 * (n // RING + (1 if n % RING > 1 else 0))
                    eng.wait_ge(S[f"raw{n % RING}"], value if q is None else value + q * 32)

                @block.tensor
                def _(pe):
                    def three(dst, w, x, start, stop):
                        for i, (a, b) in enumerate(((w[1], x[0]), (w[0], x[1]), (w[0], x[0]))):
                            last = pe.matmul(dst, a, b, start=start and i == 0, stop=stop and i == 2)
                        return last

                    def weights(n, q=None):
                        pe.wait_ge(S["lo_done"], max(n + 1, 2) if q is None else q * 8 + n + 1)
                        return w_view(WH, n, n % SPLIT), w_view(WL, n, n % SPLIT)

                    def to_features(t, k):
                        return pe.transpose(PS[:, k, P * t:P * t + P], UTOK[:, t, P * k:P * k + P], ident)

                    pe.transpose(PS[:, 7, 0:N_VEC], VEC[:, :], ident[0:N_VEC, 0:N_VEC]).then_inc(S["vec_t"], 1)
                    for k in range(KD):
                        if k == KD - 1:
                            pe.wait_ge(S["vc"], 1)
                        for t in range(TT):
                            last = to_features(t, k)
                        last.then_inc(S["ut_done"], 1)

                    held = {}

                    def in_tile(m, k0=0, k1=KD):
                        n = (m + 1) // 2
                        if n not in held:
                            held[n] = weights(n)
                        wh, wl = held[n]
                        c0, c1 = (0, 40) if m == 0 else (P * ((m + 1) % 2), P * ((m + 1) % 2) + P)
                        if k0:
                            pass
                        elif 6 <= m < 9:
                            pe.wait_ge(S["conv3"], m - 5)
                        elif m == 9:
                            pe.wait_ge(S["act_ev"], 1)
                        elif m == 10:
                            pe.wait_ge(S["conv3"], 6)
                        elif m > 10:
                            before_side(m)
                        for k in range(k0, k1):
                            if m == 0:
                                pe.wait_ge(S["xl"], k + 1)
                            last = three(PS[0:c1 - c0, in_bank(m), :], (wh[:, k, c0:c1], wl[:, k, c0:c1]),
                                         (XH[:, k, :], XL[:, k, :]), k == 0, k == KD - 1)
                        if k1 == KD:
                            last.then_inc(S["proj"], 1)

                    def before_side(item):
                        holder = SIDE[SIDE.index(item) - 2]
                        if holder == "q":
                            pe.wait_ge(S["rsb_x"], 2)
                        else:
                            pe.wait_ge(S["act_ev"], holder - 7)

                    def scan_begin(g):
                        if g:
                            pe.wait_ge(S["st_ready"], 3)
                        for c in range(TT):
                            last = pe.transpose(PS[:, 2, P * c:P * c + P], XB[:, 4 + g, P * c:P * c + P], ident)
                        last.then_inc(S["btok"], 1)
                        for c in range(TT):
                            last = pe.matmul(PS[:, 3, P * c:P * c + P], XB[:, 4 + g, P * c:P * c + P],
                                             XB[:, 6 + g, P * c:P * c + P], start=True, stop=True)
                        last.then_inc(S["cb"], 1)

                    def scan_decay(g):
                        if g:
                            pe.wait_ge(S["y_done"], 2)
                        else:
                            pe.wait_ge(S["conv3"], 5)
                        for hh in range(HG):
                            if g and hh == HG - 1:
                                pe.wait_ge(S["rsb_x"], 1)
                            for c in range(TT):
                                col = S_HEADS * c + HG * g + hh
                                for half in (1, 0):
                                    last = pe.matmul(PS[:, 4 + hh, P * c:P * c + P],
                                                     AHL[:, half, col:col + 1].to_broadcast([P, P]), TRIR[:, :],
                                                     start=half == 1, stop=half == 0)
                            last.then_inc(S["csb"], 1)

                    def scan_x(g):
                        pe.wait_ge(S["yexp"], 2 * g + 1)
                        for c in range(TT):
                            for jj in range(2):
                                last = pe.transpose(PS[:, 4 + c // 2, 256 * (c % 2) + P * jj:256 * (c % 2) + P * jj + P],
                                                    XB[:, 2 * g + jj, P * c:P * c + P], ident)
                            if c % 2:
                                last.then_inc(S["xs_t"], 1)

                    def scan_states(g):
                        pe.wait_ge(S["bt"], g + 1)
                        pe.wait_ge(S["cbm"], g + 1)
                        for c in range(TT - 1):
                            pe.wait_ge(S["xdd"], 3 * g + c + 1)
                            pe.matmul(PS[:, 2 + c // 2, 256 * (c % 2):256 * (c % 2) + 256], BT[:, c, :], XDD[:, c, :],
                                      start=True, stop=True).then_inc(S["st_mm"], 1)

                    def scan_y(g):
                        pe.wait_ge(S["xd"], 2 * g + 2)
                        pe.wait_ge(S["yexp"], 2 * g + 2)
                        for jj in range(2):
                            for hl in range(2):
                                hh = 2 * jj + hl
                                pe.wait_ge(S["m_ready"], HG * g + hh + 1)
                                for c in range(TT):
                                    last = pe.matmul(PS[64 * hl:64 * hl + 64, 6 + jj, P * c:P * c + P],
                                                     XD[:, c, 64 * hh:64 * hh + 64], E[:, hh, P * c:P * c + P],
                                                     start=True, stop=True)
                            last.then_inc(S["yd"], 1)
                        for jj in range(2):
                            for c in range(1, TT):
                                pe.wait_ge(S["st_ready"], 3 * g + c)
                                last = pe.matmul(PS[:, 4 + jj, P * c:P * c + P], ST[:, c - 1, P * jj:P * jj + P],
                                                 XB[:, 6 + g, P * c:P * c + P], start=True, stop=True)
                            last.then_inc(S["yo"], 1)

                    def scan_squares(g):
                        pe.wait_ge(S["y_done"], 2 * g + 2)
                        for jj in range(2):
                            pe.wait_ge(S["ysq"], 2 * g + jj + 1)
                            last = pe.matmul(PS[:, 7, :], ones, SCR[:, 1 + jj, :], start=(jj == 0), stop=(jj == 1))
                        last.then_inc(S["yssq"], 1)

                    for m in range(3):
                        in_tile(m)
                    pe.wait_ge(S["act_ev"], 1)
                    for t in range(TT):
                        last = pe.transpose(PS[:, 6, 8 * t:8 * t + 8], SM[32:40, P * t:P * t + P], ident[32:40, 32:40])
                    last.then_inc(S["dt_t"], 1)
                    for m in range(3, 6):
                        in_tile(m)
                    pe.wait_ge(S["a_ready"], 1)
                    pe.matmul(PS[:, 7, 0:32], tri, AA, start=True, stop=True).then_inc(S["cst"], 1)
                    in_tile(6)
                    in_tile(7)
                    pe.wait_ge(S["cst_ready"], 1)
                    pe.wait_ge(S["a_hi"], 2)
                    scan_decay(0)
                    in_tile(8)
                    in_tile(9)
                    pe.wait_ge(S["xb"], 8)
                    scan_begin(0)
                    scan_x(0)
                    in_tile(10)
                    scan_states(0)
                    in_tile(11)
                    scan_y(0)
                    scan_begin(1)
                    in_tile(12)
                    scan_squares(0)
                    scan_decay(1)
                    in_tile(13)
                    in_tile(14)
                    scan_x(1)
                    in_tile(15)
                    scan_states(1)
                    in_tile(16)
                    in_tile(17)
                    scan_y(1)
                    before_side("q")
                    pe.wait_ge(S["sq_add"], 5)
                    pe.matmul(PS[:, in_bank("q"), :], ones, SQA[:, :], start=True, stop=True).then_inc(S["cssq"], 1)
                    in_tile(18)
                    in_tile(19)
                    in_tile(20)
                    scan_squares(1)

                    pe.wait_ge(S["act_ev"], 13)
                    for i in range(3):
                        n = N_UQ + i
                        wh, wl = weights(n)
                        for k in range(2):
                            pe.wait_ge(S["cl"], 2 * i + k + 1)
                            s = c_slot(2 * i + k)
                            for mt in ((4, 5, 2, 3, 0, 1) if i == 2 and k == 1 else range(6)):
                                cols = slice(P * mt, P * mt + P)
                                last = three(PS[:, mt, :], (wh[:, k, cols], wl[:, k, cols]),
                                             (XH[:, s, :], XL[:, s, :]), i + k == 0, i == 2 and k == 1)
                                if i == 2 and k == 1:
                                    last.then_inc(S["q_done"], 1)
                        if i < 2:
                            last.then_inc(S["w_used"], 1)
                        if i == 0:
                            pe.wait_ge(S["sq_add"], 6)
                            pe.matmul(PS[:, 6, :], ones, SQA[:, :], start=True, stop=True).then_inc(S["cssq"], 1)
                            pe.wait_ge(S["rsb_x"], 3)
                            pe.matmul(PS[0:ROPE, 7, :], swap[0:ROPE, 0:ROPE], SM[0:ROPE, :], start=True, stop=True
                                      ).then_inc(S["kswap"], 1)
                    pe.wait_ge(S["cl"], 8)
                    wh, wl = weights(N_UKV)
                    for u in range(8):
                        if u < 2:
                            pe.wait_ge(S["q_rr"], u + 1)
                        elif u < 6:
                            pe.wait_ge(S["q_ev"], u - 1)
                        else:
                            pe.wait_ge(S["k_ev"], u - 5)
                        for k in range(2):
                            if u < 4:
                                cols = slice(P * u, P * u + P)
                                last = three(PS[:, KV_BANK[u], :], (wh[:, k, cols], wl[:, k, cols]),
                                             (XH[:, k, :], XL[:, k, :]), k == 0, k == 1)
                            else:
                                toks = slice(P * (u - 4), P * (u - 4) + P)
                                last = three(PS[:, KV_BANK[u], :], (XH[:, k, toks], XL[:, k, toks]),
                                             (wh[:, k, 512:1024], wl[:, k, 512:1024]), k == 0, k == 1)
                        last.then_inc(S["kv_done"], 1)
                        if u == 1:
                            pe.wait_ge(S["kro"], 1)
                            for t in range(2):
                                pe.matmul(PS[:, 6 + t, :], swap, SCR[:, t, :], start=True, stop=True
                                          ).then_inc(S["qswap"], 1)

                    pe.wait_ge(S["ylo"], 4)

                    def scores(h):
                        if h == 0:
                            pe.wait_ge(S["q_ev"], 3)
                            pe.wait_ge(S["k_ev"], 3)
                            pe.wait_ge(S["v_ev"], 2)
                        elif h == 1:
                            pe.wait_ge(S["q_ev"], 4)
                            pe.wait_ge(S["k_ev"], 4)
                        pe.wait_ge(S["q_rc"], h + 1)
                        for u, unit in enumerate(S_UNITS):
                            if h:
                                pe.wait_ge(S["p_done"], 3 * (h - 1) + u + 1)
                            for i in unit:
                                bank, col = S_BANK[i]
                                n = P * (i + 1)
                                pe.matmul(PS[:, bank, col:col + n], Q[:, h, P * i:P * i + P], K[:, h, 0:n],
                                          start=True, stop=False)
                                last = pe.matmul(PS[:, bank, col + n - CHUNK:col + n], SELB[:, :], MASKB[:, :],
                                                 start=False, stop=True)
                            last.then_inc(S["s_done"], 1)

                    def probs_transposed(h):
                        pe.wait_ge(S["pn"], h + 1)
                        if h == 0:
                            pe.wait_ge(S["v_ev"], 4)
                        for u, unit in enumerate(T_UNITS):
                            if h:
                                pe.wait_ge(S["pt_d"] if u == 1 else S["pt_a"], h if u == 1 else 2 * h - 1 + u // 2)
                            for j in unit:
                                bank, col = T_BANK[j]
                                for i in range(j, TT):
                                    at_p = P_AT[i] + P * j
                                    last = pe.transpose(PS[:, bank, col + P * (i - j):col + P * (i - j) + P],
                                                        PR[:, h % 2, at_p:at_p + P], ident)
                            last.then_inc(S["pt_done"], 1)

                    def values(h):
                        pe.wait_ge(S["pt_a"], 2 * h + 2)
                        pe.wait_ge(S["pt_d"], h + 1)
                        if h >= 4:
                            pe.wait_ge(S["o_lo"], h // 2 - 1)
                        rows = slice(64 * (h % 2), 64 * (h % 2) + 64)
                        for j in range(TT):
                            last = pe.matmul(PS[rows, 6 + (h // 2) % 2, P * j:SEQ], V[:, j, VDIM * h:VDIM * h + VDIM],
                                             PT[h % 2][:, T_AT[j]:T_AT[j] + SEQ - P * j],
                                             start=(j == 0), stop=(j == TT - 1))
                        last.then_inc(S["pv"], 1)

                    def out_rows(i, k, t):
                        kt, toks = OUT_ROWS[i][k], slice(P * t, P * t + P)
                        wh, wl = held_out[i]
                        for half in range(2):
                            cols = slice(512 * half, 512 * half + 512)
                            last = three(PS[:, 2 * t + half, :], (XH[:, kt, toks], XL[:, kt, toks]),
                                         (wh[:, k, cols], wl[:, k, cols]), i + k == 0, i == 3 and k == 1)
                        return last

                    held_out = {}

                    scores(0)
                    for h in range(HEADS):
                        if h + 1 < HEADS:
                            scores(h + 1)
                        if h == HEADS - 1:
                            held_out[0] = weights(N_OUT)
                            pe.wait_ge(S["p_done"], 3 * HEADS - 1)
                            out_rows(0, 0, 0)
                        if h:
                            values(h - 1)
                        probs_transposed(h)
                    out_rows(0, 1, 0)
                    values(HEADS - 1)

                    for i in range(2):
                        held_out[i] = weights(N_OUT + i)
                        for k in range(2):
                            for t in range(0 if i else 1, TT):
                                if i + k == 0 and t == 3:
                                    pe.wait_ge(S["o_lo"], 4)
                                last = out_rows(i, k, t)
                        last.then_inc(S["w_used"], 1)
                    for i, t in TWO_CHUNKS:
                        if t == 0:
                            held_out[2 + i] = weights(N_OUT + 2 + i)
                        for k in range(2):
                            last = out_rows(2 + i, k, t)
                        if i == 0 and t == TT - 1:
                            last.then_inc(S["w_used"], 1)
                        elif i == 1:
                            last.then_inc(S["o_done"], 1)

                    pe.wait_ge(S["post_x"], TT)
                    for t in range(TT):
                        pe.wait_ge(S["utok"], t + 1)
                        for k in MLP_ORDER:
                            last = to_features(t, k)
                            if t == TT - 1:
                                last.then_inc(S["ut_done"], 1)

                    def quarter(q, last_one):
                        for i in range(8):
                            if not (last_one and i > 5):
                                wh, wl = weights(N_MLP + i, q)
                            if i < 4:
                                for f in (2 * i, 2 * i + 1):
                                    cols = slice(P * (f % 2), P * (f % 2) + P)
                                    pe.wait_ge(S["a_done"], q * 8 + f + 1)
                                    for i_k, k in enumerate(MLP_ORDER):
                                        if f == 0:
                                            pe.wait_ge(S["xl"], KD + i_k + 1)
                                        last = three(PS[:, 4 + f % 4, :], (wh[:, k, cols], wl[:, k, cols]),
                                                     (XH[:, k, :], XL[:, k, :]), i_k == 0, i_k == KD - 1)
                                    last.then_inc(S["up_done"], 1)
                            elif last_one and i > 5:
                                if i == 6:
                                    continue
                                for kk, t in TWO_CHUNKS:
                                    if t == 0:
                                        held[kk] = weights(N_MLP + 6 + kk, q)
                                    if kk == 0:
                                        pe.wait_ge(S["down_free"], q * 8 + TT + t + 5)
                                    wh, wl = held[kk]
                                    for k in range(4):
                                        f, toks = 4 * kk + k, slice(P * t, P * t + P)
                                        last = three(PS[:, t, :], (AH[:, f, toks], AL[:, f, toks]),
                                                     (wh[:, k, :], wl[:, k, :]), f == 0, f == 7)
                                    if kk:
                                        last.then_inc(S["down_done"], 1)
                                    elif t == TT - 1:
                                        last.then_inc(S["down_k0"], 1)
                            else:
                                half, kk = (i - 4) // 2, (i - 4) % 2
                                for k in range(4):
                                    if half == 0:
                                        pe.wait_ge(S["act_lo"], q * 8 + 4 * kk + k + 3)
                                    for t in range(TT):
                                        if kk + k == 0:
                                            pe.wait_ge(S["down_free"], q * 8 + TT * half + t + 5)
                                        f, toks = 4 * kk + k, slice(P * t, P * t + P)
                                        last = three(PS[:, t, :], (AH[:, f, toks], AL[:, f, toks]),
                                                     (wh[:, k, :], wl[:, k, :]), kk + k == 0, kk == 1 and k == 3)
                                        if kk == 1 and k == 3:
                                            last.then_inc(S["down_done"], 1)
                                if kk == 0:
                                    last.then_inc(S["down_k0"], 1)

                    with pe.Fori(0, QUARTERS - 1) as q:
                        quarter(q, False)
                    quarter(QUARTERS - 1, True)

                def chunk_used(eng, n, q=None):
                    if n < N_UQ:
                        eng.wait_ge(S["proj"], 2 * n + 1)
                    elif n < N_UQ + 2:
                        eng.wait_ge(S["w_used"], n - N_UQ + 1)
                    elif n < N_UKV:
                        eng.wait_ge(S["q_done"], 6)
                    elif n == N_UKV:
                        eng.wait_ge(S["kv_done"], 8)
                    elif n < N_OUT + 3:
                        eng.wait_ge(S["w_used"], n - N_OUT + 3)
                    elif q is None:
                        eng.wait_ge(S["o_done"], TT)
                    elif n < N_MLP:
                        eng.wait_ge(S["down_done"], q * 8 + 1)
                    elif n < N_MLP + 4:
                        eng.wait_ge(S["up_done"], q * 8 + 2 * (n - N_MLP) + 2)
                    elif (n - N_MLP) % 2 == 0:
                        eng.wait_ge(S["down_k0"], q * 2 + (n - N_MLP - 4) // 2 + 1)
                    else:
                        eng.wait_ge(S["down_done"], q * 8 + 4 * ((n - N_MLP - 4) // 2) + 5)

                def cuts(n):
                    parts = split_parts(n, n % SPLIT)
                    for i, x in enumerate(parts):
                        yield x, i == len(parts) - 1

                @block.scalar
                def _(a):
                    n_steps = [0]

                    def step(ins):
                        n_steps[0] += 1
                        ins.then_inc(S["act_step"], 1)
                        a.wait_ge(S["act_step"], n_steps[0])

                    def hi(n, q=None):
                        if n:
                            chunk_ready(a, n, q)
                        if n >= SPLIT:
                            chunk_used(a, n - SPLIT, q)
                        for (raw, h, _), last in cuts(n):
                            ins = a.activation(h, raw, ACT.Copy)
                            if last:
                                ins.then_inc(S["hi_done"], 1)

                    def squares(t, x, slot=0):
                        u = UTOK[:, t, 512 * slot:512 * slot + x.shape[-1] * (x.shape[1] if len(x.shape) == 3 else 1)]
                        if len(x.shape) == 3:
                            u = u.rearrange("p (a b) -> p a b", a=2)
                        a.activation(u, x, ACT.Square, accum_out=N4[:, slot, t:t + 1]).then_inc(S["ssq"], 1)

                    def power(i, t):
                        a.wait_ge(S["nrm_x"], nth(i, t))
                        step(a.activation(N4[:, 3, t:t + 1], N4[:, 2, t:t + 1], ACT.Ln, scale=POWER_SCALE))
                        a.activation(N4[:, 4, t:t + 1], N4[:, 3, t:t + 1], ACT.Exp, scale=-0.5
                                     ).then_inc(S["nrm_y"], 1)

                    def x_high(i, col):
                        for i_k, k in enumerate(MLP_ORDER if i else range(KD)):
                            a.wait_ge(S["ut_done"], KD * i + i_k + 1)
                            a.activation(XH[:, k, :], PS[:, k, :], ACT.Copy, scale=VC[:, col + k:col + k + 1]
                                         ).then_inc(S["xh"], 1)

                    def rsqrt_wide(i):
                        a.wait_ge(S["rsb_x"], i + 1)
                        step(a.activation(SCR[:, 0, :], SCR[:, 2, :], ACT.Ln))
                        a.activation(SCR[:, 0, :], SCR[:, 0, :], ACT.Exp, scale=-0.5).then_inc(S["rsb_y"], 1)

                    a.wait_ge(S["vec_t"], 1)
                    a.activation(VC[:, :], PS[:, 7, 0:N_VEC], ACT.Copy).then_inc(S["vc"], 1)
                    hi(0)
                    a.wait_ge(S["vc"], 1)
                    x_high(0, V_PRE)

                    def silu_x(c):
                        a.wait_ge(S["conv3"], c + 1)
                        a.activation(XB[:, c, :], XB[:, c, :], ACT.Silu).then_inc(S["xb"], 1)

                    def out_of_bank(m):
                        a.wait_ge(S["proj"], m + 1)
                        src = PS[:, in_bank(m), :]
                        if m == 0:
                            a.activation(SM[:, :], src[0:40, :], ACT.Copy).then_inc(S["act_ev"], 1)
                        elif m < 9:
                            c = m - 1
                            a.activation(XB[:, c, :], src, ACT.Identity, bias=VC[:, V_CB + c:V_CB + c + 1],
                                         scale=VC[:, V_CW + 24 + c:V_CW + 25 + c]).then_inc(S["conv0"], 1)
                        elif m in Z_TILES:
                            a.activation(ZS[:, Z_TILES.index(m), :], src, ACT.Copy).then_inc(S["act_ev"], 1)
                        else:
                            i = C_TILES.index(m)
                            a.activation(CQ[:, i, :], src, ACT.Copy)
                            if i == 6:
                                a.wait_ge(S["cssq"], 1)
                            elif i >= 2:
                                a.wait_ge(S["sq_add"], min(i - 1, 5))
                            a.activation((SQA if i in (0, 6) else SQ)[:, :], src, ACT.Square).then_inc(S["act_ev"], 1)

                    for m in range(9):
                        if m % 2:
                            hi((m + 1) // 2 + 1)
                        out_of_bank(m)
                        if m >= 2:
                            silu_x(m - 2)
                        if m == 4:
                            a.preload_act_table_set("natural_log_exp_and_others")
                            a.wait_ge(S["broad"], N_BROAD)
                            a.activation(ALOG[:, :], ALOG[:, :], ACT.Exp)
                            a.wait_ge(S["dt_n"], 1)
                            a.activation(DTT[:, 5, :], DTT[:, 4, :], ACT.Exp).then_inc(S["dt_e"], 1)
                            a.wait_ge(S["dt_n"], 2)
                            a.activation(DTT[:, 7, :], DTT[:, 6, :], ACT.Ln).then_inc(S["dt_l"], 1)
                    silu_x(7)
                    a.preload_act_table_set("natural_log_exp_and_others")

                    def chunk_then(m):
                        if m % 2:
                            hi((m + 1) // 2 + 1)
                        out_of_bank(m)

                    def b_tokens(g):
                        a.wait_ge(S["btok"], g + 1)
                        a.activation(BT[:, :, :], PS[:, 2, :].rearrange("p (c n) -> p c n", c=TT), ACT.Copy
                                     ).then_inc(S["bt"], 1)

                    def decays(g):
                        if g:
                            a.wait_ge(S["y_n"], 2)
                        for jj in range(2):
                            a.wait_ge(S["dd"], HG * g + 2 * jj + 2)
                            for hl in range(2):
                                rows = slice(64 * hl, 64 * hl + 64)
                                ins = a.activation(Y[rows, jj, P:SEQ], PS[rows, 4 + 2 * jj + hl, P:SEQ], ACT.Exp)
                            ins.then_inc(S["yexp"], 1)
                            for hh in (2 * jj, 2 * jj + 1):
                                a.activation(E[:, hh, :], E[:, hh, :], ACT.Exp).then_inc(S["e_ready"], 1)
                        a.activation(CLX[:, g], CLX[:, g], ACT.Exp).then_inc(S["cdx"], 1)

                    def z_silu(g):
                        a.wait_ge(S["act_ev"], 11 if g else 3)
                        a.activation(ZS[:, 2 * g:2 * g + 2, :], ZS[:, 2 * g:2 * g + 2, :], ACT.Silu
                                     ).then_inc(S["zs"], 1)
                        a.preload_act_table_set("natural_log_exp_and_others")

                    def y_squares(g):
                        for jj in range(2):
                            a.wait_ge(S["y_done"], 2 * g + jj + 1)
                            a.activation(SCR[:, 1 + jj, :], Y[:, jj, :], ACT.Square).then_inc(S["ysq"], 1)

                    decays(0)
                    b_tokens(0)
                    chunk_then(9)
                    chunk_then(10)
                    chunk_then(11)
                    z_silu(0)
                    b_tokens(1)
                    y_squares(0)
                    chunk_then(12)
                    rsqrt_wide(0)
                    chunk_then(13)
                    decays(1)
                    chunk_then(14)
                    chunk_then(15)
                    chunk_then(16)
                    chunk_then(17)
                    rsqrt_wide(1)
                    chunk_then(18)
                    z_silu(1)
                    chunk_then(19)
                    y_squares(1)
                    chunk_then(20)

                    def c_high(i):
                        a.wait_ge(S["proj"], 21)
                        a.wait_ge(S["cqn"], i + 1)
                        a.activation(XH[:, c_slot(i), :], CQ[:, i, :], ACT.Copy).then_inc(S["ch"], 1)

                    for i in range(6):
                        c_high(i)
                    rsqrt_wide(2)
                    hi(N_UQ + 1)
                    rsqrt_wide(3)
                    hi(N_UQ + 2)
                    c_high(6)
                    c_high(7)
                    hi(N_UKV)
                    a.wait_ge(S["kro"], 1)
                    for t in range(2):
                        a.wait_ge(S["q_done"], t + 1)
                        a.activation(SCR[:, t, :], PS[:, 4 + t, :], ACT.Copy).then_inc(S["q_rr"], 1)

                    def q_nope(j):
                        a.activation(Q[0:NOPE, 2 * j, :], PS[0:64, j, :], ACT.Copy)
                        a.activation(Q[0:NOPE, 2 * j + 1, :], PS[64:128, j, :], ACT.Copy).then_inc(S["q_ev"], 1)

                    for j in (2, 3):
                        a.wait_ge(S["q_done"], j + 1)
                        q_nope(j)
                    a.wait_ge(S["q_done"], 6)
                    for k in range(4):
                        a.wait_ge(S["y_n"], k + 1)
                        a.activation(XH[:, 4 + k, :], XB[:, k, :], ACT.Copy).then_inc(S["yhi"], 1)
                    hi(N_OUT)
                    a.wait_ge(S["ylo"], 4)
                    for j in (0, 1):
                        q_nope(j)

                    def q_rotary(h):
                        t, i = h // 4, h % 4
                        a.wait_ge(S["q_ro"], t + 1)
                        a.activation(Q[NOPE:QK, h, :], SCR[ROPE * i:ROPE * i + ROPE, t, :], ACT.Copy
                                     ).then_inc(S["q_rc"], 1)

                    for h in range(4):
                        q_rotary(h)
                    for t in range(TT):
                        a.wait_ge(S["kv_done"], 5 + t)
                        a.activation(V[:, t, :], PS[:, KV_BANK[4 + t], :], ACT.Copy).then_inc(S["v_ev"], 1)

                    def p_transposed(h):
                        if h >= 2:
                            a.wait_ge(S["pv"], h - 1)
                        for u, j, n in ((0, 2, 256), (2, 0, 512)):
                            a.wait_ge(S["pt_done"], 3 * h + u + 1)
                            a.activation(PT[h % 2][:, T_AT[j]:T_AT[j] + n], PS[:, T_BANK[j][0], 0:n], ACT.Copy
                                         ).then_inc(S["pt_a"], 1)

                    def o_high(p):
                        a.wait_ge(S["pv"], 2 * p + 2)
                        a.activation(XH[:, p, :], PS[:, 6 + p % 2, :], ACT.Copy).then_inc(S["o_hi"], 1)

                    for h in range(HEADS):
                        if h >= 2:
                            a.wait_ge(S["pt_done"], 3 * (h - 1))
                        for u, unit in enumerate(S_UNITS):
                            a.wait_ge(S["nm"], 3 * h + u + 1)
                            for i in unit:
                                (bank, col), n, m = S_BANK[i], P * (i + 1), M_SLOT[i]
                                ins = a.activation(PR[:, h % 2, P_AT[i]:P_AT[i] + n], PS[:, bank, col:col + n], ACT.Exp,
                                                   bias=NM[:, h, m:m + 1], scale=SCALE, accum_out=RSUM[:, h, m:m + 1])
                            ins.then_inc(S["p_done"], 1)
                        if h < 4:
                            q_rotary(4 + h)
                        if h:
                            p_transposed(h - 1)
                        else:
                            hi(N_OUT + 1)
                        if h >= 3 and h % 2:
                            o_high((h - 2) // 2)
                    p_transposed(HEADS - 1)
                    o_high(HEADS // 2 - 1)
                    hi(N_OUT + 2)

                    hi(N_OUT + 3)
                    def next_norm(i, t):
                        stream_ready(a, i, t)
                        squares(t, H[:, t, :])

                    for t in range(TT):
                        a.wait_ge(S["o_done"], t + 1)
                        squares(t, PS[:, 2 * t:2 * t + 2, :])
                        power(1, t)
                        if t:
                            next_norm(1, t - 1)
                        if t == TT - 2:
                            hi(N_MLP)
                        if t:
                            power(2, t - 1)
                    next_norm(1, TT - 1)
                    power(2, TT - 1)
                    x_high(1, V_MLP)

                    def quarter(q, last):
                        for i in range(8):
                            if not (last and i == 7):
                                hi_next(i, q)
                            if i < 4:
                                for f in (2 * i, 2 * i + 1):
                                    a.wait_ge(S["up_done"], q * 8 + f + 1)
                                    a.wait_ge(S["a_done"], q * 8 + f + 3)
                                    a.activation(RELU[:, f % 2, :], PS[:, 4 + f % 4, :], ACT.Relu
                                                 ).then_inc(S["relu"], 1)
                                for f in (2 * i, 2 * i + 1):
                                    a.wait_ge(S["a_done"], q * 8 + f + 5)
                                    a.activation(AH[:, f, :], SQR[:, f % 2, :], ACT.Copy).then_inc(S["act_hi"], 1)

                    def hi_next(i, q):
                        n = N_MLP + i + 1
                        chunk_ready(a, n, q)
                        chunk_used(a, n - SPLIT, q)
                        a.activation(w_view(WH, n, n % SPLIT), w_view(RAW, n, n % RING), ACT.Copy).then_inc(S["hi_done"], 1)

                    with a.Fori(0, QUARTERS - 1) as q:
                        quarter(q, False)
                    quarter(QUARTERS - 1, True)
                    for half in range(2):
                        for t in range(TT):
                            a.wait_ge(S["down_free"], 8 * QUARTERS + 4 * half + t + 1)
                            squares(t, MACC[:, t, 512 * half:512 * half + 512], half)
                            if half:
                                power(3, t)
                                if t:
                                    next_norm(3, t - 1)
                                if t == TT - 2:
                                    a.wait_ge(S["next_w1"], 16)
                                    a.wait_ge(S["down_k0"], 2 * QUARTERS)
                                    split_high(a, 1).then_inc(S["next_hi"], 1)
                                if t:
                                    power(4, t - 1)
                    next_norm(3, TT - 1)
                    power(4, TT - 1)

                @block.vector
                def _(v):
                    n_steps = [0]

                    def step(ins):
                        n_steps[0] += 1
                        ins.then_inc(S["dve_step"], 1)
                        v.wait_ge(S["dve_step"], n_steps[0])

                    def lo(n, q=None):
                        v.wait_ge(S["hi_done"], max(n + 1, 2) if q is None else q * 8 + n + 1)
                        for (raw, h, l), last in cuts(n):
                            ins = v.tensor_tensor(l, raw, f32(h), ALU.subtract)
                            if last:
                                ins.then_inc(S["lo_done"], 1)

                    def mean(i, t):
                        total = N4[:, 0, t:t + 1]
                        v.wait_ge(S["ssq"], nth(i, t) + (TT if i > 2 else 0))
                        if i == 3:
                            total = N4[:, 5, t:t + 1]
                            step(v.tensor_tensor(total, N4[:, 0, t:t + 1], N4[:, 1, t:t + 1], ALU.add))
                        mean_square(v, t, total).then_inc(S["nrm_x"], 1)

                    def scale(i, t):
                        v.wait_ge(S["nrm_y"], nth(i, t))
                        newton(v, step, t)

                    def pre_norm(i, t):
                        scale(i, t)
                        normalised(v, t).then_inc(S["utok"], 1)

                    def post_norm(i, t, x):
                        scale(i, t)
                        two = (lambda z: z) if len(x.shape) == 2 else (
                            lambda z: z.rearrange("p (a b) -> p a b", a=2))
                        v.scalar_tensor_tensor(two(UTOK[:, t, :]), x, N4[:, 6, t:t + 1], two(POST[:, :]),
                                               ALU.mult, ALU.mult).then_inc(S["post_x"], 1)
                        if t:
                            mean(i + 1, t - 1)
                        if i == 1 or t == TT - 1:
                            v.wait_ge(S["post_x"], TT * (i // 2) + t + 1)
                            v.tensor_tensor(H[:, t, :], H[:, t, :], UTOK[:, t, :], ALU.add).then_inc(S["h_done"], 1)
                        if t:
                            pre_norm(i + 1, t - 1)

                    def x_low(i, col):
                        for i_k, k in enumerate(MLP_ORDER if i else range(KD)):
                            v.wait_ge(S["xh"], KD * i + i_k + 1)
                            v.scalar_tensor_tensor(XL[:, k, :], PS[:, k, :], VC[:, col + k:col + k + 1],
                                                   f32(XH[:, k, :]), ALU.mult, ALU.subtract).then_inc(S["xl"], 1)

                    def rsqrt_wide(i, src, count):
                        x, y, r = SCR[:, 2, :], SCR[:, 0, :], SCR[:, 1, :]
                        v.tensor_scalar(x, src, 1 / count, EPS, ALU.mult, ALU.add).then_inc(S["rsb_x"], 1)
                        v.wait_ge(S["rsb_y"], i + 1)
                        step(v.tensor_tensor(r, y, y, ALU.mult))
                        step(v.scalar_tensor_tensor(r, r, -0.5, x, ALU.mult, ALU.mult))
                        step(v.scalar_tensor_tensor(r, r, 1.5, y, ALU.add, ALU.mult))

                    v.wait_ge(S["vc"], 1)
                    lo(0)
                    x_low(0, V_PRE)

                    th = lambda w: w.rearrange("p (t h) -> p t h", t=TT)
                    every_t = lambda w: w.unsqueeze(1).to_broadcast([P, TT, S_HEADS])

                    def decay_logs(g):
                        for hh in range(HG):
                            v.wait_ge(S["csb"], HG * g + hh + 1)
                            bank = PS[:, 4 + hh, :]
                            for c in range(TT):
                                col = S_HEADS * c + HG * g + hh
                                v.tensor_scalar(E[:, hh, P * c:P * c + P], bank[:, P * c:P * c + P],
                                                CST[:, col:col + 1], 0.0, ALU.subtract, ALU.min)
                            v.tensor_copy(CLX[:, g, hh, :], bank[:, P - 1:SEQ:P]).then_inc(S["dd"], 1)

                    for n in range(1, 5):
                        lo(n + 1)
                        for c in (2 * n - 2, 2 * n - 1):
                            if c == 7:
                                decay_logs(0)
                            v.wait_ge(S["conv0"], c + 1)
                            for s in range(1, TAPS):
                                w = V_CW + 8 * (TAPS - 1 - s) + c
                                ins = v.scalar_tensor_tensor(XB[:, c, s:SEQ], PS[:, in_bank(c + 1), 0:SEQ - s],
                                                             VC[:, w:w + 1], XB[:, c, s:SEQ], ALU.mult, ALU.add)
                                if s < TAPS - 1:
                                    step(ins)
                            ins.then_inc(S["conv3"], 1)
                        if n == 1:
                            v.wait_ge(S["dt_t"], 1)
                            v.wait_ge(S["broad"], N_BROAD)
                            for hl in range(2):
                                part = slice(64 * hl, 64 * hl + 64)
                                v.tensor_copy(DSK[part, :], DSKB[part, hl::2])
                            step(v.tensor_tensor(th(DT), th(PS[:, 6, 0:32]), every_t(DTB[:, :]), ALU.add))
                            step(v.tensor_scalar(DTT[:, 3, :], DT, -1.0, None, ALU.mult))
                            v.tensor_tensor(DTT[:, 4, :], DT, DTT[:, 3, :], ALU.min).then_inc(S["dt_n"], 1)
                        elif n == 2:
                            v.wait_ge(S["dt_e"], 1)
                            v.tensor_scalar(DTT[:, 6, :], DTT[:, 5, :], 1.0, None, ALU.add).then_inc(S["dt_n"], 1)
                            v.wait_ge(S["dt_n"], 2)
                            step(v.tensor_scalar(DTT[:, 3, :], DTT[:, 6, :], 1.0, 1e-30, ALU.subtract, ALU.max))
                            step(v.reciprocal(DTT[:, 3, :], DTT[:, 3, :]))
                            v.wait_ge(S["dt_l"], 1)
                            step(v.tensor_tensor(DTT[:, 3, :], DTT[:, 3, :], DTT[:, 5, :], ALU.mult))
                            step(v.tensor_tensor(DTT[:, 3, :], DTT[:, 3, :], DTT[:, 7, :], ALU.mult))
                            step(v.scalar_tensor_tensor(DT, DT, 0.0, DTT[:, 3, :], ALU.max, ALU.add))
                            v.scalar_tensor_tensor(th(AA), th(DT), -1.0, every_t(ALOG[:, :]), ALU.mult, ALU.mult
                                                   ).then_inc(S["a_ready"], 1)
                            v.wait_ge(S["a_ready"], 1)
                            v.tensor_copy(AHL[:, 0, :], AA).then_inc(S["a_hi"], 1)
                            v.wait_ge(S["a_hi"], 1)
                            v.tensor_tensor(AHL[:, 1, :], AA, f32(AHL[:, 0, :]), ALU.subtract).then_inc(S["a_hi"], 1)
                        elif n == 3:
                            v.wait_ge(S["cst"], 1)
                            v.tensor_copy(CST, PS[:, 7, 0:32]).then_inc(S["cst_ready"], 1)
                            v.wait_ge(S["cst_ready"], 1)


                    def masked_cb(g):
                        v.wait_ge(S["cb"], g + 1)
                        blocks = lambda w: w.rearrange("p (c l) -> p c l", c=TT)
                        v.tensor_tensor(blocks(CBM[:, :]), blocks(PS[:, 3, :]),
                                        tri.unsqueeze(1).to_broadcast([P, TT, P]), ALU.mult).then_inc(S["cbm"], 1)

                    def x_dt(g):
                        for i in range(2):
                            v.wait_ge(S["xs_t"], 2 * g + i + 1)
                            chp = lambda w: w.rearrange("p (c h d) -> p c h d", c=2, h=HG)
                            dt4 = th(DT)[:, 2 * i:2 * i + 2, HG * g:HG * g + HG].unsqueeze(3).to_broadcast([P, 2, HG, 64])
                            v.tensor_tensor(XD[:, 2 * i:2 * i + 2, :].rearrange("p c (h d) -> p c h d", h=HG),
                                            chp(PS[:, 4 + i, :]), dt4, ALU.mult).then_inc(S["xd"], 1)

                    def block_scores(g):
                        v.wait_ge(S["xdd"], 3 * g + 3)
                        v.wait_ge(S["cbm"], g + 1)
                        for hh in range(HG):
                            v.wait_ge(S["e_ready"], HG * g + hh + 1)
                            v.tensor_tensor(E[:, hh, :], E[:, hh, :], CBM[:, :], ALU.mult).then_inc(S["m_ready"], 1)

                    def states(g):
                        v.wait_ge(S["st_mm"], 3 * g + 2)
                        v.tensor_copy(ST[:, 0, :], PS[:, 2, 0:256]).then_inc(S["st_ready"], 1)
                        v.wait_ge(S["cdx"], g + 1)
                        for c in (1, 2):
                            v.wait_ge(S["st_ready"], 3 * g + c)
                            hd = lambda w: w.rearrange("p (h d) -> p h d", h=HG)
                            step(v.tensor_tensor(hd(SCR[:, 2, 0:256]), hd(ST[:, c - 1, :]),
                                                 CLX[:, g, :, c:c + 1].to_broadcast([P, HG, 64]), ALU.mult))
                            v.wait_ge(S["st_mm"], 3 * g + c + 1)
                            v.tensor_tensor(ST[:, c, :], SCR[:, 2, 0:256],
                                            PS[:, 2 + c // 2, 256 * (c % 2):256 * (c % 2) + 256],
                                            ALU.add).then_inc(S["st_ready"], 1)

                    def outputs(g):
                        v.wait_ge(S["zs"], g + 1)
                        for jj in range(2):
                            j = 2 * g + jj
                            y = Y[:, jj, :]
                            v.wait_ge(S["yexp"], j + 1)
                            v.wait_ge(S["yd"], j + 1)
                            v.wait_ge(S["yo"], j + 1)
                            step(v.tensor_tensor(SCR[:, 0, P:SEQ], PS[:, 4 + jj, P:SEQ], y[:, P:SEQ], ALU.mult))
                            step(v.scalar_tensor_tensor(y, XB[:, j, :], DSK[:, j:j + 1], PS[:, 6 + jj, :],
                                                        ALU.mult, ALU.add))
                            step(v.tensor_tensor(y[:, P:SEQ], y[:, P:SEQ], SCR[:, 0, P:SEQ], ALU.add))
                            v.tensor_tensor(y, y, ZS[:, j, :], ALU.mult).then_inc(S["y_done"], 1)

                    def outputs_normalised(g, i):
                        v.wait_ge(S["yssq"], g + 1)
                        rsqrt_wide(i, PS[:, 7, :], INNER // GROUPS)
                        for jj in range(2):
                            w = V_SSD + 2 * g + jj
                            v.scalar_tensor_tensor(XB[:, 2 * g + jj, :], Y[:, jj, :], VC[:, w:w + 1], SCR[:, 1, :],
                                                   ALU.mult, ALU.mult).then_inc(S["y_n"], 1)

                    def c_normalised(which, i):
                        tiles, count = (range(6), Q_RANK) if which == "q" else (range(6, 8), KV_RANK)
                        v.wait_ge(S["cssq"], 1 if which == "q" else 2)
                        rsqrt_wide(i, PS[:, in_bank("q") if which == "q" else 6, :], count)
                        for c in tiles:
                            v.scalar_tensor_tensor(CQ[:, c, :], CQ[:, c, :], VC[:, V_Q + c:V_Q + c + 1], SCR[:, 1, :],
                                                   ALU.mult, ALU.mult).then_inc(S["cqn"], 1)

                    def c_low(i):
                        v.wait_ge(S["ch"], i + 1)
                        v.tensor_tensor(XL[:, c_slot(i), :], CQ[:, i, :], f32(XH[:, c_slot(i), :]), ALU.subtract
                                        ).then_inc(S["cl"], 1)

                    masked_cb(0)
                    x_dt(0)
                    lo(6)
                    block_scores(0)
                    states(0)
                    lo(7)
                    outputs(0)
                    masked_cb(1)
                    outputs_normalised(0, 0)
                    lo(8)
                    decay_logs(1)
                    x_dt(1)
                    lo(9)
                    block_scores(1)
                    states(1)
                    lo(10)
                    c_normalised("q", 1)
                    outputs(1)
                    lo(11)
                    for i in range(6):
                        c_low(i)
                    outputs_normalised(1, 2)
                    lo(N_UQ + 1)

                    v.wait_ge(S["y_n"], 4)
                    c_normalised("kv", 3)
                    lo(N_UQ + 2)
                    c_low(6)
                    c_low(7)
                    lo(N_UKV)
                    v.wait_ge(S["kswap"], 1)
                    v.wait_ge(S["cqn"], 8)
                    r = slice(0, ROPE)
                    v.tensor_tensor(SCR[r, 2, :], SM[r, :], COS[r, :], ALU.mult)
                    step(v.tensor_tensor(SCR[r, 1, :], PS[r, 7, :], SIN[r, :], ALU.mult))
                    step(v.tensor_tensor(SCR[r, 2, :], SCR[r, 2, :], SCR[r, 1, :], ALU.add))
                    v.tensor_copy(K[NOPE:QK, :, :], SCR[r, 2, :].unsqueeze(1).to_broadcast([ROPE, HEADS, SEQ])
                                  ).then_inc(S["kro"], 1)

                    for k in range(4):
                        v.wait_ge(S["yhi"], k + 1)
                        v.tensor_tensor(XL[:, 4 + k, :], XB[:, k, :], f32(XH[:, 4 + k, :]), ALU.subtract
                                        ).then_inc(S["ylo"], 1)
                    for u in range(4):
                        v.wait_ge(S["kv_done"], u + 1)
                        v.tensor_copy(K[0:NOPE, 2 * u, :], PS[0:64, KV_BANK[u], :])
                        v.tensor_copy(K[0:NOPE, 2 * u + 1, :], PS[64:128, KV_BANK[u], :]
                                      ).then_inc(S["k_ev"], 1)
                        if u in (1, 2):
                            t = u - 1
                            v.wait_ge(S["qswap"], t + 1)
                            step(v.tensor_tensor(SCR[:, 2, :], SCR[:, t, :], COS[:, :], ALU.mult))
                            step(v.tensor_tensor(SCR[:, t, :], PS[:, 6 + t, :], SIN[:, :], ALU.mult))
                            v.tensor_tensor(SCR[:, t, :], SCR[:, t, :], SCR[:, 2, :], ALU.add
                                            ).then_inc(S["q_ro"], 1)
                            v.wait_ge(S["q_ro"], t + 1)

                    def p_transposed(h):
                        if h >= 2:
                            v.wait_ge(S["pv"], h - 1)
                        v.wait_ge(S["pt_done"], 3 * h + 2)
                        v.tensor_copy(PT[h % 2][:, T_AT[1]:T_AT[1] + 512], PS[:, T_BANK[1][0], :]).then_inc(S["pt_d"], 1)

                    def o_low(p):
                        v.wait_ge(S["o_hi"], p + 1)
                        v.tensor_tensor(XL[:, p, :], PS[:, 6 + p % 2, :], f32(XH[:, p, :]), ALU.subtract
                                        ).then_inc(S["o_lo"], 1)

                    for h in range(HEADS):
                        for u, unit in enumerate(S_UNITS):
                            v.wait_ge(S["s_done"], 3 * h + u + 1)
                            for i in unit:
                                (bank, col), n, m = S_BANK[i], P * (i + 1), M_SLOT[i]
                                ins = v.tensor_reduce(MX[:, h, m:m + 1], PS[:, bank, col:col + n], AX, ALU.max)
                            ins.then_inc(S["mx"], 1)
                            v.wait_ge(S["mx"], 3 * h + u + 1)
                            m0, m1 = M_SLOT[unit[0]], M_SLOT[unit[-1]] + 1
                            v.tensor_scalar(NM[:, h, m0:m1], MX[:, h, m0:m1], -SCALE, None, ALU.mult
                                            ).then_inc(S["nm"], 1)
                        if h:
                            p_transposed(h - 1)
                        v.wait_ge(S["p_done"], 3 * h + 3)
                        step(v.reciprocal(RINV[:, h, :], RSUM[:, h, :]))
                        for i in range(TT):
                            pr, m = PR[:, h % 2, P_AT[i]:P_AT[i] + P * (i + 1)], M_SLOT[i]
                            ins = v.tensor_scalar(pr, pr, RINV[:, h, m:m + 1], None, ALU.mult)
                        ins.then_inc(S["pn"], 1)
                        if h >= 3 and h % 2:
                            o_low((h - 2) // 2)
                    p_transposed(HEADS - 1)
                    o_low(HEADS // 2 - 1)
                    v.wait_ge(S["lo_done"], N_OUT + 2)
                    lo(N_OUT + 2)
                    lo(N_OUT + 3)
                    for t in range(TT):
                        mean(1, t)
                        post_norm(1, t, PS[:, 2 * t:2 * t + 2, :])
                    mean(2, TT - 1)
                    pre_norm(2, TT - 1)
                    x_low(1, V_MLP)

                    def add_down(q, half, t):
                        acc = MACC[:, t, 512 * half:512 * half + 512]
                        v.wait_ge(S["down_done"], q * 8 + 4 * half + t + 2)
                        v.wait_ge(S["down_free"], q * 8 + 4 * half + t + 1)
                        v.tensor_tensor(acc, acc, PS[:, t, :], ALU.add).then_inc(S["down_free"], 1)

                    def quarter(q, last):
                        for i in range(8):
                            if not (last and i == 7):
                                n = N_MLP + i + 1
                                v.wait_ge(S["hi_done"], q * 8 + n + 1)
                                v.tensor_tensor(w_view(WL, n, n % SPLIT), w_view(RAW, n, n % RING),
                                                f32(w_view(WH, n, n % SPLIT)), ALU.subtract).then_inc(S["lo_done"], 1)
                            if i < 4:
                                for f in (2 * i, 2 * i + 1):
                                    v.wait_ge(S["relu"], q * 8 + f + 1)
                                    v.wait_ge(S["act_lo"], q * 8 + f + 1)
                                    v.scalar_tensor_tensor(SQR[:, f % 2, :], PS[:, 4 + f % 4, :], 0.0,
                                                           RELU[:, f % 2, :], ALU.max, ALU.mult
                                                           ).then_inc(S["a_done"], 1)
                            elif i % 2 and not (last and i == 7):
                                for t in range(TT):
                                    add_down(q, (i - 4) // 2, t)

                    v.wait_ge(S["lo_done"], N_MLP + 1)
                    v.wait_ge(S["macc0"], 1)
                    with v.Fori(0, QUARTERS - 1) as q:
                        quarter(q, False)
                    quarter(QUARTERS - 1, True)
                    v.wait_ge(S["post_mlp"], 16)
                    for t in range(TT):
                        add_down(QUARTERS - 1, 1, t)
                        mean(3, t)
                        v.wait_ge(S["down_free"], 8 * QUARTERS + TT + t + 1)
                        post_norm(3, t, MACC[:, t, :])
                    mean(4, TT - 1)
                    pre_norm(4, TT - 1)

                @block.gpsimd
                def _(g_):
                    g_.sem_inc(S["down_done"], 1)
                    g_.sem_inc(S["a_done"], 4)
                    g_.sem_inc(S["act_lo"], 2)
                    g_.sem_inc(S["down_free"], 8)
                    g_.sem_inc(S["hi_done"], 1)
                    g_.sem_inc(S["lo_done"], 1)
                    def add_squares(i):
                        g_.wait_ge(S["act_ev"], C_TILES[i] - 7)
                        if i > 1:
                            g_.wait_ge(S["sq_add"], i - 1 if i < 6 else 5)
                        g_.tensor_tensor(SQA[:, :], SQA[:, :], SQ[:, :], ALU.add).then_inc(S["sq_add"], 1)

                    def x_dt_decay(g):
                        g_.wait_ge(S["e_ready"], HG * (g + 1))
                        for c in range(TT - 1):
                            g_.wait_ge(S["xd"], 2 * g + c // 2 + 1)
                            end = E[:, :, P * c + P - 1:P * c + P].to_broadcast([P, HG, 64])
                            g_.tensor_tensor(XDD[:, c, :].rearrange("p (h d) -> p h d", h=HG),
                                             XD[:, c, :].rearrange("p (h d) -> p h d", h=HG), end, ALU.mult
                                             ).then_inc(S["xdd"], 1)

                    x_dt_decay(0)
                    for i in range(1, 4):
                        add_squares(i)
                    x_dt_decay(1)
                    for i in (4, 5, 7):
                        add_squares(i)
                    for n in (N_OUT, N_OUT + 1):
                        g_.wait_ge(S["lo_done"], n)
                        g_.wait_ge(S["hi_done"], n + 1)
                        split_low(g_, n).then_inc(S["lo_done"], 1)
                    g_.wait_ge(S["s_done"], 3 * HEADS)
                    g_.memset(MACC[:, :, :], 0.0).then_inc(S["macc0"], 1)
                    g_.wait_ge(S["hi_done"], N_MLP + 1)
                    split_low(g_, N_MLP).then_inc(S["lo_done"], 1)
                    with g_.Fori(0, QUARTERS) as q:
                        for f in range(8):
                            g_.wait_ge(S["act_hi"], q * 8 + f + 1)
                            g_.tensor_tensor(AL[:, f, :], SQR[:, f % 2, :], f32(AH[:, f, :]), ALU.subtract
                                             ).then_inc(S["act_lo"], 1)
                    for t in range(TT - 1):
                        g_.wait_ge(S["post_x"], TT + t + 1)
                        g_.tensor_tensor(H[:, t, :], H[:, t, :], UTOK[:, t, :], ALU.add).then_inc(S["h_pool"], 1)
                    g_.wait_ge(S["next_hi"], 1)
                    split_low(g_, 1)

            nc.all_engine_barrier(sems_to_clear=range(first.num, final.num + 1))


_INS = ["x", "positions", "pre_mix_norm", "w_in", "q_norm", "w_uq", "kv_norm", "w_ukv", "conv_w", "conv_b",
        "dt_bias", "a_log", "d_skip", "ssd_norm", "w_out", "post_mix_norm", "pre_mlp_norm", "w_up",
        "w_down", "post_mlp_norm"]


def kernel(**inputs):
    import concourse.bacc as _bacc
    from concourse import mybir as _mybir
    from concourse.bass_utils import run_bass_kernel_spmd as _run

    nc = _bacc.Bacc("TRN2", target_bir_lowering=False, num_devices=1)
    arrays, args = {}, {}
    for name in _INS:
        a = np.ascontiguousarray(inputs[name])
        arrays[f"in_{name}_dram"] = a
        args[name] = nc.dram_tensor(f"in_{name}_dram", a.shape, _mybir.dt.from_np(a.dtype), kind="ExternalInput").ap()
    arrays["constants_dram"] = constants()
    consts = nc.dram_tensor("constants_dram", (P, N_CONST), _mybir.dt.float32, kind="ExternalInput").ap()
    out = nc.dram_tensor("out_0_dram", (1, SEQ, D_MODEL), _mybir.dt.float32, kind="ExternalOutput").ap()
    trunk(nc, args, consts, out)
    r = _run(nc, [arrays], core_ids=[0])
    return r.results[0]["out_0_dram"]
```
